# Optimizing a Trainium2 kernel written in Bass

```python
import math
import jax
import jax.numpy as jnp
from jax import lax
import numpy as np
import jax, jax.numpy as jnp

D_MODEL = 1024
BATCH = 1
SEQ = 256
DEPTH = 1

GRID_W = 64
CTX_LEN = 256
EPS = 1e-6
N_MOD = 6

D_HY = 512
HY_ORDER = 2
HY_BANDS = 16
HY_EMB = 1 + 2 * HY_BANDS
HY_FFN = 64
HY_DECAY_TARGET = 1e-2
HY_FAST_PCT = 0.3
HY_SLOW_PCT = 1.5

NA_HEADS = 8
HEAD_DIM = 64
D_NA = NA_HEADS * HEAD_DIM
WIN_ROWS = 8
WIN_COLS = 16
ROPE_THETA = 10000.0
NEG_INF = -1e30

PEER_HEADS = 8
PEER_N_KEYS = 128
PEER_N_EXPERTS = PEER_N_KEYS * PEER_N_KEYS
PEER_TOPK = 16
PEER_D_KEY = 256
PEER_D_HALF = PEER_D_KEY // 2
PEER_BLOCK = 128

COL_HY = 0
COL_Q = COL_HY + 3 * D_HY
COL_K = COL_Q + D_NA
COL_V = COL_K + D_NA
COL_G_HY = COL_V + D_NA
COL_G_NA = COL_G_HY + D_MODEL
N_PROJ = COL_G_NA + D_MODEL


def rmsnorm(x, g):
    x32 = x.astype(jnp.float32)
    y = x32 * lax.rsqrt(jnp.mean(x32 * x32, axis=-1, keepdims=True) + EPS)
    return (y * g.astype(jnp.float32)).astype(x.dtype)

def modulate(x, g, shift, scale):
    return rmsnorm(x, g) * (1.0 + scale) + shift

def adaln(cond, p):
    m = jax.nn.silu(cond) @ p['w_ada'] + p['b_ada']
    return m.reshape(cond.shape[:-1] + (N_MOD, D_MODEL))

def hyena_filters(L, p):
    f32 = jnp.float32
    t = jnp.linspace(0.0, 1.0, L, dtype=f32)[:, None]
    w = (2.0 * math.pi / L) * jnp.arange(L, dtype=f32)[:, None]
    bands = jnp.linspace(1e-4, HY_BANDS - 1.0, HY_BANDS, dtype=f32)[None, :]
    feats = jnp.concatenate([t, jnp.cos(bands * w), -jnp.sin(bands * w)], axis=-1)
    freq = p['hy_sin_freq'].astype(f32)
    h = jnp.sin(freq * (feats @ p['hy_f1_w'].astype(f32) + p['hy_f1_b'].astype(f32)))
    h = jnp.sin(freq * (h @ p['hy_f2_w'].astype(f32) + p['hy_f2_b'].astype(f32)))
    h = jnp.sin(freq * (h @ p['hy_f3_w'].astype(f32) + p['hy_f3_b'].astype(f32)))
    h = (h @ p['hy_f4_w'].astype(f32)).reshape(L, HY_ORDER, 2, D_HY)
    deltas = jnp.abs(jnp.linspace(math.log(HY_DECAY_TARGET) / HY_SLOW_PCT,
                                  math.log(HY_DECAY_TARGET) / HY_FAST_PCT, D_HY, dtype=f32))
    h = h * jnp.exp(-t * deltas)[:, None, None, :]
    h = h / jnp.sum(jnp.abs(h), axis=(0, 2), keepdims=True)
    fwd, bwd = h[:, :, 0], h[:, :, 1]
    return jnp.concatenate([fwd, jnp.zeros_like(fwd[:1]), bwd[:0:-1]], axis=0)

def hyena(zh, p):
    B, L, _ = zh.shape
    cw = p['hy_conv_w']
    zp = jnp.pad(zh, ((0, 0), (1, 1), (0, 0)))
    zc = cw[0] * zp[:, :-2] + cw[1] * zp[:, 1:-1] + cw[2] * zp[:, 2:] + p['hy_conv_b']
    v, x1, x2 = jnp.split(zc.astype(jnp.float32), 3, axis=-1)
    kf = jnp.fft.rfft(hyena_filters(L, p), axis=0)
    skip = p['hy_skip'].astype(jnp.float32)
    y = v
    for o, gate in enumerate((x1, x2)):
        yf = jnp.fft.rfft(y, n=2 * L, axis=1)
        conv = jnp.fft.irfft(yf * kf[:, o][None], n=2 * L, axis=1)[:, :L]
        y = gate * (conv + skip[o] * y)
    return y.astype(zh.dtype)

def axial_rope(x):
    f32 = jnp.float32
    S = x.shape[1]
    pos = jnp.arange(S, dtype=jnp.int32)
    rows = (pos // GRID_W).astype(f32)
    cols = (pos % GRID_W).astype(f32)
    half = HEAD_DIM // 2
    nf = half // 2
    inv = ROPE_THETA ** (-jnp.arange(nf, dtype=f32) / nf)

    def rot(xp, ps):
        ang = ps[:, None] * inv[None, :]
        cos = jnp.cos(ang)[None, :, None, :]
        sin = jnp.sin(ang)[None, :, None, :]
        a, b = xp[..., :nf], xp[..., nf:]
        return jnp.concatenate([a * cos - b * sin, a * sin + b * cos], axis=-1)

    x32 = x.astype(f32)
    return jnp.concatenate([rot(x32[..., :half], rows), rot(x32[..., half:], cols)], axis=-1).astype(x.dtype)

def neighbourhood_attention(q, k, v, k_ctx, v_ctx, rpb):
    B, S, H, Dh = q.shape
    rows = S // GRID_W
    wr = min(WIN_ROWS, rows)
    r = np.arange(rows)
    row_start = np.clip(r - wr // 2, 0, rows - wr)
    row_idx = row_start[:, None] + np.arange(wr)[None, :]
    col = np.arange(GRID_W)
    col_start = np.clip(col - WIN_COLS // 2, 0, GRID_W - WIN_COLS)
    col_mask = (col[None, :] >= col_start[:, None]) & (col[None, :] < col_start[:, None] + WIN_COLS)
    dr_idx = row_idx - r[:, None] + (WIN_ROWS - 1)
    dc_idx = np.clip(col[None, :] - col[:, None], -(WIN_COLS - 1), WIN_COLS - 1) + (WIN_COLS - 1)
    bias = rpb[:, dr_idx[:, None, :, None], dc_idx[None, :, None, :]]

    qg = q.reshape(B, rows, GRID_W, H, Dh)
    kg = k.reshape(B, rows, GRID_W, H, Dh)[:, row_idx]
    vg = v.reshape(B, rows, GRID_W, H, Dh)[:, row_idx]
    scale = HEAD_DIM ** -0.5
    s_loc = jnp.einsum('brqhd,brikhd->bhrqik', qg, kg).astype(jnp.float32) * scale + bias.astype(jnp.float32)
    s_loc = jnp.where(col_mask[:, None, :], s_loc, NEG_INF).reshape(B, H, rows, GRID_W, wr * GRID_W)
    s_ctx = jnp.einsum('brqhd,bchd->bhrqc', qg, k_ctx).astype(jnp.float32) * scale
    p = jax.nn.softmax(jnp.concatenate([s_loc, s_ctx], axis=-1), axis=-1).astype(v.dtype)
    n_loc = wr * GRID_W
    p_loc = p[..., :n_loc].reshape(B, H, rows, GRID_W, wr, GRID_W)
    out = (jnp.einsum('bhrqik,brikhd->brqhd', p_loc, vg)
           + jnp.einsum('bhrqc,bchd->brqhd', p[..., n_loc:], v_ctx))
    return out.reshape(B, S, H, Dh)

def context_attention(q, k, v):
    s = jnp.einsum('bqhd,bkhd->bhqk', q, k).astype(jnp.float32) * (HEAD_DIM ** -0.5)
    p = jax.nn.softmax(s, axis=-1).astype(v.dtype)
    return jnp.einsum('bhqk,bkhd->bqhd', p, v)

def context_kv(h_ctx, p):
    B, C, _ = h_ctx.shape
    k = (h_ctx @ p['w_in'][:, COL_K:COL_V] + p['b_in'][COL_K:COL_V]).reshape(B, C, NA_HEADS, HEAD_DIM)
    v = (h_ctx @ p['w_in'][:, COL_V:COL_G_HY] + p['b_in'][COL_V:COL_G_HY]).reshape(B, C, NA_HEADS, HEAD_DIM)
    return rmsnorm(k, p['k_norm_g']), v

def token_mixer(h, p, attend):
    B, L, _ = h.shape
    z = h @ p['w_in'] + p['b_in']
    q = rmsnorm(z[..., COL_Q:COL_K].reshape(B, L, NA_HEADS, HEAD_DIM), p['q_norm_g'])
    k = rmsnorm(z[..., COL_K:COL_V].reshape(B, L, NA_HEADS, HEAD_DIM), p['k_norm_g'])
    v = z[..., COL_V:COL_G_HY].reshape(B, L, NA_HEADS, HEAD_DIM)
    y_hy = hyena(z[..., COL_HY:COL_Q], p) @ p['w_hy_out']
    y_na = attend(q, k, v).reshape(B, L, D_NA) @ p['w_na_out']
    gate = jax.nn.sigmoid(z[..., COL_G_HY:N_PROJ].astype(jnp.float32)).astype(h.dtype)
    merged = gate[..., :D_MODEL] * y_hy + gate[..., D_MODEL:] * y_na
    return merged @ p['w_out']

def peer(h, p):
    B, L, D = h.shape
    T = B * L
    hf = h.reshape(T, D)
    q = (hf @ p['peer_w_q']).reshape(T, PEER_HEADS, 2, PEER_D_HALF)
    s = jnp.einsum('thpd,hpnd->thpn', q, p['peer_keys']).astype(jnp.float32)
    top_s, top_i = lax.top_k(s, PEER_TOPK)
    cand_s = (top_s[:, :, 0, :, None] + top_s[:, :, 1, None, :]).reshape(T, PEER_HEADS, PEER_TOPK * PEER_TOPK)
    cand_i = (top_i[:, :, 0, :, None] * PEER_N_KEYS + top_i[:, :, 1, None, :]).reshape(T, PEER_HEADS, PEER_TOPK * PEER_TOPK)
    best_s, best_pos = lax.top_k(cand_s, PEER_TOPK)
    idx = jnp.take_along_axis(cand_i, best_pos, axis=-1)
    g = jax.nn.softmax(best_s, axis=-1).astype(h.dtype)
    nb = T // PEER_BLOCK
    u_tab, v_tab = p['peer_u'], p['peer_v']

    def block(args):
        xb, ib, gb = args
        act = jax.nn.gelu(jnp.einsum('td,thkd->thk', xb, u_tab[ib]), approximate=False)
        return jnp.einsum('thk,thkd->td', gb * act, v_tab[ib])

    out = lax.map(block, (hf.reshape(nb, PEER_BLOCK, D),
                          idx.reshape(nb, PEER_BLOCK, PEER_HEADS, PEER_TOPK),
                          g.reshape(nb, PEER_BLOCK, PEER_HEADS, PEER_TOPK)))
    return out.reshape(B, L, D)

def first_inputs(seed: int = 0) -> dict:
    key = jax.random.key(seed)
    ks = jax.random.split(key, 32)
    f32 = jnp.float32

    def nrm(k, shape, scale):
        return jax.random.normal(k, shape, f32) * scale

    Ld = DEPTH
    return {
        'x': nrm(ks[0], (BATCH, SEQ, D_MODEL), 1.0),
        'c': nrm(ks[1], (BATCH, D_MODEL), 1.0),
        'ctx': nrm(ks[2], (BATCH, CTX_LEN, D_MODEL), 1.0),
        'c_ctx': nrm(ks[3], (D_MODEL,), 1.0),
        'norm1_g': 1.0 + nrm(ks[4], (Ld, D_MODEL), 0.02),
        'norm2_g': 1.0 + nrm(ks[5], (Ld, D_MODEL), 0.02),
        'w_ada': nrm(ks[6], (Ld, D_MODEL, N_MOD * D_MODEL), D_MODEL ** -0.5),
        'b_ada': nrm(ks[7], (Ld, N_MOD * D_MODEL), 0.02),
        'w_in': nrm(ks[8], (Ld, D_MODEL, N_PROJ), D_MODEL ** -0.5),
        'b_in': nrm(ks[9], (Ld, N_PROJ), 0.02),
        'hy_conv_w': nrm(ks[10], (Ld, 3, 3 * D_HY), 3 ** -0.5),
        'hy_conv_b': nrm(ks[11], (Ld, 3 * D_HY), 0.02),
        'hy_f1_w': nrm(ks[12], (Ld, HY_EMB, HY_FFN), HY_EMB ** -0.5),
        'hy_f1_b': nrm(ks[13], (Ld, HY_FFN), 0.02),
        'hy_f2_w': nrm(ks[14], (Ld, HY_FFN, HY_FFN), HY_FFN ** -0.5),
        'hy_f2_b': nrm(ks[15], (Ld, HY_FFN), 0.02),
        'hy_f3_w': nrm(ks[16], (Ld, HY_FFN, HY_FFN), HY_FFN ** -0.5),
        'hy_f3_b': nrm(ks[17], (Ld, HY_FFN), 0.02),
        'hy_f4_w': nrm(ks[18], (Ld, HY_FFN, HY_ORDER * 2 * D_HY), HY_FFN ** -0.5),
        'hy_sin_freq': 1.0 + nrm(ks[19], (Ld, HY_FFN), 0.02),
        'hy_skip': nrm(ks[20], (Ld, HY_ORDER, D_HY), 0.5),
        'q_norm_g': 1.0 + nrm(ks[21], (Ld, HEAD_DIM), 0.02),
        'k_norm_g': 1.0 + nrm(ks[22], (Ld, HEAD_DIM), 0.02),
        'na_rpb': nrm(ks[23], (Ld, NA_HEADS, 2 * WIN_ROWS - 1, 2 * WIN_COLS - 1), 0.02),
        'w_hy_out': nrm(ks[24], (Ld, D_HY, D_MODEL), D_HY ** -0.5),
        'w_na_out': nrm(ks[25], (Ld, D_NA, D_MODEL), D_NA ** -0.5),
        'w_out': nrm(ks[26], (Ld, D_MODEL, D_MODEL), D_MODEL ** -0.5),
        'peer_w_q': nrm(ks[27], (Ld, D_MODEL, PEER_HEADS * PEER_D_KEY), D_MODEL ** -0.5),
        'peer_keys': nrm(ks[28], (Ld, PEER_HEADS, 2, PEER_N_KEYS, PEER_D_HALF), PEER_D_HALF ** -0.5),
        'peer_u': nrm(ks[29], (Ld, PEER_N_EXPERTS, D_MODEL), D_MODEL ** -0.5),
        'peer_v': nrm(ks[30], (Ld, PEER_N_EXPERTS, D_MODEL), 0.5),
    }

def first_block(x, c, ctx, c_ctx, norm1_g, norm2_g, w_ada, b_ada, w_in, b_in, hy_conv_w, hy_conv_b,
              hy_f1_w, hy_f1_b, hy_f2_w, hy_f2_b, hy_f3_w, hy_f3_b, hy_f4_w, hy_sin_freq, hy_skip,
              q_norm_g, k_norm_g, na_rpb, w_hy_out, w_na_out, w_out, peer_w_q, peer_keys, peer_u, peer_v):
    for layer in range(DEPTH):
        p = {
            'norm1_g': norm1_g[layer], 'norm2_g': norm2_g[layer],
            'w_ada': w_ada[layer], 'b_ada': b_ada[layer],
            'w_in': w_in[layer], 'b_in': b_in[layer],
            'hy_conv_w': hy_conv_w[layer], 'hy_conv_b': hy_conv_b[layer],
            'hy_f1_w': hy_f1_w[layer], 'hy_f1_b': hy_f1_b[layer],
            'hy_f2_w': hy_f2_w[layer], 'hy_f2_b': hy_f2_b[layer],
            'hy_f3_w': hy_f3_w[layer], 'hy_f3_b': hy_f3_b[layer],
            'hy_f4_w': hy_f4_w[layer], 'hy_sin_freq': hy_sin_freq[layer], 'hy_skip': hy_skip[layer],
            'q_norm_g': q_norm_g[layer], 'k_norm_g': k_norm_g[layer], 'na_rpb': na_rpb[layer],
            'w_hy_out': w_hy_out[layer], 'w_na_out': w_na_out[layer], 'w_out': w_out[layer],
            'peer_w_q': peer_w_q[layer], 'peer_keys': peer_keys[layer],
            'peer_u': peer_u[layer], 'peer_v': peer_v[layer],
        }
        m_lat = adaln(c, p)
        m_ctx = adaln(c_ctx, p)
        sh1, sc1, g1, sh2, sc2, g2 = [m_lat[:, i:i + 1] for i in range(N_MOD)]
        ch1, cs1, cg1, ch2, cs2, cg2 = [m_ctx[i:i + 1] for i in range(N_MOD)]

        h_ctx = modulate(ctx, p['norm1_g'], ch1, cs1)
        k_ctx, v_ctx = context_kv(h_ctx, p)

        def attend_latent(q, k, v, k_ctx=k_ctx, v_ctx=v_ctx, rpb=p['na_rpb']):
            return neighbourhood_attention(axial_rope(q), axial_rope(k), v, k_ctx, v_ctx, rpb)

        h = modulate(x, p['norm1_g'], sh1, sc1)
        x_next = x + g1 * token_mixer(h, p, attend_latent)
        x_next = x_next + g2 * peer(modulate(x_next, p['norm2_g'], sh2, sc2), p)

        if layer + 1 < DEPTH:
            ctx_next = ctx + cg1 * token_mixer(h_ctx, p, context_attention)
            ctx = ctx_next + cg2 * peer(modulate(ctx_next, p['norm2_g'], ch2, cs2), p)
        x = x_next
    return x


DEPTH_2 = 2

N_HEADS = 8
HEAD_DIM_2 = 128
N_KV_HEADS = 2
Q_PER_KV = N_HEADS // N_KV_HEADS
ATTN_WIDTH = N_HEADS * HEAD_DIM_2
KV_WIDTH = N_KV_HEADS * HEAD_DIM_2
IDX_HEADS = 8
IDX_DIM = 64
TOPK_MAX = 256
Q_BLOCK = 128
ROPE_THETA_2 = 500000.0
ROPE_FRACTION = 4

SSD_EXPAND = 2
SSD_INNER = SSD_EXPAND * D_MODEL
SSD_HEAD_DIM = 64
SSD_HEADS = SSD_INNER // SSD_HEAD_DIM
SSD_GROUPS = 4
SSD_HEADS_PER_GROUP = SSD_HEADS // SSD_GROUPS
SSD_STATE = 128
SSD_CONV = 4
SSD_CHUNK = 128
SSD_CONV_DIM = SSD_INNER + 2 * SSD_GROUPS * SSD_STATE

FFN_DIM = 2816
FFN_CONV = 3
NORM_EPS = 1e-6

IN_SPLITS = (ATTN_WIDTH, KV_WIDTH, KV_WIDTH, IDX_HEADS * IDX_DIM, IDX_DIM, IDX_HEADS,
             SSD_INNER, SSD_CONV_DIM, SSD_HEADS, D_MODEL, D_MODEL)
IN_COLS = (ATTN_WIDTH + 2 * KV_WIDTH + IDX_HEADS * IDX_DIM + IDX_DIM + IDX_HEADS
           + SSD_INNER + SSD_CONV_DIM + SSD_HEADS + 2 * D_MODEL)


def rms_norm(x, w):
    xf = x.astype(jnp.float32)
    y = xf * lax.rsqrt(jnp.mean(xf * xf, axis=-1, keepdims=True) + NORM_EPS)
    return (y * w.astype(jnp.float32)).astype(x.dtype)

def rope_tables(seq, rot_dim):
    inv = ROPE_THETA_2 ** (-jnp.arange(0, rot_dim, 2, dtype=jnp.float32) / rot_dim)
    ang = jnp.arange(seq, dtype=jnp.float32)[:, None] * inv[None, :]
    return jnp.cos(ang), jnp.sin(ang)

def apply_partial_rope(t, cos, sin):
    half = cos.shape[-1]
    rot = 2 * half
    c = cos[None, :, None, :]
    s = sin[None, :, None, :]
    tf = t[..., :rot].astype(jnp.float32)
    x1, x2 = tf[..., :half], tf[..., half:]
    r = jnp.concatenate([x1 * c - x2 * s, x2 * c + x1 * s], axis=-1).astype(t.dtype)
    return jnp.concatenate([r, t[..., rot:]], axis=-1)

def causal_dwconv(u, w, b):
    width = w.shape[0]
    seq = u.shape[1]
    up = jnp.pad(u, ((0, 0), (width - 1, 0), (0, 0)))
    out = b
    for j in range(width):
        out = out + up[:, j:j + seq] * w[j]
    return out

def dsa_attention(q, k, v, q_idx, k_idx, w_idx):
    bsz, seq = q.shape[0], q.shape[1]
    topk = min(TOPK_MAX, seq // 4)
    n_blk = seq // Q_BLOCK
    kv = jnp.concatenate([k, v], axis=-1)
    k_idx_f = k_idx.astype(jnp.float32)
    kpos = jnp.arange(seq)
    scale = HEAD_DIM_2 ** -0.5

    def block(i):
        t0 = i * Q_BLOCK
        sl = lambda a: lax.dynamic_slice_in_dim(a, t0, Q_BLOCK, axis=1)
        qpos = t0 + jnp.arange(Q_BLOCK)
        qi = sl(q_idx).astype(jnp.float32)
        wi = sl(w_idx).astype(jnp.float32)
        rel = jax.nn.relu(jnp.einsum('bqhd,bsd->bqhs', qi, k_idx_f))
        score = jnp.einsum('bqhs,bqh->bqs', rel, wi)
        causal = kpos[None, :] <= qpos[:, None]
        score = jnp.where(causal[None], score, -jnp.inf)
        _, sel = lax.top_k(score, topk)
        valid = sel <= qpos[None, :, None]
        kv_sel = jax.vmap(lambda a, ix: a[ix])(kv, sel)
        k_sel, v_sel = kv_sel[..., :HEAD_DIM_2], kv_sel[..., HEAD_DIM_2:]
        qb = sl(q).reshape(bsz, Q_BLOCK, N_KV_HEADS, Q_PER_KV, HEAD_DIM_2)
        logits = jnp.einsum('bqhgd,bqkhd->bqhgk', qb, k_sel).astype(jnp.float32) * scale
        logits = jnp.where(valid[:, :, None, None, :], logits, -jnp.inf)
        p = jax.nn.softmax(logits, axis=-1).astype(v.dtype)
        o = jnp.einsum('bqhgk,bqkhd->bqhgd', p, v_sel)
        return o.reshape(bsz, Q_BLOCK, ATTN_WIDTH)

    out = lax.map(block, jnp.arange(n_blk))
    return out.transpose(1, 0, 2, 3).reshape(bsz, seq, ATTN_WIDTH)

def ssd_scan(xdt, adt, bm, cm):
    bsz, seq = xdt.shape[0], xdt.shape[1]
    nc = seq // SSD_CHUNK
    X = xdt.reshape(bsz, nc, SSD_CHUNK, SSD_GROUPS, SSD_HEADS_PER_GROUP, SSD_HEAD_DIM)
    Bc = bm.reshape(bsz, nc, SSD_CHUNK, SSD_GROUPS, SSD_STATE)
    Cc = cm.reshape(bsz, nc, SSD_CHUNK, SSD_GROUPS, SSD_STATE)
    A = adt.reshape(bsz, nc, SSD_CHUNK, SSD_GROUPS, SSD_HEADS_PER_GROUP).transpose(0, 3, 4, 1, 2)
    A_cs = jnp.cumsum(A, axis=-1)
    tril = jnp.tril(jnp.ones((SSD_CHUNK, SSD_CHUNK), dtype=bool))
    seg = A_cs[..., :, None] - A_cs[..., None, :]
    Lmat = jnp.exp(jnp.where(tril, seg, -jnp.inf))
    CB = jnp.einsum('bclgn,bcsgn->bcgls', Cc, Bc)
    y_diag = jnp.einsum('bcgls,bgecls,bcsgep->bclgep', CB, Lmat, X)
    decay_states = jnp.exp(A_cs[..., -1:] - A_cs)
    states = jnp.einsum('bclgn,bgecl,bclgep->bcgepn', Bc, decay_states, X)
    chunk_decay = jnp.exp(A_cs[..., -1])

    def step(h, inp):
        s_c, d_c = inp
        return h * d_c[..., None, None] + s_c, h

    h0 = jnp.zeros(states.shape[:1] + states.shape[2:], states.dtype)
    _, states_in = lax.scan(step, h0, (states.transpose(1, 0, 2, 3, 4, 5), chunk_decay.transpose(3, 0, 1, 2)))
    states_in = states_in.transpose(1, 0, 2, 3, 4, 5)
    y_off = jnp.einsum('bclgn,bcgepn,bgecl->bclgep', Cc, states_in, jnp.exp(A_cs))
    return (y_diag + y_off).reshape(bsz, seq, SSD_HEADS, SSD_HEAD_DIM)

def mamba2_branch(z, xbc, dt_raw, conv_w, conv_b, dt_bias, a_log, d_skip, norm_w):
    bsz, seq = z.shape[0], z.shape[1]
    xbc = jax.nn.silu(causal_dwconv(xbc, conv_w, conv_b))
    gn = SSD_GROUPS * SSD_STATE
    xs = xbc[..., :SSD_INNER].reshape(bsz, seq, SSD_HEADS, SSD_HEAD_DIM)
    bm = xbc[..., SSD_INNER:SSD_INNER + gn].reshape(bsz, seq, SSD_GROUPS, SSD_STATE)
    cm = xbc[..., SSD_INNER + gn:].reshape(bsz, seq, SSD_GROUPS, SSD_STATE)
    dt = jax.nn.softplus(dt_raw.astype(jnp.float32) + dt_bias.astype(jnp.float32))
    A = -jnp.exp(a_log.astype(jnp.float32))
    y = ssd_scan(xs * dt[..., None], dt * A, bm, cm) + xs * d_skip[:, None]
    y = y.reshape(bsz, seq, SSD_INNER) * jax.nn.silu(z.astype(jnp.float32))
    yg = y.astype(jnp.float32).reshape(bsz, seq, SSD_GROUPS, SSD_INNER // SSD_GROUPS)
    yg = yg * lax.rsqrt(jnp.mean(yg * yg, axis=-1, keepdims=True) + NORM_EPS)
    y = yg.reshape(bsz, seq, SSD_INNER) * norm_w.astype(jnp.float32)
    return y.astype(z.dtype)

def hybrid_mixer(h, w_in, ssd_conv_w, ssd_conv_b, ssd_dt_bias, ssd_a_log, ssd_d, ssd_norm_w,
                 w_proj_attn, w_proj_ssd, w_out):
    bsz, seq = h.shape[0], h.shape[1]
    proj = h @ w_in
    offsets = np.cumsum(np.array(IN_SPLITS))[:-1].tolist()
    (q, k, v, qi, ki, wi, z, xbc, dt_raw, g_attn, g_ssd) = jnp.split(proj, offsets, axis=-1)
    cos_a, sin_a = rope_tables(seq, HEAD_DIM_2 // ROPE_FRACTION)
    cos_i, sin_i = rope_tables(seq, IDX_DIM // ROPE_FRACTION)
    q = apply_partial_rope(q.reshape(bsz, seq, N_HEADS, HEAD_DIM_2), cos_a, sin_a)
    k = apply_partial_rope(k.reshape(bsz, seq, N_KV_HEADS, HEAD_DIM_2), cos_a, sin_a)
    v = v.reshape(bsz, seq, N_KV_HEADS, HEAD_DIM_2)
    qi = apply_partial_rope(qi.reshape(bsz, seq, IDX_HEADS, IDX_DIM), cos_i, sin_i)
    ki = apply_partial_rope(ki.reshape(bsz, seq, 1, IDX_DIM), cos_i, sin_i)[:, :, 0]
    a = dsa_attention(q, k, v, qi, ki, wi)
    b = mamba2_branch(z, xbc, dt_raw, ssd_conv_w, ssd_conv_b, ssd_dt_bias, ssd_a_log, ssd_d, ssd_norm_w)
    merged = jax.nn.sigmoid(g_attn) * (a @ w_proj_attn) + jax.nn.sigmoid(g_ssd) * (b @ w_proj_ssd)
    return merged @ w_out

def conv_glu_ffn(h, w_up, conv_w, conv_b, w_down):
    u = causal_dwconv(h @ w_up, conv_w, conv_b)
    gate, val = u[..., :FFN_DIM], u[..., FFN_DIM:]
    return (jax.nn.silu(gate) * val) @ w_down

def second_inputs(seed: int = 0) -> dict:
    key = jax.random.key(seed)
    ks = jax.random.split(key, 20)
    nrm = lambda k, shape, s: jax.random.normal(k, shape, jnp.float32) * s
    x = nrm(ks[0], (BATCH, SEQ, D_MODEL), 1.0)
    norm_mix_w = 1.0 + nrm(ks[1], (DEPTH_2, D_MODEL), 0.02)
    w_in = nrm(ks[2], (DEPTH_2, D_MODEL, IN_COLS), D_MODEL ** -0.5)
    ssd_conv_w = nrm(ks[3], (DEPTH_2, SSD_CONV, SSD_CONV_DIM), SSD_CONV ** -0.5)
    ssd_conv_b = nrm(ks[4], (DEPTH_2, SSD_CONV_DIM), 0.01)
    u = jax.random.uniform(ks[5], (DEPTH_2, SSD_HEADS), jnp.float32)
    dt0 = jnp.exp(u * (math.log(0.1) - math.log(0.001)) + math.log(0.001))
    ssd_dt_bias = dt0 + jnp.log(-jnp.expm1(-dt0))
    ssd_a_log = jnp.log(jax.random.uniform(ks[6], (DEPTH_2, SSD_HEADS), jnp.float32, minval=1.0, maxval=16.0))
    ssd_d = 1.0 + nrm(ks[7], (DEPTH_2, SSD_HEADS), 0.1)
    ssd_norm_w = 1.0 + nrm(ks[8], (DEPTH_2, SSD_INNER), 0.02)
    w_proj_attn = nrm(ks[9], (DEPTH_2, ATTN_WIDTH, D_MODEL), ATTN_WIDTH ** -0.5)
    w_proj_ssd = nrm(ks[10], (DEPTH_2, SSD_INNER, D_MODEL), SSD_INNER ** -0.5)
    w_out = nrm(ks[11], (DEPTH_2, D_MODEL, D_MODEL), D_MODEL ** -0.5)
    norm_ffn_w = 1.0 + nrm(ks[12], (DEPTH_2, D_MODEL), 0.02)
    ffn_w_up = nrm(ks[13], (DEPTH_2, D_MODEL, 2 * FFN_DIM), D_MODEL ** -0.5)
    ffn_conv_w = nrm(ks[14], (DEPTH_2, FFN_CONV, 2 * FFN_DIM), FFN_CONV ** -0.5)
    ffn_conv_b = nrm(ks[15], (DEPTH_2, 2 * FFN_DIM), 0.01)
    ffn_w_down = nrm(ks[16], (DEPTH_2, FFN_DIM, D_MODEL), FFN_DIM ** -0.5)
    norm_final_w = 1.0 + nrm(ks[17], (D_MODEL,), 0.02)
    return {'x': x, 'norm_mix_w': norm_mix_w, 'w_in': w_in, 'ssd_conv_w': ssd_conv_w,
            'ssd_conv_b': ssd_conv_b, 'ssd_dt_bias': ssd_dt_bias, 'ssd_a_log': ssd_a_log,
            'ssd_d': ssd_d, 'ssd_norm_w': ssd_norm_w, 'w_proj_attn': w_proj_attn,
            'w_proj_ssd': w_proj_ssd, 'w_out': w_out, 'norm_ffn_w': norm_ffn_w,
            'ffn_w_up': ffn_w_up, 'ffn_conv_w': ffn_conv_w, 'ffn_conv_b': ffn_conv_b,
            'ffn_w_down': ffn_w_down, 'norm_final_w': norm_final_w}

def second_block(x, norm_mix_w, w_in, ssd_conv_w, ssd_conv_b, ssd_dt_bias, ssd_a_log, ssd_d, ssd_norm_w,
              w_proj_attn, w_proj_ssd, w_out, norm_ffn_w, ffn_w_up, ffn_conv_w, ffn_conv_b,
              ffn_w_down, norm_final_w):
    for l in range(DEPTH_2):
        h = rms_norm(x, norm_mix_w[l])
        x = x + hybrid_mixer(h, w_in[l], ssd_conv_w[l], ssd_conv_b[l], ssd_dt_bias[l], ssd_a_log[l],
                             ssd_d[l], ssd_norm_w[l], w_proj_attn[l], w_proj_ssd[l], w_out[l])
        h = rms_norm(x, norm_ffn_w[l])
        x = x + conv_glu_ffn(h, ffn_w_up[l], ffn_conv_w[l], ffn_conv_b[l], ffn_w_down[l])
    return rms_norm(x, norm_final_w)


def setup_inputs(seed=0):
    out = dict(first_inputs(seed))
    for name, value in second_inputs(seed + 1).items():
        if name != "x":
            out[name + "_2"] = value
    return out


def reference(
    x, c, ctx, c_ctx, norm1_g, norm2_g, w_ada, b_ada, w_in, b_in, hy_conv_w, hy_conv_b, hy_f1_w,
    hy_f1_b, hy_f2_w, hy_f2_b, hy_f3_w, hy_f3_b, hy_f4_w, hy_sin_freq, hy_skip, q_norm_g,
    k_norm_g, na_rpb, w_hy_out, w_na_out, w_out, peer_w_q, peer_keys, peer_u, peer_v,
    norm_mix_w_2, w_in_2, ssd_conv_w_2, ssd_conv_b_2, ssd_dt_bias_2, ssd_a_log_2, ssd_d_2,
    ssd_norm_w_2, w_proj_attn_2, w_proj_ssd_2, w_out_2, norm_ffn_w_2, ffn_w_up_2, ffn_conv_w_2,
    ffn_conv_b_2, ffn_w_down_2, norm_final_w_2,
):
    x = first_block(
        x, c, ctx, c_ctx, norm1_g, norm2_g, w_ada, b_ada, w_in, b_in, hy_conv_w, hy_conv_b,
        hy_f1_w, hy_f1_b, hy_f2_w, hy_f2_b, hy_f3_w, hy_f3_b, hy_f4_w, hy_sin_freq, hy_skip,
        q_norm_g, k_norm_g, na_rpb, w_hy_out, w_na_out, w_out, peer_w_q, peer_keys, peer_u,
        peer_v,
    )
    return second_block(
        x, norm_mix_w_2, w_in_2, ssd_conv_w_2, ssd_conv_b_2, ssd_dt_bias_2, ssd_a_log_2,
        ssd_d_2, ssd_norm_w_2, w_proj_attn_2, w_proj_ssd_2, w_out_2, norm_ffn_w_2, ffn_w_up_2,
        ffn_conv_w_2, ffn_conv_b_2, ffn_w_down_2, norm_final_w_2,
    )


_drawn_inputs = setup_inputs


def setup_inputs(seed=0):
    import zlib

    import numpy as np

    out = dict(_drawn_inputs(seed))
    spreads = {}
    factors = {'q_norm_g': 5.428,
     'k_norm_g': 4.98,
     'na_rpb': 13.408,
     'ssd_conv_b_2': 4.934,
     'ssd_norm_w_2': 3.517,
     'ffn_conv_b_2': 5.364,
     'norm_final_w_2': 8.05,
     'hy_sin_freq': 3.373,
     'norm_ffn_w_2': 4.513}
    for name, (base, spread) in spreads.items():
        noise = np.random.default_rng([zlib.crc32(name.encode()), seed]).standard_normal(out[name].shape)
        drawn = base * np.exp(spread * noise) if base else spread * noise
        out[name] = jnp.asarray(drawn.astype(out[name].dtype))
    for name, factor in factors.items():
        out[name] = (out[name] * factor).astype(out[name].dtype)
    return out
```

```python
import math
from contextlib import ExitStack

import numpy as np

import concourse.bass as bass
from concourse import mybir
from concourse.alu_op_type import AluOpType as ALU

ACT = mybir.ActivationFunctionType
F32 = mybir.dt.float32
I32 = mybir.dt.int32
U32 = mybir.dt.uint32
AX = mybir.AxisListType.X

P = 128
SEQ, D = 256, 1024
TT = SEQ // P
KD = D // P
EPS = 1e-6
NEG = -1e30
TAKEN = -3e38

D_HY, NA_HEADS, HD = 512, 8, 64
HY_T = D_HY // P
BANDS, FFN_HY = 16, 64
GRID_W, WIN_COLS, WIN_ROWS = 64, 16, 8
PEER_HEADS, N_KEYS, TOPK = 8, 128, 16
LAYERS, H2, HD2, KVH = 2, 8, 128, 2
IDX_HEADS, IDX_DIM = 8, 64
SEL = min(256, SEQ // 4)
SSD_INNER, SSD_H, SSD_P, SSD_G, SSD_N = 2048, 32, 64, 4, 128
HPG = SSD_H // SSD_G
FFN = 2816
FT = FFN // P

CHUNK = 4096
RING = 3
BANKS = 8
U_RING, V_RING = 8, 16

_S = np.cumsum([0, 1024, 256, 256, 512, 64, 8, 2048, 3072, 32, 1024, 1024])
C2 = dict(zip("q k v qi ki wi z xbc dt ga gs end".split(), [int(v) for v in _S]))


def chunked(w, nk, nn):
    K, N = w.shape
    v = w.reshape(K // P // nk, nk, P, N // nn, nn)
    return np.ascontiguousarray(v.transpose(3, 0, 2, 1, 4)).reshape(-1, P, nk * nn)


def columns(v):
    return v.reshape(-1, P).T


def shape_constants():
    f64 = np.float64
    t = np.arange(SEQ)
    c = {}
    c["ident"] = np.eye(P)
    k, l = np.meshgrid(np.arange(P), np.arange(P), indexing="ij")
    c["upto"] = (k <= l)
    c["ones"] = np.ones((P, P))
    c["after"] = np.tile(np.where(l >= k, 0.0, NEG), (1, 4))
    q = (np.arange(TT)[None, :, None] * P + np.arange(P)[:, None, None])
    c["causal"] = np.where(np.arange(SEQ)[None, None, :] <= q, 0.0, NEG)
    nf = HD // 4
    inv = 10000.0 ** (-np.arange(nf) / nf)
    inv = inv.astype(np.float32)
    pos = [(t // GRID_W), (t % GRID_W)]
    cc, ss = [], []
    for p_ in pos:
        a = (p_[:, None].astype(np.float32) * inv[None, :]).astype(np.float32).astype(f64)
        cc += [np.cos(a), np.cos(a)]
        ss += [-np.sin(a), np.sin(a)]
    rows = lambda m: m.reshape(TT, P, -1).transpose(1, 0, 2)
    c["rope_c"], c["rope_s"] = rows(np.concatenate(cc, 1)), rows(np.concatenate(ss, 1))
    for name, rot in (("a", HD2 // 4), ("i", IDX_DIM // 4)):
        iv = (500000.0 ** (-np.arange(0, rot, 2, dtype=np.float32) / rot)).astype(np.float32)
        a = (t[:, None].astype(np.float32) * iv[None, :]).astype(np.float32).astype(f64)
        c["rope2_c" + name] = rows(np.concatenate([np.cos(a), np.cos(a)], 1))
        c["rope2_s" + name] = rows(np.concatenate([-np.sin(a), np.sin(a)], 1))
    c["count16"] = np.tile(np.arange(TOPK), (P, 1))
    c["zeros"] = np.zeros((P, P))
    c["epscol"] = np.full((P, 1), EPS)
    return {n: np.ascontiguousarray(v.reshape(P, -1), dtype=np.float32) for n, v in c.items()}


def hyena_constants():
    L = SEQ
    t = np.arange(L)
    f = np.arange(L)
    th = 2 * np.pi * np.outer(t, f) / (2 * L)
    cos, sin = np.cos(th), np.sin(th)
    alt = (-1.0) ** t
    c = {}
    tiles = lambda m: m.reshape(TT, P, -1).transpose(1, 0, 2)
    c["dft_c"], c["dft_s"] = tiles(cos), tiles(sin)
    fi = -sin.copy()
    fi[:, 0] = alt
    c["dft_i"] = tiles(fi)
    w = np.full(L, 2.0)
    w[0] = 1.0
    ir = (w[:, None] * cos.T) / (2 * L)
    ii = -2.0 * sin.T / (2 * L)
    ii[0] = alt / (2 * L)
    c["idft_r"], c["idft_i"] = tiles(ir), tiles(ii)
    c["alt"] = tiles(alt[:, None])
    not0 = np.ones((P, 1))
    not0[0] = 0
    c["not_first"] = not0
    tt = np.linspace(0.0, 1.0, L, dtype=np.float32)[:, None]
    wv = (2.0 * math.pi / L) * np.arange(L, dtype=np.float32)[:, None]
    b = np.linspace(1e-4, BANDS - 1.0, BANDS, dtype=np.float32)[None, :]
    feats = np.concatenate([tt, np.cos(b * wv), -np.sin(b * wv)], -1)
    ft = np.zeros((P, L))
    ft[: feats.shape[1]] = feats.T
    c["feats"] = ft
    dl = np.abs(np.linspace(math.log(1e-2) / 1.5, math.log(1e-2) / 0.3, D_HY, dtype=np.float32))
    c["decay"] = tiles(np.exp(-tt.astype(np.float32) * dl))
    return {n: np.ascontiguousarray(v.reshape(P, -1), dtype=np.float32) for n, v in c.items()}


def pack(parts):
    at, where = 0, {}
    for n, v in parts.items():
        where[n] = (at, v.shape[1])
        at += v.shape[1]
    return np.ascontiguousarray(np.concatenate(list(parts.values()), 1), dtype=np.float32), where


def lay_out(i):
    o = {}
    i = {k: np.asarray(v) for k, v in i.items()}
    rows = lambda m: np.ascontiguousarray(m.reshape(TT, P, -1).transpose(1, 0, 2)).reshape(P, -1)
    o["x"], o["ctx"] = rows(i["x"][0]), rows(i["ctx"][0])
    o["consts"], w_c = pack(shape_constants())
    o["hyc"], w_h = pack(hyena_constants())
    w_in, b_in = i["w_in"][0], i["b_in"][0]
    cols = {
        "c": np.stack([columns(i["c"][0]), columns(i["c_ctx"])], 2).reshape(P, -1),
        "g1n": columns(i["norm1_g"][0]), "g2n": columns(i["norm2_g"][0]),
        "b_ada": columns(i["b_ada"][0]), "b_hy": columns(b_in[: 3 * D_HY]),
        "cw": np.concatenate([columns(i["hy_conv_w"][0][j]) for j in range(3)], 1),
        "cb": columns(i["hy_conv_b"][0]),
        "skip": np.concatenate([columns(i["hy_skip"][0][j]) for j in range(2)], 1),
    }
    small = lambda v: np.pad(v[:, None], ((0, P - v.shape[0]), (0, 0)))
    cols |= {"f1b": small(i["hy_f1_b"][0]), "f2b": small(i["hy_f2_b"][0]), "f3b": small(i["hy_f3_b"][0]),
             "freq": small(i["hy_sin_freq"][0])}
    for l in range(LAYERS):
        cols[f"mixw{l}"] = columns(i["norm_mix_w_2"][l])
        cols[f"ffnw{l}"] = columns(i["norm_ffn_w_2"][l])
        cols[f"scw{l}"] = np.concatenate([columns(i["ssd_conv_w_2"][l][j]) for j in range(4)], 1)
        cols[f"scb{l}"] = columns(i["ssd_conv_b_2"][l])
        cols[f"snw{l}"] = columns(i["ssd_norm_w_2"][l])
        cols[f"fcw{l}"] = np.concatenate([columns(i["ffn_conv_w_2"][l][j]) for j in range(3)], 1)
        cols[f"fcb{l}"] = columns(i["ffn_conv_b_2"][l])
    o["cols"], w_v = pack(cols)
    padk = lambda w: np.pad(w, ((0, P - w.shape[0]), (0, 0)))
    o["hyw"], w_w = pack({"f1": padk(i["hy_f1_w"][0]), "f2": padk(i["hy_f2_w"][0]),
                          "f3": padk(i["hy_f3_w"][0]), "f4": padk(i["hy_f4_w"][0])})
    o["b_ada_row"] = i["b_ada"][0][None]
    o["b_in_row"] = b_in[None]
    o["qk_g"] = np.concatenate([i["q_norm_g"][0], i["k_norm_g"][0]])[None]
    o["dt_bias"] = i["ssd_dt_bias_2"].reshape(1, -1)
    o["a_log"] = i["ssd_a_log_2"].reshape(1, -1)
    o["ssd_d"] = i["ssd_d_2"].reshape(1, -1)
    o["final_w"] = i["norm_final_w_2"][None]
    r, wr = np.arange(SEQ // GRID_W), min(WIN_ROWS, SEQ // GRID_W)
    start = np.clip(r - wr // 2, 0, SEQ // GRID_W - wr)
    assert wr == SEQ // GRID_W and (start == 0).all()
    col = np.arange(GRID_W)
    dr = r[None, :] - r[:, None] + WIN_ROWS - 1
    dc = np.clip(col[None, :] - col[:, None], -(WIN_COLS - 1), WIN_COLS - 1) + WIN_COLS - 1
    bias = i["na_rpb"][0][:, dr[:, None, :, None], dc[None, :, None, :]].reshape(NA_HEADS, TT, P, SEQ)
    o["rpb"] = np.ascontiguousarray(bias.transpose(0, 2, 1, 3)).reshape(NA_HEADS, P, TT * SEQ)
    cs = np.clip(col - WIN_COLS // 2, 0, GRID_W - WIN_COLS)
    ok = (col[None, :] >= cs[:, None]) & (col[None, :] < cs[:, None] + WIN_COLS)
    okf = np.broadcast_to(ok[None, :, None, :], (4, GRID_W, 4, GRID_W)).reshape(TT, P, SEQ)
    o["na_mask"] = np.ascontiguousarray(np.where(okf, 0.0, NEG).astype(np.float32).transpose(1, 0, 2)).reshape(P, -1)
    o["w_ada"] = chunked(i["w_ada"][0], 8, 512)
    o["w_in"] = chunked(w_in, 8, 512)
    o["w_hy_out"] = chunked(i["w_hy_out"][0], 4, 1024)
    o["w_na_out"] = chunked(i["w_na_out"][0], 4, 1024)
    o["w_out"] = chunked(i["w_out"][0], 8, 512)
    o["w_pq"] = chunked(i["peer_w_q"][0], 8, 512)
    keys = i["peer_keys"][0].reshape(2 * PEER_HEADS, N_KEYS, P)
    o["keysT"] = np.ascontiguousarray(keys.transpose(2, 0, 1)).reshape(P, -1)
    o["peer_u"], o["peer_v"] = i["peer_u"][0], i["peer_v"][0]
    w2 = i["w_in_2"]
    pick = lambda l, *n: np.concatenate([w2[l][:, C2[a]:C2[b]] for a, b in n], 1)
    o["w2_qkv"] = np.stack([chunked(pick(l, ("q", "ki")), 8, 512) for l in range(LAYERS)])
    o["w2_small"] = np.stack([chunked(pick(l, ("ki", "z"), ("dt", "ga")), 8, 104) for l in range(LAYERS)])
    o["w2_z"] = np.stack([chunked(pick(l, ("z", "xbc")), 8, 512) for l in range(LAYERS)])
    o["w2_xbc"] = np.stack([chunked(pick(l, ("xbc", "dt")), 8, 512) for l in range(LAYERS)])
    o["w2_g"] = np.stack([chunked(pick(l, ("ga", "end")), 8, 512) for l in range(LAYERS)])
    o["w2_pa"] = np.stack([chunked(i["w_proj_attn_2"][l], 8, 512) for l in range(LAYERS)])
    o["w2_ps"] = np.stack([chunked(i["w_proj_ssd_2"][l], 8, 512) for l in range(LAYERS)])
    o["w2_o"] = np.stack([chunked(i["w_out_2"][l], 8, 512) for l in range(LAYERS)])
    up = i["ffn_w_up_2"].reshape(LAYERS, D, 2, FT // 2, 2 * P).transpose(0, 1, 3, 2, 4).reshape(LAYERS, D, 2 * FFN)
    o["w2_up"] = np.stack([chunked(up[l], 8, 512) for l in range(LAYERS)])
    dn = i["ffn_w_down_2"]
    o["w2_dn"] = np.stack([chunked(dn[l], FT // 2, 256) for l in range(LAYERS)])
    return {k: np.ascontiguousarray(v) for k, v in o.items()}, {"consts": w_c, "hyc": w_h, "cols": w_v, "hyw": w_w}


def psum_order():
    g = []
    add = lambda name, n=1: g.extend((name, i) for i in range(n))
    add("mlp", 3), add("filter", 8), add("absum", 2)
    for o in range(2):
        g.extend([("dftf", 4 * o + i) for i in range(4)] + [("nyq", o)])
    for ch in range(12):
        g.append(("ada", ch))
        if ch >= 1 and ch - 1 in ADA_COLS:
            g.append(("adaT", ADA_COLS.index(ch - 1)))
    add("hT0", KD), add("hcT", KD)
    add("zhy", 12), add("zqkv", 10), add("vrow", 2)
    for o in range(2):
        g.extend([("spec", 4 * o + i) for i in range(4)] + [("conv", 4 * o + i) for i in range(4)])
        if o == 0:
            add("yrow", 2)
    add("naT", 8), add("nacT", 4)
    for h in range(NA_HEADS):
        g.extend([("nas", 2 * h), ("nas", 2 * h + 1)])
        if h >= 1:
            g.extend([("nap", 2 * h - 2), ("nap", 2 * h - 1), ("nao", h - 1)])
    h = NA_HEADS
    g.extend([("nap", 2 * h - 2), ("nap", 2 * h - 1), ("nao", h - 1)])
    add("gate", 8), add("mix", 8), add("mT", KD), add("wout", 4)
    add("hfT", KD), add("hfrow", 4), add("pq", 16), add("ps", 8)
    add("acc", 4)
    for l in range(LAYERS):
        L = f"L{l}."
        add(L + "hT", KD), add(L + "qkv", 8), add(L + "small", 2), add(L + "xbc", 24)
        add(L + "qT", 10), add(L + "qiT", 5), add(L + "is", 6), add(L + "z", 8)
        for t in range(TT):
            banks = range(2 * t, 4 * t + 2)
            g.extend([(L + "s", b) for b in banks] + [(L + "p", b) for b in banks])
            g.extend([(L + "o", 2 * t), (L + "o", 2 * t + 1)])
        add(L + "acs", 1), add(L + "X", 8), add(L + "Brow", 1), add(L + "cb", 2)
        add(L + "st", 4)
        for i in range(SSD_G * TT):
            g.extend([(L + "seg", 2 * i), (L + "seg", 2 * i + 1)])
            if i >= 1:
                g.extend([(L + "y", i - 1)] + ([(L + "yo", i - 1)] if (i - 1) % TT else []))
        i = SSD_G * TT
        g.extend([(L + "y", i - 1), (L + "yo", i - 1)])
        add(L + "gate", 8), add(L + "yT", 16), add(L + "pa", 4), add(L + "ps", 4), add(L + "mT", KD), add(L + "wo", 4)
        add(L + "fT", KD), add(L + "up", 44), add(L + "dn", 8)
    return g


ADA_COLS = [0, 1, 2, 3, 6, 7, 8, 9]


def weight_order():
    w = []

    def add(name, l, idx, last, n=CHUNK):
        w.extend((name, l, i, n, last(j)) for j, i in enumerate(idx))

    add("w_ada", None, range(12), lambda j: ("ada", j))
    add("w_in", None, range(3), lambda j: ("zhy", 4 * j + 3))
    add("w_in", None, range(3, 6), lambda j: ("zqkv", 4 * j + 1))
    add("w_in", None, range(6, 10), lambda j: ("gate", 2 * j + 1))
    add("w_hy_out", None, range(1), lambda j: ("mix", 3))
    add("w_na_out", None, range(1), lambda j: ("mix", 7))
    add("w_out", None, range(2), lambda j: ("wout", 2 * j + 1))
    add("w_pq", None, range(4), lambda j: ("pq", 4 * j + 3))
    for l in range(LAYERS):
        L = f"L{l}."
        add("w2_qkv", l, range(4), lambda j: (L + "qkv", 2 * j + 1))
        add("w2_small", l, range(1), lambda j: (L + "small", 1), 8 * 104)
        add("w2_xbc", l, range(6), lambda j: (L + "xbc", 4 * j + 3))
        add("w2_z", l, range(4), lambda j: (L + "z", 2 * j + 1))
        add("w2_g", l, range(4), lambda j: (L + "gate", 2 * j + 1))
        add("w2_pa", l, range(2), lambda j: (L + "pa", 2 * j + 1))
        add("w2_ps", l, range(4), lambda j: (L + "ps", j // 2 * 2 + 1))
        add("w2_o", l, range(2), lambda j: (L + "wo", 2 * j + 1))
        add("w2_up", l, range(11), lambda j: (L + "up", 4 * j + 3))
        add("w2_dn", l, range(8), lambda j: (L + "dn", j // 2 * 2 + 1), 11 * 256)
    return w


class Progress:

    def __init__(self, eng, steps):
        self.eng, self.steps, self.n, self.last = eng, steps, 0, None

    def done(self, ins):
        self.n += 1
        ins.then_inc(self.steps, 1)
        self.last = (self.steps, self.n)

    def reaches(self, ins, sem, value):
        ins.then_inc(sem, 1)
        self.last = (sem, value)

    def settle(self):
        self.eng.wait_ge(*self.last)


def build(nc, d, where, out):
    ctx = ExitStack()
    sb = lambda n, cols, rows=P, dt=F32: ctx.enter_context(nc.sbuf_tensor(n, [rows, cols], dt))
    order = psum_order()
    turn = {g: n for n, g in enumerate(order)}
    assert len(turn) == len(order)
    wplan = weight_order()

    wring = ctx.enter_context(nc.sbuf_tensor("wring", [P, RING, CHUNK], F32))
    x = ctx.enter_context(nc.sbuf_tensor("x_rows", [P, TT, D], F32))
    xs = ctx.enter_context(nc.sbuf_tensor("x_scaled", [P, TT, D], F32))
    hT = ctx.enter_context(nc.sbuf_tensor("hT", [P, KD, SEQ], F32))
    n_c = sum(n for _, n in where["consts"].values())
    n_v = sum(n for _, n in where["cols"].values())
    consts, cols = sb("consts", n_c), sb("cols", n_v)
    act_junk, dve_junk = sb("act_junk", D), sb("dve_junk", D)
    small = sb("small_values", 1024)
    ARENA = 28700
    arena = sb("arena", ARENA)
    psum = ctx.enter_context(nc.psum_tensor("psum", [P, BANKS, 512], F32))

    def K(name):
        a, n = where["consts"][name]
        return consts[:, a:a + n]

    def V(name, j=0, n=1):
        a, _ = where["cols"][name]
        return cols[:, a + j:a + j + n]

    def area(at, *shape):
        n = int(np.prod(shape))
        assert at + n <= ARENA, (at, n)
        ap = arena[:, at:at + n]
        if len(shape) == 2:
            ap = ap.rearrange("p (a b) -> p a b", b=shape[1])
        if len(shape) == 3:
            ap = ap.rearrange("p (a b c) -> p a b c", b=shape[1], c=shape[2])
        return ap

    def sm(at, n):
        return small[:, at:at + n]

    ident, upto, ones = K("ident"), K("upto"), K("ones")

    ss, std, rinv = sm(0, 4), sm(4, 4), sm(8, 4)
    cT = sm(12, 16).rearrange("p (k v) -> p k v", v=2)
    adaT = sm(28, 64).rearrange("p (k v) -> p k v", v=2)
    mod_a = sm(92, 24).rearrange("p (s k) -> p s k", k=8)
    one_row = sm(116, 128)
    nsum, nstd, ninv = sm(244, 48), sm(292, 48), sm(340, 48)
    amax, asum, ainv = sm(388, 16), sm(404, 16), sm(420, 16)
    dt_s = sm(436, 64)
    adt = sm(500, 64)
    acs_s, last_s, nacs_s = sm(564, 64), sm(628, 32), sm(660, 64)
    eacs, dstate = sm(724, 64), sm(788, 32)
    negA = sm(820, 32)
    lnw = sm(852, 4)
    gsum, gstd, ginv = sm(856, 8), sm(864, 8), sm(872, 8)
    wi_s = sm(880, 16)
    best8 = sm(896, 8)
    t64 = sm(904, 64)

    sems = {}

    def S(name):
        if name not in sems:
            sems[name] = ctx.enter_context(nc.semaphore(name))
        return sems[name]

    psum_filled = S("psum_filled")
    bank_read = [S(f"bank_read{b}") for b in range(BANKS)]
    weights_in = [S(f"weights_in{r}") for r in range(RING)]

    def bank(name, i):
        return psum[:, turn[(name, i)] % BANKS, :]

    def wait_filled(eng, name, i):
        eng.wait_ge(psum_filled, turn[(name, i)] + 1)

    def wait_read(eng, name, i):
        n = turn[(name, i)]
        eng.wait_ge(bank_read[n % BANKS], n // BANKS + 1)

    def read_value(name, i):
        n = turn[(name, i)]
        return bank_read[n % BANKS], n // BANKS + 1

    hyc_n = sum(n for _, n in where["hyc"].values())
    hyw_n = sum(n for _, n in where["hyw"].values())
    A_K = hyc_n
    A_G = A_K + 5120
    A_R = A_G + 2048
    hyc = arena[:, 0:hyc_n]

    def HC(name):
        a, n = where["hyc"][name]
        return hyc[:, a:a + n]

    def HC3(name, n):
        return HC(name).rearrange("p (k n) -> p k n", n=n)

    def HW(name):
        a, n = where["hyw"][name]
        return arena[:, A_R + a:A_R + a + n]

    Kr = area(A_K, 2, 2, 512)
    Ki = area(A_K + 2048, 2, 2, 512)
    Kr0 = area(A_K + 4096, 2, 512)
    G = area(A_G, 2, D)
    A_F = A_R + hyw_n
    filt = area(A_F, 2, 4, 512)
    A_FT = A_F + 4096
    mlp_h = area(A_FT, SEQ)
    mlp_k = area(A_FT + 256, SEQ)
    mlp_u = area(A_FT + 512, SEQ)
    rnorm = area(A_FT + 1024, 2, 512)
    fabs = area(A_FT + 2048, 2, 2, 512)
    bias_g = area(A_FT + 4096, 2, D)
    A_CTX = A_FT + 4096 + 2048
    xc = area(A_CTX, TT, D)
    hcT = area(A_CTX + 2048, KD, SEQ)
    ada_row = dve_junk[0:2, :].rearrange("p (a b) -> p a b", b=512)
    zcT = area(A_R, 12, SEQ)
    qkv = area(A_R + 3072, TT, 1536)
    kvc = area(A_R + 6144, TT, D)
    bias_qkv = area(A_R + 8192, 1536)
    A_M = A_R + 9728
    zpre = area(A_M, 4, SEQ)
    assert A_M + 1024 <= A_CTX
    vrow = area(A_M + 1024, TT, 512)
    prod_r = area(A_M + 2048, 2, 512)
    prod_i = area(A_M + 3072, 2, 512)
    tmp_a = area(A_M + 4096, 512)
    y1T = area(A_M + 4608, HY_T, SEQ)
    yhT = area(A_R, HY_T, SEQ)
    naq = area(0, TT, D)
    nat = area(2048, TT, D)
    nakc = area(4096, TT, 512)
    naqT = area(5120, 8, SEQ)
    nakcT = area(7168, 4, SEQ)
    assert 8192 <= A_G
    nabias = area(A_M, 2, TT * SEQ)
    namask = area(A_M + 1024, TT * SEQ)
    nap = area(A_M + 1536, 2, 512)
    napT = area(A_M + 2560, 4, SEQ)
    naoT = area(A_M + 3584, 4, SEQ)
    qk_g = area(A_M + 4608, 2 * HD)
    bias_gate = area(0, 2048)
    sig = area(2048, TT, 2048)
    merged = area(6144, TT, D)
    assert 6144 + 2048 <= A_G and A_M + 4736 <= ARENA
    keysT = area(0, 16, P)
    pqT = area(2048, 16, SEQ)
    scr = area(A_G + 2048, 16, P)
    scw = area(A_G + 4096, 16, P)
    cand = area(A_G + 6144, 8, 256)
    candw = area(A_G + 8192, 8, 256)
    oh = area(A_G + 10240, 8, 256)
    tops = area(A_G + 12288, 16, 16)
    topi_u = area(A_G + 12544, 256).bitcast(U32).rearrange("p (a b) -> p a b", b=16)
    topi = area(A_G + 12800, 16, 16)
    bests = area(A_G + 13056, 8, 16)
    bpos_u = area(A_G + 13184, 128).bitcast(U32).rearrange("p (a b) -> p a b", b=16)
    bpos = area(A_G + 13312, 8, 16)
    b_hi = area(A_G + 13440, 8, 16)
    b_lo = area(A_G + 13568, 8, 16)
    i_hi = area(A_G + 13696, 8, 16)
    P_END = ARENA - 700
    pidx = area(P_END, TT * 128).bitcast(I32).rearrange("p (a b) -> p a b", b=16)
    pgate = area(P_END + 256, TT * 8, 16)
    pidx_now = area(P_END + 512, 32).bitcast(I32)
    pdot = area(P_END + 544, 16)
    pact = area(P_END + 560, 16)
    pw = area(P_END + 576, 16)
    assert A_G + 13824 <= P_END
    u_rows = area(0, U_RING, D)
    v_rows = area(A_G + 2048, V_RING, D)
    assert U_RING * D <= A_G and A_G + 2048 + V_RING * D <= P_END
    diag = hT[:].rearrange("p a b -> p (a b)").rearrange("p (a b) -> p a b", b=P)

    qkv2 = area(0, TT, 2048)
    small2 = area(4096, TT, 104)
    qkT = area(4352, 10, SEQ)
    qiT = area(6912, 5, SEQ)
    isc, iscw = area(8192, TT, SEQ), area(8704, TT, SEQ)
    kid = area(9216, TT, P)
    madd = area(9216, TT, SEQ)
    rel = area(9728, 8, SEQ)
    pr = area(11776, 8, SEQ)
    prT = area(13824, TT, D)
    aT = area(16384, 8, SEQ)
    zs = area(18432, TT, SSD_INNER)
    xbcT = area(22528, 24, SEQ)
    X = area(0, TT, SSD_INNER)
    Xdt = area(4352, TT, SSD_INNER)
    Brow = area(8448, 512)
    Xdec = area(8960, SSD_INNER)
    cb = area(11008, 8, P)
    Lm = area(12032, 2, D)
    st = area(14080, 4, 512)
    yT = area(4352, 16, SEQ)
    sig2 = area(22528, TT, 2048)
    merged2 = area(8448, TT, D)
    gT = area(0, FT, SEQ)
    conv_o = area(5632, 8, SEQ)
    final_w = area(12032, D)
    amax2, asum2, ainv2 = sm(12, 8), sm(20, 8), sm(28, 8)
    x64, u64, v64 = sm(40, 64), sm(104, 64), sm(168, 64)
    dtb, alog, dskip = sm(244, 64), sm(308, 64), sm(372, 64)
    SCALE2 = HD2 ** -0.5

    def index_heads(b_):
        if b_ < 2:
            return 0, P, list(range(b_, IDX_HEADS, 2))
        first = 4 * ((b_ - 2) // 2) + b_ % 2
        return 1, SEQ, [first, first + 2]

    MAGIC = 1.5 * 2.0 ** 23
    C1, C2_, C3 = 6.28125, 0.0019350051879882812, 3.0199159819e-07
    BIG = lambda l: f"L{l}."
    U_SLOTS_PER_HEAD = TOPK // U_RING

    def row_b(name, a, n):
        return d[name][0:1, a:a + n].to_broadcast([P, n])

    block = ctx.enter_context(nc.Block())

    def finish(sp):
        sp.wait_ge(S("out_ready"), 2)
        sp.dma_start(out, x[:]).then_inc(S("out_stored"), 16)
        sp.wait_ge(S("out_stored"), 16)

    @block.sync
    def _(sp):
        sp.dma_start(consts[:], d["consts"]).then_inc(S("consts_in"), 16)
        sp.dma_start(x[:], d["x"].rearrange("p (a b) -> p a b", b=D)).then_inc(S("x_in"), 16)
        for c, (name, l, i, n, _) in enumerate(wplan):
            if c >= RING:
                wait_filled(sp, *wplan[c - RING][4])
            src = d[name][i] if l is None else d[name][l, i]
            sp.dma_start(wring[:, c % RING, 0:n], src).then_inc(weights_in[c % RING], 16)
        finish(sp)

    @block.tensor
    def _(pe):
        state = {"turn": 0, "chunk": 0}

        def open_(name, i):
            n = turn[(name, i)]
            assert n == state["turn"], (name, i, order[state["turn"]])
            state["turn"] += 1
            if n >= BANKS:
                pe.wait_ge(bank_read[n % BANKS], n // BANKS)
            return psum[:, n % BANKS, :]

        def close(ins):
            ins.then_inc(psum_filled, 1)

        def take(name, l=None):
            c = state["chunk"]
            assert wplan[c][:2] == (name, l), (wplan[c], name, l)
            state["chunk"] += 1
            pe.wait_ge(weights_in[c % RING], 16 * (c // RING + 1))
            return wring[:, c % RING, :]

        mm = lambda o, a, b, start, stop: nc.tensor.matmul(o, a, b, start=start, stop=stop, skip_group_check=True)

        def rows_mm(o, srcT, nk, t, w, n, start=True, stop=True, k0=0, at=0):
            W = w.shape[-1] // nk
            for k in range(nk):
                m = mm(o, srcT[:, k0 + k, t * P:(t + 1) * P], w[:, k * W + at:k * W + at + n],
                       start and k == 0, stop and k == nk - 1)
            return m

        def transposes(name, i, srcs):
            o = open_(name, i)
            for j, s in enumerate(srcs):
                n = s.shape[0]
                m = nc.tensor.transpose(o[0:s.shape[-1], j * n:(j + 1) * n], s, ident[0:n, 0:n])
            close(m)

        tile = lambda t: slice(t * P, (t + 1) * P)

        pe.wait_ge(S("consts_in"), 16)
        pe.wait_ge(S("hyc_in"), 16)
        pe.wait_ge(S("hyw_in"), 16)
        for i in range(3):
            o = open_("mlp", i)
            if i:
                pe.wait_ge(S("mlp_h"), i)
            rhs = HC("feats")[0:64, :] if i == 0 else mlp_h[0:64, :]
            close(mm(o[0:64, 0:SEQ], HW(f"f{i + 1}")[0:64, :], rhs, True, True))
        pe.wait_ge(S("mlp_h"), 3)
        for t in range(TT):
            for j in range(4):
                o = open_("filter", 4 * t + j)
                close(mm(o, mlp_h[0:64, tile(t)], HW("f4")[0:64, j * 512:(j + 1) * 512], True, True))
        for o_ in range(2):
            o = open_("absum", o_)
            pe.wait_ge(S("fabs_ready"), 2 * o_ + 2)
            for t in range(TT):
                for j in range(2):
                    m = mm(o, ones, fabs[:, t, j, :], t + j == 0, t + j == 2)
            close(m)
        for o_ in range(2):
            pe.wait_ge(S("filters_ready"), o_ + 1)
            for i in range(4):
                o = open_("dftf", 4 * o_ + i)
                f, kind = i % 2, i // 2
                for t in range(TT):
                    m = mm(o, HC3("dft_s" if kind else "dft_c", SEQ)[:, t, tile(f)],
                           filt[:, t, 2 * o_ + kind, :], t == 0, t == TT - 1)
                close(m)
            o = open_("nyq", o_)
            for t in range(TT):
                m = mm(o[0:1, :], HC("alt")[:, t:t + 1], filt[:, t, 2 * o_, :], t == 0, t == TT - 1)
            close(m)

        def ada_columns(ci):
            wait_read(pe, "ada", ADA_COLS[ci])
            o = open_("adaT", ci)
            for j in range(4):
                m = nc.tensor.transpose(o[:, 2 * j:2 * j + 2], ada_row[0:2, ci % 2, j * P:(j + 1) * P],
                                        ident[0:2, 0:2])
            close(m)

        pe.wait_ge(S("c_ready"), 1)
        for ch in range(12):
            w = take("w_ada")
            o = open_("ada", ch)
            for k in range(KD):
                if ch in ADA_COLS:
                    m = mm(o[0:2, :], cT[:, k, :], w[:, k * 512:(k + 1) * 512], k == 0, k == KD - 1)
                else:
                    m = mm(o, cT[:, k, 0:1].to_broadcast([P, P]), w[:, k * 512:(k + 1) * 512],
                           k == 0, k == KD - 1)
            close(m)
            if ch >= 1 and ch - 1 in ADA_COLS:
                ada_columns(ADA_COLS.index(ch - 1))

        pe.wait_ge(S("scaled"), 1)
        for k in range(KD):
            transposes("hT0", k, [xs[:, t, tile(k)] for t in range(TT)])
        for k in range(KD):
            transposes("hcT", k, [xc[:, t, tile(k)] for t in range(TT)])
        for k in range(KD):
            wait_read(pe, "hT0", k)
        for c in range(3):
            w = take("w_in")
            for m_ in range(4):
                o = open_("zhy", 4 * c + m_)
                for k in range(KD):
                    m = mm(o[:, 0:SEQ], w[:, k * 512 + m_ * P:k * 512 + (m_ + 1) * P], hT[:, k, :],
                           k == 0, k == KD - 1)
                close(m)
        for k in range(KD):
            wait_read(pe, "hcT", k)
        n = 0
        for j in range(3):
            w = take("w_in")
            for src in (hT, hcT)[:1 if j == 0 else 2]:
                for t in range(TT):
                    close(rows_mm(open_("zqkv", n), src, KD, t, w, 512))
                    n += 1

        pe.wait_ge(S("conv_done"), 4)
        for t in range(TT):
            transposes("vrow", t, [zcT[:, m_, tile(t)] for m_ in range(HY_T)])
        for o_ in range(2):
            for t in range(TT):
                wait_read(pe, "vrow" if o_ == 0 else "yrow", t)
            for i in range(4):
                f, kind = i // 2, i % 2
                o = open_("spec", 4 * o_ + i)
                for t in range(TT):
                    m = mm(o, HC3("dft_i" if kind else "dft_c", SEQ)[:, t, tile(f)], vrow[:, t, :],
                           t == 0, t == TT - 1)
                close(m)
            pe.wait_ge(S("product_ready"), 2 * o_ + 2)
            for m_ in range(HY_T):
                o = open_("conv", 4 * o_ + m_)
                for f in range(2):
                    mm(o[:, 0:SEQ], prod_r[:, f, tile(m_)], HC3("idft_r", SEQ)[:, f, :], f == 0, False)
                    m = mm(o[:, 0:SEQ], prod_i[:, f, tile(m_)], HC3("idft_i", SEQ)[:, f, :], False, f == 1)
                close(m)
            if o_ == 0:
                pe.wait_ge(S("y1_ready"), HY_T)
                for t in range(TT):
                    transposes("yrow", t, [y1T[:, m_, tile(t)] for m_ in range(HY_T)])

        pe.wait_ge(S("na_rows"), 1)
        for g in range(8):
            transposes("naT", g, [nat[:, t, tile(g)] for t in range(TT)])
        for g in range(4):
            transposes("nacT", g, [nakc[:, t, tile(g)] for t in range(TT)])
        for g in range(8):
            wait_read(pe, "naT", g)
        for g in range(4):
            wait_read(pe, "nacT", g)

        def na_scores(h):
            p_, s_ = h // 2, slice(64 * (h % 2), 64 * (h % 2) + 64)
            pe.wait_ge(S("bias_ready"), h + 1)
            for t in range(TT):
                o = open_("nas", 2 * h + t)
                q = naqT[s_, p_, tile(t)]
                mm(o[:, 0:SEQ], q, naqT[s_, 4 + p_, :], True, False)
                mm(o[:, 0:SEQ], ident, nabias[:, h % 2, t * SEQ:(t + 1) * SEQ], False, False)
                close(mm(o[:, SEQ:2 * SEQ], q, nakcT[s_, p_, :], False, True))

        def na_out(h):
            for t in range(TT):
                pe.wait_ge(S("na_prob"), 2 * h + t + 1)
                transposes("nap", 2 * h + t, [nap[:, t, tile(j)] for j in range(4)])
            for t in range(TT):
                wait_read(pe, "nap", 2 * h + t)
            o = open_("nao", h)
            p_ = h // 2
            for j in range(4):
                v = qkv[:, j, D + p_ * P:D + (p_ + 1) * P] if j < 2 else kvc[:, j - 2, 512 + p_ * P:512 + (p_ + 1) * P]
                m = mm(o[:, 0:SEQ], v, napT[:, j, :], j == 0, j == 3)
            close(m)

        for h in range(NA_HEADS):
            na_scores(h)
            if h >= 1:
                na_out(h - 1)
        na_out(NA_HEADS - 1)

        for c in range(4):
            w = take("w_in")
            for t in range(TT):
                close(rows_mm(open_("gate", 2 * c + t), hT, KD, t, w, 512))
        pe.wait_ge(S("yh_ready"), HY_T)
        wait_read(pe, "nao", NA_HEADS - 1)
        wait_read(pe, "nao", NA_HEADS - 2)
        for n, (name, src) in enumerate((("w_hy_out", yhT), ("w_na_out", naoT))):
            w = take(name)
            for t in range(TT):
                for half in range(2):
                    close(rows_mm(open_("mix", 4 * n + 2 * t + half), src, HY_T, t, w, 512, at=512 * half))
        pe.wait_ge(S("merged"), 1)
        for k in range(KD):
            transposes("mT", k, [merged[:, t, tile(k)] for t in range(TT)])
        for k in range(KD):
            wait_read(pe, "mT", k)
        for c in range(2):
            w = take("w_out")
            for t in range(TT):
                close(rows_mm(open_("wout", 2 * c + t), hT, KD, t, w, 512))

        pe.wait_ge(S("scaled"), 2)
        for k in range(KD):
            transposes("hfT", k, [xs[:, t, tile(k)] for t in range(TT)])
        for k in range(KD):
            wait_read(pe, "hfT", k)
        for t in range(TT):
            for half in range(2):
                transposes("hfrow", 2 * t + half, [hT[:, 4 * half + j, tile(t)] for j in range(4)])
        for c in range(4):
            w = take("w_pq")
            for m_ in range(4):
                o = open_("pq", 4 * c + m_)
                for k in range(KD):
                    m = mm(o[:, 0:SEQ], w[:, k * 512 + m_ * P:k * 512 + (m_ + 1) * P], hT[:, k, :],
                           k == 0, k == KD - 1)
                close(m)
        pe.wait_ge(S("keys_in"), 16)
        for m_ in range(16):
            wait_read(pe, "pq", m_)
        for t in range(TT):
            for q_ in range(4):
                o = open_("ps", 4 * t + q_)
                for j in range(4):
                    m = mm(o[:, tile(j)], pqT[:, 4 * q_ + j, tile(t)], keysT[:, 4 * q_ + j, :], j == 0, j == 3)
                close(m)

        for t in range(TT):
            acc = [open_("acc", 2 * t + half) for half in range(2)]
            for half in range(2):
                mm(acc[half], K("zeros"), G[:, 1, 0:512], True, False)
            for h in range(PEER_HEADS):
                g = t * PEER_HEADS + h
                pe.wait_ge(S("diag_ready"), g + 1)
                for j in range(TOPK):
                    pe.wait_ge(S(f"v_in{j}"), 16 * (g + 1))
                    for half in range(2):
                        m = mm(acc[half], diag[:, j, :], v_rows[:, j, half * 512:(half + 1) * 512], False,
                               False)
                    m.then_inc(S("v_used"), 1)
            for half in range(2):
                close(mm(acc[half], K("zeros"), G[:, 1, 0:512], False, True))

        for l in range(LAYERS):
            L = f"L{l}."

            def feature_mm(name, i, w, m_):
                o = open_(name, i)
                for k in range(KD):
                    m = mm(o[:, 0:SEQ], w[:, k * 512 + m_ * P:k * 512 + (m_ + 1) * P], hT[:, k, :],
                           k == 0, k == KD - 1)
                close(m)

            pe.wait_ge(S("scaled"), 3 + 2 * l)
            for k in range(KD):
                transposes(L + "hT", k, [xs[:, t, tile(k)] for t in range(TT)])
            for k in range(KD):
                wait_read(pe, L + "hT", k)
            for c in range(4):
                w = take("w2_qkv", l)
                for t in range(TT):
                    close(rows_mm(open_(L + "qkv", 2 * c + t), hT, KD, t, w, 512))
            w = take("w2_small", l)[:, 0:8 * 104]
            for t in range(TT):
                close(rows_mm(open_(L + "small", t)[:, 0:104], hT, KD, t, w, 104))
            for c in range(6):
                w = take("w2_xbc", l)
                for m_ in range(4):
                    feature_mm(L + "xbc", 4 * c + m_, w, m_)
            pe.wait_ge(S("roped"), l + 1)
            for h in range(10):
                transposes(L + "qT", h, [qkv2[:, t, tile(h)] for t in range(TT)])
            for h in range(5):
                transposes(L + "qiT", h, [kid[:, t, :] if h == 4 else qkv2[:, t, 1536 + h * P:1536 + (h + 1) * P]
                                          for t in range(TT)])
            for h in range(5):
                wait_read(pe, L + "qiT", h)
            for b_ in range(6):
                t, n_keys, heads_b = index_heads(b_)
                per = len(heads_b)
                o = open_(L + "is", b_)
                for j, h in enumerate(heads_b):
                    s_ = slice(64 * (h % 2), 64 * (h % 2) + 64)
                    m = mm(o[:, j * n_keys:(j + 1) * n_keys], qiT[s_, h // 2, tile(t)], qiT[s_, 4, 0:n_keys],
                           j == 0, j == per - 1)
                close(m)
            for c in range(4):
                w = take("w2_z", l)
                for t in range(TT):
                    close(rows_mm(open_(L + "z", 2 * c + t), hT, KD, t, w, 512))
            for h in range(10):
                wait_read(pe, L + "qT", h)
            for t in range(TT):
                n_keys, per = (P, 4) if t == 0 else (SEQ, 2)
                for b_ in range(8 // per):
                    o = open_(L + "s", 2 * t + b_)
                    for j in range(per):
                        h = b_ * per + j
                        m = mm(o[:, j * n_keys:(j + 1) * n_keys], qkT[:, h, tile(t)], qkT[:, 8 + h // 4, 0:n_keys],
                               j == 0, j == per - 1)
                    close(m)
                pe.wait_ge(S("prob2"), TT * l + t + 1)
                for b_ in range(2 * t + 2):
                    kt, half = b_ // 2, b_ % 2
                    transposes(L + "p", 2 * t + b_, [pr[:, 4 * half + j, tile(kt)] for j in range(4)])
                for b_ in range(2 * t + 2):
                    wait_read(pe, L + "p", 2 * t + b_)
                for c in range(KVH):
                    o = open_(L + "o", 2 * t + c)
                    for kt in range(t + 1):
                        m = mm(o, qkv2[:, kt, 1280 + c * P:1280 + (c + 1) * P], prT[:, kt, 512 * c:512 * c + 512],
                               kt == 0, kt == t)
                    close(m)
            pe.wait_ge(S("adt_ready"), l + 1)
            o = open_(L + "acs", 0)
            for c in range(TT):
                mm(o[:, 32 * c:32 * c + 32], upto, adt[:, 32 * c:32 * c + 32], c == 0, False)
            close(mm(o[:, 64:96], ones, adt[:, 0:32], False, True))
            pe.wait_ge(S("xbc_ready"), 24 * l + 24)
            for t in range(TT):
                for q_ in range(4):
                    transposes(L + "X", 4 * t + q_, [xbcT[:, 4 * q_ + j, tile(t)] for j in range(4)])
            transposes(L + "Brow", 0, [xbcT[:, 16 + g, tile(0)] for g in range(4)])
            for c in range(TT):
                o = open_(L + "cb", c)
                for g in range(4):
                    m = mm(o[:, tile(g)], xbcT[:, 16 + g, tile(c)], xbcT[:, 20 + g, tile(c)], g == 0, g == 3)
                close(m)
            wait_read(pe, L + "Brow", 0)
            pe.wait_ge(S("xdec_ready"), l + 1)
            for g in range(4):
                close(mm(open_(L + "st", g), Brow[:, tile(g)], Xdec[:, 512 * g:512 * g + 512], True, True))

            def ssd_out(i):
                g, c = i // TT, i % TT
                pe.wait_ge(S("decay_ready"), 8 * l + i + 1)
                o = open_(L + "y", i)
                for h in range(HPG):
                    m = mm(o[:, SSD_P * h:SSD_P * (h + 1)], Lm[:, i % 2, tile(h)],
                           Xdt[:, c, 512 * g + SSD_P * h:512 * g + SSD_P * (h + 1)], h == 0, h == HPG - 1)
                close(m)
                if c:
                    wait_read(pe, L + "st", g)
                    close(mm(open_(L + "yo", i), xbcT[:, 20 + g, tile(c)], st[:, g, :], True, True))

            for i in range(SSD_G * TT):
                g, c = i // TT, i % TT
                for half in range(2):
                    o = open_(L + "seg", 2 * i + half)
                    mm(o, ident, K("after"), True, False)
                    for j in range(4):
                        h = g * HPG + 4 * half + j
                        m = mm(o[:, tile(j)], adt[:, 32 * c + h:32 * c + h + 1].to_broadcast([P, P]), upto,
                               False, j == 3)
                    close(m)
                if i:
                    ssd_out(i - 1)
            ssd_out(SSD_G * TT - 1)
            for c in range(4):
                w = take("w2_g", l)
                for t in range(TT):
                    close(rows_mm(open_(L + "gate", 2 * c + t), hT, KD, t, w, 512))
            pe.wait_ge(S("y_ready"), l + 1)
            for m_ in range(16):
                transposes(L + "yT", m_, [X[:, t, tile(m_)] for t in range(TT)])
            for c in range(2):
                w = take("w2_pa", l)
                for t in range(TT):
                    close(rows_mm(open_(L + "pa", 2 * c + t), aT, KD, t, w, 512))
            for m_ in range(16):
                wait_read(pe, L + "yT", m_)
            for c in range(2):
                o2 = [open_(L + "ps", 2 * c + t) for t in range(TT)]
                for half in range(2):
                    w = take("w2_ps", l)
                    for t in range(TT):
                        m = rows_mm(o2[t], yT, KD, t, w, 512, start=half == 0, stop=half == 1, k0=8 * half)
                        if half:
                            close(m)
            pe.wait_ge(S("merged"), 2 + l)
            for k in range(KD):
                transposes(L + "mT", k, [merged2[:, t, tile(k)] for t in range(TT)])
            for k in range(KD):
                wait_read(pe, L + "mT", k)
            for c in range(2):
                w = take("w2_o", l)
                for t in range(TT):
                    close(rows_mm(open_(L + "wo", 2 * c + t), hT, KD, t, w, 512))
            pe.wait_ge(S("scaled"), 4 + 2 * l)
            for k in range(KD):
                transposes(L + "fT", k, [xs[:, t, tile(k)] for t in range(TT)])
            for k in range(KD):
                wait_read(pe, L + "fT", k)
            for c in range(FT // 2):
                w = take("w2_up", l)
                for m_ in range(4):
                    feature_mm(L + "up", 4 * c + m_, w, m_)
            pe.wait_ge(S("glu_ready"), FT * (l + 1))
            for c in range(4):
                o2 = [open_(L + "dn", 2 * c + t) for t in range(TT)]
                for half in range(2):
                    w = take("w2_dn", l)[:, 0:11 * 256]
                    for t in range(TT):
                        m = rows_mm(o2[t][:, 0:256], gT, 11, t, w, 256, start=half == 0, stop=half == 1,
                                    k0=11 * half)
                        if half:
                            close(m)

    @block.scalar
    def _(act):
        a = Progress(act, S("scalar_steps"))
        A = nc.scalar.activation
        act.dma_start(cols[:], d["cols"]).then_inc(S("cols_in"), 16)
        act.dma_start(arena[:, A_R:A_R + hyw_n], d["hyw"]).then_inc(S("hyw_in"), 16)
        act.dma_start(hyc, d["hyc"]).then_inc(S("hyc_in"), 16)

        def read_out(name, i, out_, in_, func=ACT.Copy, **kw):
            wait_filled(act, name, i)
            a.reaches(A(out_, in_, func, **kw), *read_value(name, i))

        def norm_std(n, srcs):
            for s_, v in enumerate(srcs):
                a.done(A(act_junk[:], v, ACT.Square, accum_out=ss[:, s_:s_ + 1]))
                a.settle()
            a.reaches(A(std[:, 0:len(srcs)], ss[:, 0:len(srcs)], ACT.Sqrt, scale=1.0 / D, bias=K("epscol")),
                     S("std_ready"), n + 1)

        def modulated(name, dst, s_, shift, v):
            for k in range(1, KD, 2):
                read_out(name, k, dst[:, k, :], bank(name, k)[:, 0:SEQ], ACT.Identity,
                         scale=mod_a[:, s_, k:k + 1], bias=adaT[:, shift + k, v:v + 1])

        act.wait_ge(S("cols_in"), 16)
        a.reaches(A(cT, V("c", 0, 16).rearrange("p (k v) -> p k v", v=2), ACT.Silu), S("c_ready"), 1)
        for i in range(3):
            act.wait_ge(S("mlp_arg"), i + 1)
            a.reaches(A(mlp_h[0:64, :], mlp_u[0:64, :], ACT.Sin), S("mlp_h"), i + 1)
        for t in range(TT):
            for j in range(4):
                wait_read(act, "filter", 4 * t + j)
        for o_ in range(2):
            if o_:
                wait_filled(act, "absum", 0)
            for t in range(TT):
                a.reaches(A(fabs[:, t, :, :], filt[:, t, 2 * o_:2 * o_ + 2, :], ACT.Abs), S("fabs_ready"),
                         2 * o_ + t + 1)
        for o_ in range(2):
            for i in range(4):
                f, kind = i % 2, i // 2
                wait_filled(act, "dftf", 4 * o_ + i)
                b_ = bank("dftf", 4 * o_ + i)
                if kind == 0 and f == 0:
                    a.done(A(Kr0[:, o_, :], b_, ACT.Copy))
                    a.settle()
                read_out("dftf", 4 * o_ + i, (Ki if kind else Kr)[:, o_, f, :], b_)
            read_out("nyq", o_, Kr0[0:1, o_, :], bank("nyq", o_)[0:1, :])
        act.wait_ge(S("x_in"), 16)
        act.wait_ge(S("ctx_in"), 16)
        norm_std(0, [x[:, 0, :], x[:, 1, :], xc[:, 0, :], xc[:, 1, :]])
        for ci, ch in enumerate(ADA_COLS):
            if ci >= 2:
                wait_filled(act, "adaT", ci - 2)
            read_out("ada", ch, ada_row[0:2, ci % 2, :], bank("ada", ch)[0:2, :])
        act.wait_ge(S("mod_ready"), 1)
        modulated("hT0", hT, 0, 0, 0)
        modulated("hcT", hcT, 1, 0, 1)
        for m_ in range(12):
            if m_ >= 4:
                act.wait_ge(S("conv_done"), m_ - 3)
            read_out("zhy", m_, zpre[:, m_ % 4, :], bank("zhy", m_)[:, 0:SEQ], ACT.Identity, bias=V("b_hy", m_))
        for t in range(TT):
            read_out("vrow", t, vrow[:, t, :], bank("vrow", t))
        for t in range(TT):
            read_out("yrow", t, vrow[:, t, :], bank("yrow", t))
        act.wait_ge(S("na_sumsq"), 1)
        a.reaches(A(nstd, nsum, ACT.Sqrt, scale=1.0 / HD, bias=K("epscol")), S("na_std"), 1)
        for g in range(8):
            read_out("naT", g, naqT[:, g, :], bank("naT", g)[:, 0:SEQ])
        for g in range(4):
            read_out("nacT", g, nakcT[:, g, :], bank("nacT", g)[:, 0:SEQ])

        def na_turned(h):
            if h >= 1:
                wait_filled(act, "nao", h - 1)
            for t in range(TT):
                read_out("nap", 2 * h + t, napT[:, :, t * P:(t + 1) * P],
                         bank("nap", 2 * h + t).rearrange("p (a b) -> p a b", b=P))
            s_ = slice(64 * (h % 2), 64 * (h % 2) + 64)
            read_out("nao", h, naoT[s_, h // 2, :], bank("nao", h)[s_, 0:SEQ])

        for h in range(NA_HEADS + 1):
            if h < NA_HEADS:
                for t in range(TT):
                    act.wait_ge(S("na_max"), 2 * h + t + 1)
                    if h >= 1:
                        wait_filled(act, "nap", 2 * h - 2 + t)
                    read_out("nas", 2 * h + t, nap[:, t, :], bank("nas", 2 * h + t), ACT.Exp,
                             bias=amax[:, 2 * h + t:2 * h + t + 1],
                             accum_out=asum[:, 2 * h + t:2 * h + t + 1])
            if h >= 1:
                na_turned(h - 1)
        for n in range(8):
            wait_read(act, "gate", n)
            c, t = n // 2, n % 2
            sg = sig[:, t, c * 512:(c + 1) * 512]
            a.reaches(A(sg, sg, ACT.Sigmoid), S("sig_ready"), n + 1)
        for k in range(1, KD, 2):
            read_out("mT", k, hT[:, k, :], bank("mT", k)[:, 0:SEQ])
        act.wait_ge(S("x_updated"), 1)
        norm_std(1, [x[:, 0, :], x[:, 1, :]])
        modulated("hfT", hT, 2, 16, 0)
        for n in range(1, 4, 2):
            read_out("hfrow", n, xs[:, n // 2, 512 * (n % 2):512 * (n % 2) + 512], bank("hfrow", n))
        for m_ in range(1, 16, 2):
            read_out("pq", m_, pqT[:, m_, :], bank("pq", m_)[:, 0:SEQ])
        for t in range(TT):
            if t:
                act.wait_ge(S("scores_used"), 1)
            for q_ in range(4):
                read_out("ps", 4 * t + q_, scr[:, 4 * q_:4 * q_ + 4, :],
                         bank("ps", 4 * t + q_).rearrange("p (a b) -> p a b", b=P))
            act.wait_ge(S("peer_shifted"), t + 1)
            a.reaches(A(bests, bests, ACT.Exp), S("peer_exp"), t + 1)
        for g in range(TT * PEER_HEADS):
            act.wait_ge(S("dots_ready"), g + 1)
            a.reaches(A(pact, pdot, ACT.Gelu), S("gelu_ready"), g + 1)

        def scaled_columns(name, n, dst, wcol):
            for k in range(1, n, 2):
                read_out(name, k, dst[:, k, :], bank(name, k)[:, 0:SEQ], ACT.Copy, scale=V(wcol, k))

        for l in range(LAYERS):
            L = f"L{l}."
            act.wait_ge(S("x_updated"), 2 + 2 * l)
            norm_std(2 + 2 * l, [x[:, 0, :], x[:, 1, :]])
            scaled_columns(L + "hT", KD, hT, f"mixw{l}")
            for n in range(8):
                read_out(L + "qkv", n, qkv2[:, n % 2, 512 * (n // 2):512 * (n // 2) + 512], bank(L + "qkv", n))
            for t in range(TT):
                read_out(L + "small", t, small2[:, t, :], bank(L + "small", t)[:, 0:104])
            act.wait_ge(S("rows_in"), 48)
            for m_ in range(24):
                act.wait_ge(S("xconv"), 24 * l + m_ + 1)
                a.reaches(A(xbcT[:, m_, :], xbcT[:, m_, :], ACT.Silu), S("xbc_ready"), 24 * l + m_ + 1)
            for h in range(10):
                read_out(L + "qT", h, qkT[:, h, :], bank(L + "qT", h)[:, 0:SEQ])
            for h in range(5):
                read_out(L + "qiT", h, qiT[:, h, :], bank(L + "qiT", h)[:, 0:SEQ])
            for b_ in range(6):
                _, n_keys, heads_b = index_heads(b_)
                if b_ == 2:
                    act.wait_ge(S("rel_used"), TT * l + 1)
                read_out(L + "is", b_, rel[:, heads_b[0]:heads_b[-1] + 1:2, 0:n_keys],
                         bank(L + "is", b_).rearrange("p (h k) -> p h k", k=n_keys), ACT.Relu)
            for n in range(8):
                read_out(L + "z", n, zs[:, n % 2, 512 * (n // 2):512 * (n // 2) + 512], bank(L + "z", n), ACT.Silu)
            for t in range(TT):
                n_keys = P * (t + 1)
                act.wait_ge(S("max2"), TT * l + t + 1)
                for h in range(H2):
                    a.done(A(pr[:, h, 0:n_keys], pr[:, h, 0:n_keys], ACT.Exp, bias=amax2[:, h:h + 1],
                             accum_out=asum2[:, h:h + 1]))
                a.settle()
                act.sem_inc(S("exp2"), 1)
                if t:
                    for c in range(KVH):
                        wait_filled(act, L + "o", c)
                for b_ in range(2 * t + 2):
                    kt, half = b_ // 2, b_ % 2
                    read_out(L + "p", 2 * t + b_, prT[:, kt, 512 * half:512 * half + 512], bank(L + "p", 2 * t + b_))
                for c in range(KVH):
                    read_out(L + "o", 2 * t + c, aT[:, 4 * c:4 * c + 4, t * P:(t + 1) * P],
                             bank(L + "o", 2 * t + c).rearrange("p (h q) -> p h q", q=P))
            act.wait_ge(S("dt_abs"), l + 1)
            a.done(A(u64, u64, ACT.Exp, scale=-1.0))
            a.reaches(A(negA, alog[:, 32 * l:32 * l + 32], ACT.Exp), S("dt_exp"), l + 1)
            act.wait_ge(S("acs_ready"), l + 1)
            a.done(A(eacs, acs_s, ACT.Exp))
            a.reaches(A(dstate, last_s, ACT.Exp), S("acs_exp"), l + 1)
            for t in range(TT):
                for q_ in range(4):
                    read_out(L + "X", 4 * t + q_, X[:, t, 512 * q_:512 * q_ + 512], bank(L + "X", 4 * t + q_))
            read_out(L + "Brow", 0, Brow, bank(L + "Brow", 0))
            for c in range(TT):
                read_out(L + "cb", c, cb[:, 4 * c:4 * c + 4, :],
                         bank(L + "cb", c).rearrange("p (g q) -> p g q", q=P))
            for g in range(4):
                read_out(L + "st", g, st[:, g, :], bank(L + "st", g))
            for i in range(SSD_G * TT):
                g, c = i // TT, i % TT
                if i >= 2:
                    wait_filled(act, L + "y", i - 2)
                for half in range(2):
                    wait_filled(act, L + "seg", 2 * i + half)
                    for j in range(4):
                        h = g * HPG + 4 * half + j
                        o = Lm[:, i % 2, (4 * half + j) * P:(4 * half + j + 1) * P]
                        src, bias = bank(L + "seg", 2 * i + half)[:, j * P:(j + 1) * P], nacs_s[:, 32 * c + h:32 * c + h + 1]
                        if j < 3:
                            a.done(A(o, src, ACT.Exp, bias=bias))
                        else:
                            a.reaches(A(o, src, ACT.Exp, bias=bias), *read_value(L + "seg", 2 * i + half))
            for n in range(8):
                read_out(L + "gate", n, sig2[:, n % 2, 512 * (n // 2):512 * (n // 2) + 512], bank(L + "gate", n),
                         ACT.Sigmoid)
            act.wait_ge(S("yz_ready"), l + 1)
            for t in range(TT):
                for g in range(SSD_G):
                    a.done(A(act_junk[:, 0:512], X[:, t, 512 * g:512 * g + 512], ACT.Square,
                             accum_out=gsum[:, 4 * t + g:4 * t + g + 1]))
                    a.settle()
            a.reaches(A(gstd, gsum, ACT.Sqrt, scale=1.0 / 512, bias=K("epscol")), S("gstd_ready"), l + 1)
            scaled_columns(L + "yT", 16, yT, f"snw{l}")
            for k in range(1, KD, 2):
                read_out(L + "mT", k, hT[:, k, :], bank(L + "mT", k)[:, 0:SEQ])
            act.wait_ge(S("x_updated"), 3 + 2 * l)
            norm_std(3 + 2 * l, [x[:, 0, :], x[:, 1, :]])
            scaled_columns(L + "fT", KD, hT, f"ffnw{l}")
            for i in range(FT):
                act.wait_ge(S("gate_conv"), FT * l + i + 1)
                o = conv_o[:, (i // 2) % 2 * 4 + i % 2, :]
                a.reaches(A(o, o, ACT.Silu), S("gate_silu"), FT * l + i + 1)
        act.wait_ge(S("x_updated"), 6)
        norm_std(6, [x[:, 0, :], x[:, 1, :]])

    @block.vector
    def _(dve):
        v = Progress(dve, S("vector_steps"))
        T = nc.vector

        def readv(name, i, ins):
            v.reaches(ins, *read_value(name, i))

        def norm_scale(n, srcs, dsts):
            dve.wait_ge(S("std_ready"), n + 1)
            m = len(srcs)
            v.done(T.reciprocal(rinv[:, 0:m], std[:, 0:m]))
            v.settle()
            for i, (s_, o) in enumerate(zip(srcs, dsts)):
                ins = T.tensor_scalar(o, s_, rinv[:, i:i + 1], None, ALU.mult)
                if i < m - 1:
                    v.done(ins)
            v.reaches(ins, S("scaled"), n + 1)

        def modulated(name, dst, s_, shift, c):
            for k in range(0, KD, 2):
                wait_filled(dve, name, k)
                readv(name, k, T.tensor_scalar(dst[:, k, :], bank(name, k)[:, 0:SEQ], mod_a[:, s_, k:k + 1],
                                               adaT[:, shift + k, c:c + 1], ALU.mult, ALU.add))

        def tt(o, a_, b_, op):
            v.done(T.tensor_tensor(o, a_, b_, op))

        def ts(o, a_, s1, s2, op0, op1=None):
            v.done(T.tensor_scalar(o, a_, s1, s2, op0, op1) if op1 is not None else
                   T.tensor_scalar(o, a_, s1, None, op0))

        def stt(o, a_, s_, b_, op0, op1):
            v.done(T.scalar_tensor_tensor(out=o, in0=a_, scalar=s_, in1=b_, op0=op0, op1=op1))

        dve.wait_ge(S("cols_in"), 16)
        u, kk = mlp_u[0:64, :], mlp_k[0:64, :]
        for i in range(3):
            wait_filled(dve, "mlp", i)
            readv("mlp", i, T.tensor_scalar(u, bank("mlp", i)[0:64, 0:SEQ], V(f"f{i + 1}b")[0:64, :],
                                            V("freq")[0:64, :], ALU.add, ALU.mult))
            v.settle()
            ts(kk, u, 1.0 / (2 * math.pi), MAGIC, ALU.mult, ALU.add)
            v.settle()
            ts(kk, kk, -MAGIC, None, ALU.add)
            for cc in (C1, C2_, C3):
                v.settle()
                stt(u, kk, -cc, u, ALU.mult, ALU.add)
            v.settle()
            v.reaches(T.tensor_scalar(u, u, 3.1415925, -3.1415925, ALU.min, ALU.max), S("mlp_arg"), i + 1)
        dve.wait_ge(S("hyc_in"), 16)
        for t in range(TT):
            for j in range(4):
                wait_filled(dve, "filter", 4 * t + j)
                readv("filter", 4 * t + j, T.tensor_tensor(filt[:, t, j, :], bank("filter", 4 * t + j),
                                                           HC3("decay", 512)[:, t, :], ALU.mult))
        for o_ in range(2):
            wait_filled(dve, "absum", o_)
            readv("absum", o_, T.reciprocal(rnorm[:, o_, :], bank("absum", o_)))
            for t in range(TT):
                fw, bw, tmp = filt[:, t, 2 * o_, :], filt[:, t, 2 * o_ + 1, :], dve_junk[:, t * 512:(t + 1) * 512]
                v.settle()
                if t == 0:
                    stt(tmp, bw, HC("not_first"), fw, ALU.mult, ALU.add)
                else:
                    tt(tmp, bw, fw, ALU.add)
                v.settle()
                tt(bw, bw, fw, ALU.subtract)
                v.settle()
                tt(fw, tmp, rnorm[:, o_, :], ALU.mult)
                ins = T.tensor_tensor(bw, bw, rnorm[:, o_, :], ALU.mult)
                if t == TT - 1:
                    v.reaches(ins, S("filters_ready"), o_ + 1)
                else:
                    v.done(ins)
        norm_scale(0, [x[:, 0, :], x[:, 1, :], xc[:, 0, :], xc[:, 1, :]],
                   [xs[:, 0, :], xs[:, 1, :], xc[:, 0, :], xc[:, 1, :]])
        dve.wait_ge(S("bias_g_in"), 32)
        for ch in range(12):
            if ch - 1 in ADA_COLS:
                ci = ADA_COLS.index(ch - 1)
                wait_filled(dve, "adaT", ci)
                readv("adaT", ci, T.tensor_tensor(
                    adaT[:, 4 * ci:4 * ci + 4, :], bank("adaT", ci)[:, 0:8].rearrange("p (j v) -> p j v", v=2),
                    V("b_ada", 4 * (ch - 1), 4).unsqueeze(2).to_broadcast([P, 4, 2]), ALU.add))
                v.settle()
            if ch not in ADA_COLS:
                wait_filled(dve, "ada", ch)
                g_, half = ch // 10, ch % 2
                gs = G[:, g_, 512 * half:512 * half + 512]
                readv("ada", ch, T.tensor_tensor(gs, bank("ada", ch), bias_g[:, g_, 512 * half:512 * half + 512],
                                                 ALU.add))
        v.settle()
        for s_, (sc, c, g_) in enumerate(((8, 0, "g1n"), (8, 1, "g1n"), (24, 0, "g2n"))):
            ins = T.scalar_tensor_tensor(out=mod_a[:, s_, :], in0=adaT[:, sc:sc + 8, c], scalar=1.0,
                                         in1=V(g_, 0, 8), op0=ALU.add, op1=ALU.mult)
            if s_ == 2:
                v.reaches(ins, S("mod_ready"), 1)
            else:
                v.done(ins)
        v.settle()
        modulated("hT0", hT, 0, 0, 0)
        modulated("hcT", hcT, 1, 0, 1)
        for m_ in range(12):
            wait_read(dve, "zhy", m_)
            z, o = zpre[:, m_ % 4, :], zcT[:, m_, :]
            ts(o, z, V("cw", 12 + m_), V("cb", m_), ALU.mult, ALU.add)
            v.settle()
            stt(o[:, 1:SEQ], z[:, 0:SEQ - 1], V("cw", m_), o[:, 1:SEQ], ALU.mult, ALU.add)
            v.settle()
            v.reaches(T.scalar_tensor_tensor(out=o[:, 0:SEQ - 1], in0=z[:, 1:SEQ], scalar=V("cw", 24 + m_),
                                            in1=o[:, 0:SEQ - 1], op0=ALU.mult, op1=ALU.add),
                     S("conv_done"), m_ + 1)
        dve.wait_ge(S("bias_qkv_in"), 16)
        n = 0
        for j in range(3):
            for src in range(1 if j == 0 else 2):
                for t in range(TT):
                    wait_filled(dve, "zqkv", n)
                    o = qkv[:, t, j * 512:(j + 1) * 512] if src == 0 else kvc[:, t, (j - 1) * 512:j * 512]
                    readv("zqkv", n, T.tensor_tensor(o, bank("zqkv", n), bias_qkv[:, j * 512:(j + 1) * 512], ALU.add))
                    n += 1
        for o_ in range(2):
            for f in range(2):
                yr, yi = bank("spec", 4 * o_ + 2 * f), bank("spec", 4 * o_ + 2 * f + 1)
                kr, ki = Kr[:, o_, f, :], Ki[:, o_, f, :]
                k2 = Kr0[:, o_, :] if f == 0 else kr
                wait_filled(dve, "spec", 4 * o_ + 2 * f + 1)
                v.settle()
                tt(prod_r[:, f, :], yr, kr, ALU.mult)
                tt(tmp_a, yi, ki, ALU.mult)
                readv("spec", 4 * o_ + 2 * f, T.tensor_tensor(prod_i[:, f, :], yr, ki, ALU.mult))
                v.settle()
                tt(prod_r[:, f, :], prod_r[:, f, :], tmp_a, ALU.subtract)
                v.settle()
                readv("spec", 4 * o_ + 2 * f + 1, T.tensor_tensor(tmp_a, yi, k2, ALU.mult))
                v.settle()
                v.reaches(T.tensor_tensor(prod_i[:, f, :], prod_i[:, f, :], tmp_a, ALU.add),
                         S("product_ready"), 2 * o_ + f + 1)
            src, dst, gate0 = (zcT, y1T, 4) if o_ == 0 else (y1T, yhT, 8)
            for m_ in range(HY_T):
                wait_filled(dve, "conv", 4 * o_ + m_)
                readv("conv", 4 * o_ + m_, T.scalar_tensor_tensor(
                    out=dst[:, m_, :], in0=src[:, m_, :], scalar=V("skip", 4 * o_ + m_),
                    in1=bank("conv", 4 * o_ + m_)[:, 0:SEQ], op0=ALU.mult, op1=ALU.add))
                v.settle()
                v.reaches(T.tensor_tensor(dst[:, m_, :], dst[:, m_, :], zcT[:, gate0 + m_, :], ALU.mult),
                         S("y1_ready" if o_ == 0 else "yh_ready"), m_ + 1)
        wait_filled(dve, "conv", 7)
        heads = lambda ap: ap.rearrange("p (h e) -> p h e", e=HD)
        for t in range(TT):
            tt(nat[:, t, :], qkv[:, t, 0:D], qkv[:, t, 0:D], ALU.mult)
            tt(nakc[:, t, :], kvc[:, t, 0:512], kvc[:, t, 0:512], ALU.mult)
        v.settle()
        for t in range(TT):
            v.done(T.tensor_reduce(nsum[:, 16 * t:16 * t + 16], heads(nat[:, t, :]), AX, ALU.add))
            ins = T.tensor_reduce(nsum[:, 32 + 8 * t:40 + 8 * t], heads(nakc[:, t, :]), AX, ALU.add)
            if t == 0:
                v.done(ins)
            else:
                v.reaches(ins, S("na_sumsq"), 1)
        dve.wait_ge(S("na_std"), 1)
        v.done(T.reciprocal(ninv, nstd))
        v.settle()
        for t in range(TT):
            ts(ninv[:, 16 * t:16 * t + 8], ninv[:, 16 * t:16 * t + 8], HD ** -0.5, None, ALU.mult)
        v.settle()
        dve.wait_ge(S("qk_g_in"), 16)
        for t in range(TT):
            inv = ninv[:, 16 * t:16 * t + 16].unsqueeze(2).to_broadcast([P, 16, HD])
            tt(heads(naq[:, t, :]), heads(qkv[:, t, 0:D]), inv, ALU.mult)
            inv = ninv[:, 32 + 8 * t:40 + 8 * t].unsqueeze(2).to_broadcast([P, 8, HD])
            tt(heads(nakc[:, t, :]), heads(kvc[:, t, 0:512]), inv, ALU.mult)
        v.settle()
        for t in range(TT):
            for s_ in range(2):
                g_ = qk_g[:, HD * s_:HD * (s_ + 1)].unsqueeze(1).to_broadcast([P, 8, HD])
                hs = heads(naq[:, t, 512 * s_:512 * s_ + 512])
                tt(hs, hs, g_, ALU.mult)
            tt(heads(nakc[:, t, :]), heads(nakc[:, t, :]), g_, ALU.mult)
        v.settle()
        for t in range(TT):
            c64 = K("rope_c")[:, HD * t:HD * t + HD].unsqueeze(1).to_broadcast([P, 16, HD])
            tt(heads(nat[:, t, :]), heads(naq[:, t, :]), c64, ALU.mult)
            for ab in range(2):
                pick = lambda ap: ap.rearrange("p (h f b e) -> p h f b e", f=2, b=2, e=16)
                for f in range(2):
                    s64 = K("rope_s")[:, HD * t + 32 * f + 16 * ab:HD * t + 32 * f + 16 * ab + 16]
                    tt(pick(dve_junk[:])[:, :, f, ab, :], pick(naq[:, t, :])[:, :, f, 1 - ab, :],
                       s64.unsqueeze(1).to_broadcast([P, 16, 16]), ALU.mult)
            v.settle()
            ins = T.tensor_tensor(nat[:, t, :], nat[:, t, :], dve_junk[:], ALU.add)
            if t == 0:
                v.done(ins)
                v.settle()
            else:
                v.reaches(ins, S("na_rows"), 1)
        dve.wait_ge(S("na_mask_in"), 16)

        def masked_bias(h):
            dve.wait_ge(S(f"rpb_in{h % 2}"), 16 * (h // 2 + 1))
            v.reaches(T.tensor_tensor(nabias[:, h % 2, :], nabias[:, h % 2, :], namask, ALU.add),
                     S("bias_ready"), h + 1)

        masked_bias(0)
        for h in range(NA_HEADS):
            if h + 1 < NA_HEADS:
                masked_bias(h + 1)
            for t in range(TT):
                i = 2 * h + t
                wait_filled(dve, "nas", i)
                v.reaches(T.tensor_reduce(amax[:, i:i + 1], bank("nas", i), AX, ALU.max, negate=True),
                         S("na_max"), i + 1)
            for t in range(TT):
                i = 2 * h + t
                wait_read(dve, "nas", i)
                v.done(T.reciprocal(ainv[:, i:i + 1], asum[:, i:i + 1]))
                v.settle()
                v.reaches(T.tensor_scalar(nap[:, t, :], nap[:, t, :], ainv[:, i:i + 1], None, ALU.mult),
                         S("na_prob"), i + 1)
        dve.wait_ge(S("bias_gate_in"), 16)
        wait_filled(dve, "nao", NA_HEADS - 1)
        for n in range(8):
            c, t = n // 2, n % 2
            wait_filled(dve, "gate", n)
            readv("gate", n, T.tensor_tensor(sig[:, t, c * 512:(c + 1) * 512], bank("gate", n),
                                             bias_gate[:, c * 512:(c + 1) * 512], ALU.add))
        dve.wait_ge(S("sig_ready"), 8)
        for n in range(8):
            src, t, half = n // 4, n // 2 % 2, n % 2
            sg = sig[:, t, D * src + 512 * half:D * src + 512 * half + 512]
            mg = merged[:, t, 512 * half:512 * half + 512]
            wait_filled(dve, "mix", n)
            if src == 0:
                readv("mix", n, T.tensor_tensor(mg, bank("mix", n), sg, ALU.mult))
            else:
                readv("mix", n, T.tensor_tensor(sg, bank("mix", n), sg, ALU.mult))
                v.settle()
                ins = T.tensor_tensor(mg, mg, sg, ALU.add)
                if n == 7:
                    v.reaches(ins, S("merged"), 1)
                else:
                    v.done(ins)
        for k in range(0, KD, 2):
            wait_filled(dve, "mT", k)
            readv("mT", k, T.tensor_copy(hT[:, k, :], bank("mT", k)[:, 0:SEQ]))
        for n in range(4):
            c, t = n // 2, n % 2
            wait_filled(dve, "wout", n)
            tmp = dve_junk[:, 512 * (n % 2):512 * (n % 2) + 512]
            readv("wout", n, T.tensor_tensor(tmp, bank("wout", n), G[:, 0, 512 * c:512 * c + 512], ALU.mult))
            v.settle()
            xv = x[:, t, 512 * c:512 * c + 512]
            ins = T.tensor_tensor(xv, xv, tmp, ALU.add)
            if n == 3:
                v.reaches(ins, S("x_updated"), 1)
            else:
                v.done(ins)
        norm_scale(1, [x[:, 0, :], x[:, 1, :]], [xs[:, 0, :], xs[:, 1, :]])
        modulated("hfT", hT, 2, 16, 0)
        for n in range(0, 4, 2):
            wait_filled(dve, "hfrow", n)
            readv("hfrow", n, T.tensor_copy(xs[:, n // 2, 512 * (n % 2):512 * (n % 2) + 512], bank("hfrow", n)))
        for m_ in range(0, 16, 2):
            wait_filled(dve, "pq", m_)
            readv("pq", m_, T.tensor_copy(pqT[:, m_, :], bank("pq", m_)[:, 0:SEQ]))

        def best_sixteen(n, vals, work, top, pos, freed=None):
            for i in range(n):
                v.done(T.max(top[:, i, 0:8], vals[:, i, :]))
            v.settle()
            for i in range(n):
                v.done(T.max_index(pos[:, i, 0:8], top[:, i, 0:8], vals[:, i, :]))
            for i in range(n):
                ins = T.match_replace(work[:, i, :], top[:, i, 0:8], vals[:, i, :], TAKEN)
                if freed and i == n - 1:
                    v.reaches(ins, *freed)
                else:
                    v.done(ins)
            v.settle()
            for i in range(n):
                v.done(T.max(top[:, i, 8:16], work[:, i, :]))
            v.settle()
            for i in range(n):
                v.done(T.max_index(pos[:, i, 8:16], top[:, i, 8:16], work[:, i, :]))
            v.settle()

        bc = lambda ap, ax, shape: ap.unsqueeze(ax).to_broadcast(shape)
        for t in range(TT):
            for q_ in range(4):
                wait_read(dve, "ps", 4 * t + q_)
            best_sixteen(16, scr, scw, tops, topi_u, (S("scores_used"), t + 1))
            v.done(T.tensor_copy(topi, topi_u))
            th = tops.rearrange("p (h s) k -> p h s k", s=2)
            tt(cand.rearrange("p h (a b) -> p h a b", b=16), bc(th[:, :, 0, :], 3, [P, 8, 16, 16]),
               bc(th[:, :, 1, :], 2, [P, 8, 16, 16]), ALU.add)
            v.settle()
            best_sixteen(8, cand, candw, bests, bpos_u)
            hi_u, lo_u = b_hi.bitcast(U32), b_lo.bitcast(U32)
            ts(hi_u, bpos_u, 4, None, ALU.logical_shift_right)
            ts(lo_u, bpos_u, 15, None, ALU.bitwise_and)
            v.settle()
            v.done(T.tensor_copy(bpos, hi_u))
            v.settle()
            v.done(T.tensor_copy(b_hi, lo_u))
            v.settle()
            ti = topi.rearrange("p (h s) k -> p h s k", s=2)
            oh3 = oh.rearrange("p h (k a) -> p (h k) a", a=16)
            oh4 = oh.rearrange("p h (k a) -> p h k a", a=16)
            flat = lambda ap: ap.rearrange("p h k -> p (h k)")
            for s_, (pos, dst) in enumerate(((bpos, i_hi), (b_hi, b_lo))):
                tt(oh3, bc(flat(pos), 2, [P, 128, 16]), bc(K("count16"), 1, [P, 128, 16]), ALU.is_equal)
                v.settle()
                tt(oh4, oh4, bc(ti[:, :, s_, :], 2, [P, 8, 16, 16]), ALU.mult)
                v.settle()
                v.done(T.tensor_reduce(flat(dst), oh3, AX, ALU.add))
                v.settle()
            stt(pidx[:, 8 * t:8 * t + 8, :], i_hi, float(N_KEYS), b_lo, ALU.mult, ALU.add)
            v.done(T.tensor_copy(bpos[:, :, 0], bests[:, :, 0]))
            v.settle()
            v.reaches(T.tensor_tensor(bests, bests, bc(bpos[:, :, 0], 2, [P, 8, 16]), ALU.subtract),
                     S("peer_shifted"), t + 1)
            dve.wait_ge(S("peer_exp"), t + 1)
            v.done(T.tensor_reduce(bpos[:, :, 0], bests, AX, ALU.add))
            v.settle()
            v.done(T.reciprocal(bpos[:, :, 1], bpos[:, :, 0]))
            v.settle()
            tt(pgate[:, 8 * t:8 * t + 8, :], bests, bc(bpos[:, :, 1], 2, [P, 8, 16]), ALU.mult)
            v.settle()

        heads_n = TT * PEER_HEADS

        def stage(g):
            v.reaches(T.tensor_copy(pidx_now[:, TOPK * (g % 2):TOPK * (g % 2) + TOPK], pidx[:, g, :]),
                     S("picks_ready"), g + 1)

        for n in range(8):
            wait_filled(dve, "ps", n)
        stage(0)
        stage(1)
        for g in range(heads_n):
            t = g // PEER_HEADS
            for j in range(TOPK):
                s_ = j % U_RING
                dve.wait_ge(S(f"u_in{s_}"), 16 * (U_SLOTS_PER_HEAD * g + j // U_RING + 1))
                v.settle()
                v.reaches(T.tensor_tensor_reduce(out=dve_junk[:], in0=u_rows[:, s_, :], in1=xs[:, t, :], scale=1.0,
                                                scalar=0.0, op0=ALU.mult, op1=ALU.add,
                                                accum_out=pdot[:, j:j + 1]), S("u_used"), TOPK * g + j + 1)
                if j == 9 and 1 <= g < heads_n - 1:
                    dve.wait_ge(S("v_used"), TOPK * g)
                    stage(g + 1)
            v.settle()
            dve.sem_inc(S("dots_ready"), 1)
            dve.wait_ge(S("gelu_ready"), g + 1)
            tt(pw, pact, pgate[:, g, :], ALU.mult)
            v.settle()
            if g:
                dve.wait_ge(S("v_used"), TOPK * g)
            v.reaches(T.tensor_tensor(diag, bc(ident, 1, [P, TOPK, P]), bc(pw, 2, [P, TOPK, P]), ALU.mult),
                     S("diag_ready"), g + 1)
            if g % PEER_HEADS == PEER_HEADS - 1:
                for half in range(2):
                    wait_filled(dve, "acc", 2 * t + half)
                    hs = slice(512 * half, 512 * half + 512)
                    readv("acc", 2 * t + half, T.tensor_tensor(dve_junk[:, hs], bank("acc", 2 * t + half),
                                                               G[:, 1, hs], ALU.mult))
                    v.settle()
                    ins = T.tensor_tensor(x[:, t, hs], x[:, t, hs], dve_junk[:, hs], ALU.add)
                    if g == heads_n - 1 and half:
                        v.reaches(ins, S("x_updated"), 2)
                    else:
                        v.done(ins)
                        v.settle()

        def scaled_columns(name, n, dst, wcol):
            for k in range(0, n, 2):
                wait_filled(dve, name, k)
                readv(name, k, T.tensor_scalar(dst[:, k, :], bank(name, k)[:, 0:SEQ], V(wcol, k), None, ALU.mult))

        def rope2(view, heads_, r, c_, s_):
            xr = view[:, :, 0:2 * r]
            t1 = dve_junk[:, 0:heads_ * 2 * r].rearrange("p (h e) -> p h e", e=2 * r)
            t2 = dve_junk[:, 512:512 + heads_ * 2 * r].rearrange("p (h e) -> p h e", e=2 * r)
            tt(t1, xr, bc(c_, 1, [P, heads_, 2 * r]), ALU.mult)
            for ab in range(2):
                tt(t2[:, :, ab * r:(ab + 1) * r], xr[:, :, (1 - ab) * r:(2 - ab) * r],
                   bc(s_[:, ab * r:(ab + 1) * r], 1, [P, heads_, r]), ALU.mult)
            v.settle()
            tt(xr, t1, t2, ALU.add)
            v.settle()

        def conv_in(name, i, o, wcol, bcol, taps, stride, col):
            wait_filled(dve, name, i)
            ps = bank(name, i)[:, 0:SEQ]
            ts(o, ps, V(wcol, stride * (taps - 1) + col), V(bcol, col), ALU.mult, ALU.add)
            for j in range(1, taps):
                v.settle()
                ins = T.scalar_tensor_tensor(out=o[:, j:SEQ], in0=ps[:, 0:SEQ - j],
                                             scalar=V(wcol, stride * (taps - 1 - j) + col), in1=o[:, j:SEQ],
                                             op0=ALU.mult, op1=ALU.add)
                if j < taps - 1:
                    v.done(ins)
            readv(name, i, ins)
            v.settle()

        for l in range(LAYERS):
            L = f"L{l}."
            norm_scale(2 + 2 * l, [x[:, 0, :], x[:, 1, :]], [xs[:, 0, :], xs[:, 1, :]])
            scaled_columns(L + "hT", KD, hT, f"mixw{l}")
            for n in range(8):
                wait_read(dve, L + "qkv", n)
            for t in range(TT):
                wait_read(dve, L + "small", t)
                rope2(qkv2[:, t, 0:1280].rearrange("p (h e) -> p h e", e=HD2), 10, 16,
                      K("rope2_ca")[:, 32 * t:32 * t + 32], K("rope2_sa")[:, 32 * t:32 * t + 32])
                rope2(qkv2[:, t, 1536:2048].rearrange("p (h e) -> p h e", e=IDX_DIM), 8, 8,
                      K("rope2_ci")[:, 16 * t:16 * t + 16], K("rope2_si")[:, 16 * t:16 * t + 16])
                rope2(small2[:, t, 0:64].unsqueeze(1), 1, 8,
                      K("rope2_ci")[:, 16 * t:16 * t + 16], K("rope2_si")[:, 16 * t:16 * t + 16])
                v.done(T.tensor_copy(kid[:, t, 0:64], small2[:, t, 0:64]))
                v.done(T.tensor_copy(kid[:, t, 64:128], small2[:, t, 0:64]))
            v.settle()
            dve.sem_inc(S("roped"), 1)
            for m_ in range(24):
                conv_in(L + "xbc", m_, xbcT[:, m_, :], f"scw{l}", f"scb{l}", 4, 24, m_)
                dve.sem_inc(S("xconv"), 1)
            dve.wait_ge(S("rows_in"), 48)
            h64 = lambda ap: ap.rearrange("p (t h) -> p t h", h=32)
            tt(h64(x64), small2[:, :, 72:104], bc(dtb[:, 32 * l:32 * l + 32], 1, [P, TT, 32]), ALU.add)
            v.settle()
            ts(v64, x64, -1.0, None, ALU.mult)
            v.settle()
            v.reaches(T.tensor_tensor(u64, x64, v64, ALU.max), S("dt_abs"), l + 1)
            for t in range(TT):
                n_keys = P * (t + 1)
                for b_ in range(2) if t == 0 else range(2, 6):
                    wait_read(dve, L + "is", b_)
                sc, sw = isc[:, t, 0:n_keys], iscw[:, t, 0:n_keys]
                ca = K("causal")[:, SEQ * t:SEQ * t + n_keys]
                wi = small2[:, t, 64:72]
                ts(sc, rel[:, 0, 0:n_keys], wi[:, 0:1], None, ALU.mult)
                for h in range(1, IDX_HEADS):
                    v.settle()
                    ins = T.scalar_tensor_tensor(out=sc, in0=rel[:, h, 0:n_keys], scalar=wi[:, h:h + 1], in1=sc,
                                                 op0=ALU.mult, op1=ALU.add)
                    if h < IDX_HEADS - 1:
                        v.done(ins)
                v.reaches(ins, S("rel_used"), TT * l + t + 1)
                v.settle()
                tt(sc, sc, ca, ALU.add)
                for r in range(SEL // 8):
                    a_, b_ = (sc, sw) if r % 2 == 0 else (sw, sc)
                    v.settle()
                    v.done(T.max(best8, a_))
                    v.settle()
                    v.done(T.match_replace(b_, best8, a_, TAKEN))
                v.settle()
                ts(sw, sc, TAKEN, -NEG, ALU.is_equal, ALU.mult)
                v.settle()
                stt(madd[:, t, 0:n_keys], sw, NEG, ca, ALU.add, ALU.add)
            v.settle()
            for t in range(TT):
                n_keys, per = (P, 4) if t == 0 else (SEQ, 2)
                if t:
                    wait_filled(dve, L + "p", 1)
                for b_ in range(8 // per):
                    wait_filled(dve, L + "s", 2 * t + b_)
                    readv(L + "s", 2 * t + b_, T.scalar_tensor_tensor(
                        out=pr[:, b_ * per:(b_ + 1) * per, 0:n_keys],
                        in0=bank(L + "s", 2 * t + b_).rearrange("p (h k) -> p h k", k=n_keys), scalar=SCALE2,
                        in1=bc(madd[:, t, 0:n_keys], 1, [P, per, n_keys]), op0=ALU.mult, op1=ALU.add))
                v.settle()
                v.reaches(T.tensor_reduce(amax2, pr[:, :, 0:n_keys], AX, ALU.max, negate=True), S("max2"),
                         TT * l + t + 1)
                dve.wait_ge(S("exp2"), TT * l + t + 1)
                v.done(T.reciprocal(ainv2, asum2))
                v.settle()
                v.reaches(T.tensor_tensor(pr[:, :, 0:n_keys], pr[:, :, 0:n_keys], bc(ainv2, 2, [P, 8, n_keys]),
                                         ALU.mult), S("prob2"), TT * l + t + 1)
            dve.wait_ge(S("dt_exp"), l + 1)
            t2_, p_ = dve_junk[:, 0:64], dve_junk[:, 64:128]
            ts(v64, u64, 2.0, None, ALU.add)
            v.settle()
            v.done(T.reciprocal(v64, v64))
            v.settle()
            tt(v64, u64, v64, ALU.mult)
            v.settle()
            tt(t2_, v64, v64, ALU.mult)
            v.settle()
            ts(p_, t2_, 1.0 / 15, None, ALU.mult)
            for n in (13, 11, 9, 7, 5, 3):
                v.settle()
                stt(p_, p_, 1.0 / n, t2_, ALU.add, ALU.mult)
            v.settle()
            stt(p_, p_, 1.0, v64, ALU.add, ALU.mult)
            v.settle()
            ts(p_, p_, 2.0, None, ALU.mult)
            v.settle()
            stt(dt_s, x64, 0.0, p_, ALU.max, ALU.add)
            v.settle()
            v.reaches(T.scalar_tensor_tensor(out=h64(adt), in0=h64(dt_s), scalar=-1.0,
                                            in1=bc(negA, 1, [P, TT, 32]), op0=ALU.mult, op1=ALU.mult),
                     S("adt_ready"), l + 1)
            wait_filled(dve, L + "acs", 0)
            v.done(T.tensor_copy(acs_s, bank(L + "acs", 0)[:, 0:64]))
            v.settle()
            ts(nacs_s, acs_s, -1.0, None, ALU.mult)
            readv(L + "acs", 0, T.tensor_tensor(last_s, bank(L + "acs", 0)[:, 64:96], acs_s[:, 0:32], ALU.subtract))
            v.settle()
            dve.sem_inc(S("acs_ready"), 1)
            h32 = lambda ap: ap.rearrange("p (h e) -> p h e", e=SSD_P)
            for t in range(TT):
                for q_ in range(4):
                    wait_read(dve, L + "X", 4 * t + q_)
                if t == 0:
                    wait_filled(dve, L + "o", 3)
                tt(h32(Xdt[:, t, :]), h32(X[:, t, :]), bc(dt_s[:, 32 * t:32 * t + 32], 2, [P, 32, SSD_P]), ALU.mult)
                v.settle()
                if t == 0:
                    dve.wait_ge(S("acs_exp"), l + 1)
                    v.reaches(T.tensor_tensor(h32(Xdec), h32(Xdt[:, 0, :]), bc(dstate, 2, [P, 32, SSD_P]), ALU.mult),
                             S("xdec_ready"), l + 1)
            for t in range(TT):
                tt(h32(X[:, t, :]), h32(X[:, t, :]), bc(dskip[:, 32 * l:32 * l + 32], 2, [P, 32, SSD_P]), ALU.mult)
            v.settle()

            def ssd_y(i):
                g, c = i // TT, i % TT
                xv = X[:, c, 512 * g:512 * g + 512]
                wait_filled(dve, L + "y", i)
                readv(L + "y", i, T.tensor_tensor(xv, xv, bank(L + "y", i), ALU.add))
                if c:
                    wait_filled(dve, L + "yo", i)
                    tmp = dve_junk[:, 0:512]
                    readv(L + "yo", i, T.tensor_tensor(
                        h32(tmp), h32(bank(L + "yo", i)),
                        bc(eacs[:, 32 * c + 8 * g:32 * c + 8 * g + 8], 2, [P, 8, SSD_P]), ALU.mult))
                    v.settle()
                    tt(xv, xv, tmp, ALU.add)
                v.settle()

            for i in range(SSD_G * TT):
                g, c = i // TT, i % TT
                for half in range(2):
                    wait_read(dve, L + "seg", 2 * i + half)
                if i == 0:
                    wait_read(dve, L + "cb", 0)
                    wait_read(dve, L + "cb", 1)
                lm = Lm[:, i % 2, :].rearrange("p (h q) -> p h q", q=P)
                v.reaches(T.tensor_tensor(lm, lm, bc(cb[:, 4 * c + g, :], 1, [P, HPG, P]), ALU.mult),
                         S("decay_ready"), 8 * l + i + 1)
                if i:
                    ssd_y(i - 1)
            ssd_y(SSD_G * TT - 1)
            for n in range(8):
                wait_read(dve, L + "z", n)
            for t in range(TT):
                ins = T.tensor_tensor(X[:, t, :], X[:, t, :], zs[:, t, :], ALU.mult)
                if t == 0:
                    v.done(ins)
                else:
                    v.reaches(ins, S("yz_ready"), l + 1)
            dve.wait_ge(S("gstd_ready"), l + 1)
            v.done(T.reciprocal(ginv, gstd))
            v.settle()
            for t in range(TT):
                xg = X[:, t, :].rearrange("p (g e) -> p g e", e=512)
                ins = T.tensor_tensor(xg, xg, bc(ginv[:, 4 * t:4 * t + 4], 2, [P, 4, 512]), ALU.mult)
                if t == 0:
                    v.done(ins)
                else:
                    v.reaches(ins, S("y_ready"), l + 1)
            scaled_columns(L + "yT", 16, yT, f"snw{l}")
            for n in range(8):
                wait_read(dve, L + "gate", n)
            for n in range(8):
                name, src, m_ = ("pa", 0, n) if n < 4 else ("ps", 1, n - 4)
                c, t = m_ // 2, m_ % 2
                sg = sig2[:, t, D * src + 512 * c:D * src + 512 * c + 512]
                mg = merged2[:, t, 512 * c:512 * c + 512]
                wait_filled(dve, L + name, m_)
                if src == 0:
                    readv(L + name, m_, T.tensor_tensor(mg, bank(L + name, m_), sg, ALU.mult))
                else:
                    readv(L + name, m_, T.tensor_tensor(sg, bank(L + name, m_), sg, ALU.mult))
                    v.settle()
                    ins = T.tensor_tensor(mg, mg, sg, ALU.add)
                    if n == 7:
                        v.reaches(ins, S("merged"), 2 + l)
                    else:
                        v.done(ins)
            for k in range(0, KD, 2):
                wait_filled(dve, L + "mT", k)
                readv(L + "mT", k, T.tensor_copy(hT[:, k, :], bank(L + "mT", k)[:, 0:SEQ]))

            def residual(name, n, width, value):
                for i in range(n):
                    c, t = i // 2, i % 2
                    wait_filled(dve, name, i)
                    xv = x[:, t, width * c:width * c + width]
                    readv(name, i, T.tensor_tensor(xv, xv, bank(name, i)[:, 0:width], ALU.add))
                v.settle()
                dve.sem_inc(S("x_updated"), 1)

            residual(L + "wo", 4, 512, 3 + 2 * l)
            norm_scale(3 + 2 * l, [x[:, 0, :], x[:, 1, :]], [xs[:, 0, :], xs[:, 1, :]])
            scaled_columns(L + "fT", KD, hT, f"ffnw{l}")
            for c in range(FT // 2):
                for m_ in range(4):
                    col = 2 * c + m_ if m_ < 2 else FT + 2 * c + m_ - 2
                    o = conv_o[:, c % 2 * 4 + m_, :]
                    conv_in(L + "up", 4 * c + m_, o, f"fcw{l}", f"fcb{l}", 3, 2 * FT, col)
                    if m_ < 2:
                        dve.sem_inc(S("gate_conv"), 1)
                for m_ in range(2):
                    i = 2 * c + m_
                    dve.wait_ge(S("gate_silu"), FT * l + i + 1)
                    v.reaches(T.tensor_tensor(gT[:, i, :], conv_o[:, c % 2 * 4 + m_, :],
                                             conv_o[:, c % 2 * 4 + 2 + m_, :], ALU.mult),
                             S("glu_ready"), FT * l + i + 1)
            residual(L + "dn", 8, 256, 4 + 2 * l)
        dve.wait_ge(S("std_ready"), 7)
        v.done(T.reciprocal(rinv[:, 0:2], std[:, 0:2]))
        dve.wait_ge(S("final_w_in"), 16)
        v.settle()
        for t in range(TT):
            v.reaches(T.scalar_tensor_tensor(out=x[:, t, :], in0=x[:, t, :], scalar=rinv[:, t:t + 1], in1=final_w,
                                            op0=ALU.mult, op1=ALU.mult), S("out_ready"), t + 1)

    @block.gpsimd
    def _(pool):
        pool.dma_start(xc, d["ctx"].rearrange("p (a b) -> p a b", b=D)).then_inc(S("ctx_in"), 16)
        for g_, at in enumerate((2 * D, 5 * D)):
            pool.dma_start(bias_g[:, g_, :], row_b("b_ada_row", at, D)).then_inc(S("bias_g_in"), 16)
        wait_filled(pool, "nyq", 1)
        pool.dma_start(bias_qkv, row_b("b_in_row", 3 * D_HY, 1536)).then_inc(S("bias_qkv_in"), 16)
        wait_filled(pool, "conv", 7)
        pool.wait_ge(S("yh_ready"), HY_T)
        pool.dma_start(qk_g, row_b("qk_g", 0, 2 * HD)).then_inc(S("qk_g_in"), 16)
        pool.dma_start(namask, d["na_mask"]).then_inc(S("na_mask_in"), 16)
        for h in range(NA_HEADS):
            if h >= 2:
                wait_filled(pool, "nas", 2 * (h - 2) + 1)
            pool.dma_start(nabias[:, h % 2, :], d["rpb"][h]).then_inc(S(f"rpb_in{h % 2}"), 16)
        wait_filled(pool, "nacT", 3)
        pool.dma_start(bias_gate, row_b("b_in_row", 3 * D_HY + 1536, 2048)).then_inc(S("bias_gate_in"), 16)
        wait_filled(pool, "mT", KD - 1)
        pool.wait_ge(S("merged"), 1)
        wait_filled(pool, "gate", 7)
        pool.dma_start(keysT, d["keysT"].rearrange("p (a b) -> p a b", b=P)).then_inc(S("keys_in"), 16)

        def gather(dst, table, g, j, sem):
            pool.indirect_dma_start(out=dst, out_offset=None, in_=d[table],
                                    in_offset=bass.IndirectOffsetOnAxis(
                                        ap=pidx_now[:, TOPK * (g % 2) + j:TOPK * (g % 2) + j + 1], axis=0)
                                    ).then_inc(S(sem), 16)

        for g in range(TT * PEER_HEADS):
            pool.wait_ge(S("picks_ready"), g + 1)
            for j in range(TOPK + U_RING):
                if j < TOPK:
                    n = TOPK * g + j
                    if n >= U_RING:
                        pool.wait_ge(S("u_used"), n - U_RING + 1)
                    gather(u_rows[:, j % U_RING, :], "peer_u", g, j, f"u_in{j % U_RING}")
                if j >= U_RING:
                    m_ = j - U_RING
                    if g:
                        pool.wait_ge(S("v_used"), TOPK * (g - 1) + m_ + 1)
                    gather(v_rows[:, m_, :], "peer_v", g, m_, f"v_in{m_}")

        wait_filled(pool, "acc", 3)
        pool.wait_ge(S("x_updated"), 2)
        for name, dst in (("dt_bias", dtb), ("a_log", alog), ("ssd_d", dskip)):
            pool.dma_start(dst, row_b(name, 0, 64)).then_inc(S("rows_in"), 16)
        wait_filled(pool, f"L{LAYERS - 1}.mT", KD - 1)
        pool.dma_start(final_w, row_b("final_w", 0, D)).then_inc(S("final_w_in"), 16)
    ctx.close()


def kernel(**inputs):
    import concourse.bacc as bacc
    from concourse.bass_utils import run_bass_kernel_spmd

    arrays, where = lay_out(inputs)
    nc = bacc.Bacc("TRN2", target_bir_lowering=False, num_devices=1)
    d = {n: nc.dram_tensor(f"in_{n}", a.shape, mybir.dt.from_np(a.dtype), kind="ExternalInput").ap()
         for n, a in arrays.items()}
    out = nc.dram_tensor("out_rows", (P, TT, D), F32, kind="ExternalOutput").ap()
    build(nc, d, where, out)
    r = run_bass_kernel_spmd(nc, [{f"in_{n}": a for n, a in arrays.items()}], core_ids=[0])
    return r.results[0]["out_rows"].transpose(1, 0, 2).reshape(1, SEQ, D)
```

```python
import math
from contextlib import ExitStack

import numpy as np

import concourse.bass as bass
from concourse import mybir
from concourse.alu_op_type import AluOpType as ALU

ACT = mybir.ActivationFunctionType
F32 = mybir.dt.float32
F32R = mybir.dt.float32r
I32 = mybir.dt.int32
U32 = mybir.dt.uint32
AX = mybir.AxisListType.X

P = 128
SEQ, D = 256, 1024
TT = SEQ // P
KD = D // P
EPS = 1e-6
NEG = -1e30
TAKEN = -3e38

D_HY, NA_HEADS, HD = 512, 8, 64
HY_T = D_HY // P
BANDS, FFN_HY = 16, 64
GRID_W, WIN_COLS, WIN_ROWS = 64, 16, 8
PEER_HEADS, N_KEYS, TOPK = 8, 128, 16
LAYERS, H2, HD2, KVH = 2, 8, 128, 2
IDX_HEADS, IDX_DIM = 8, 64
SEL = min(256, SEQ // 4)
SSD_INNER, SSD_H, SSD_P, SSD_G, SSD_N = 2048, 32, 64, 4, 128
HPG = SSD_H // SSD_G
FFN = 2816
FT = FFN // P

CHUNK = 1024
RING = 6
SPLIT_RING = 4
GLU_RING = 8
BANKS = 8
U_RING, V_RING = 8, 8

_S = np.cumsum([0, 1024, 256, 256, 512, 64, 8, 2048, 3072, 32, 1024, 1024])
C2 = dict(zip("q k v qi ki wi z xbc dt ga gs end".split(), [int(v) for v in _S]))


def chunked(w, nk, nn):
    K, N = w.shape
    v = w.reshape(K // P // nk, nk, P, N // nn, nn)
    return np.ascontiguousarray(v.transpose(3, 0, 2, 1, 4)).reshape(-1, P, nk * nn)


def columns(v):
    return v.reshape(-1, P).T


def shape_constants():
    f64 = np.float64
    t = np.arange(SEQ)
    c = {}
    c["ident"] = np.eye(P)
    k, l = np.meshgrid(np.arange(P), np.arange(P), indexing="ij")
    c["upto"] = (k <= l)
    c["ones"] = np.ones((P, P))
    c["after"] = np.where(l >= k, 0.0, NEG)
    c["causal"] = np.concatenate([np.zeros((P, P)), np.where(l <= k, 0.0, NEG)], 1)
    nf = HD // 4
    inv = 10000.0 ** (-np.arange(nf) / nf)
    inv = inv.astype(np.float32)
    pos = [(t // GRID_W), (t % GRID_W)]
    cc, ss = [], []
    for p_ in pos:
        a = (p_[:, None].astype(np.float32) * inv[None, :]).astype(np.float32).astype(f64)
        cc += [np.cos(a), np.cos(a)]
        ss += [-np.sin(a), np.sin(a)]
    rows = lambda m: m.reshape(TT, P, -1).transpose(1, 0, 2)
    c["rope_c"], c["rope_s"] = rows(np.concatenate(cc, 1)), rows(np.concatenate(ss, 1))
    for name, rot in (("a", HD2 // 4), ("i", IDX_DIM // 4)):
        iv = (500000.0 ** (-np.arange(0, rot, 2, dtype=np.float32) / rot)).astype(np.float32)
        a = (t[:, None].astype(np.float32) * iv[None, :]).astype(np.float32).astype(f64)
        c["rope2_c" + name] = rows(np.concatenate([np.cos(a), np.cos(a)], 1))
        c["rope2_s" + name] = rows(np.concatenate([-np.sin(a), np.sin(a)], 1))
    c["count16"] = np.tile(np.arange(TOPK), (P, 1))
    c["epscol"] = np.full((P, 1), EPS)
    return {n: np.ascontiguousarray(v.reshape(P, -1), dtype=np.float32) for n, v in c.items()}


def hyena_constants():
    L = SEQ
    t = np.arange(L)
    f = np.arange(L)
    th = 2 * np.pi * np.outer(t, f) / (2 * L)
    cos, sin = np.cos(th), np.sin(th)
    alt = (-1.0) ** t
    c = {}
    tiles = lambda m: m.reshape(TT, P, -1).transpose(1, 0, 2)
    c["dft_c"], c["dft_s"] = tiles(cos), tiles(sin)
    fi = -sin.copy()
    fi[:, 0] = alt
    c["dft_i"] = tiles(fi)
    w = np.full(L, 2.0)
    w[0] = 1.0
    ir = (w[:, None] * cos.T) / (2 * L)
    ii = -2.0 * sin.T / (2 * L)
    ii[0] = alt / (2 * L)
    c["idft_r"], c["idft_i"] = tiles(ir), tiles(ii)
    c["alt"] = tiles(alt[:, None])
    not0 = np.ones((P, 1))
    not0[0] = 0
    c["not_first"] = not0
    tt = np.linspace(0.0, 1.0, L, dtype=np.float32)[:, None]
    wv = (2.0 * math.pi / L) * np.arange(L, dtype=np.float32)[:, None]
    b = np.linspace(1e-4, BANDS - 1.0, BANDS, dtype=np.float32)[None, :]
    feats = np.concatenate([tt, np.cos(b * wv), -np.sin(b * wv)], -1)
    ft = np.zeros((P, L))
    ft[: feats.shape[1]] = feats.T
    c["feats"] = ft
    dl = np.abs(np.linspace(math.log(1e-2) / 1.5, math.log(1e-2) / 0.3, D_HY, dtype=np.float32))
    c["decay"] = tiles(np.exp(-tt.astype(np.float32) * dl))
    return {n: np.ascontiguousarray(v.reshape(P, -1), dtype=np.float32) for n, v in c.items()}


def pack(parts):
    at, where = 0, {}
    for n, v in parts.items():
        where[n] = (at, v.shape[1])
        at += v.shape[1]
    return np.ascontiguousarray(np.concatenate(list(parts.values()), 1), dtype=np.float32), where


def lay_out(i):
    o = {}
    i = {k: np.asarray(v) for k, v in i.items()}
    rows = lambda m: np.ascontiguousarray(m.reshape(TT, P, -1).transpose(1, 0, 2)).reshape(P, -1)
    o["x"], o["ctx"] = rows(i["x"][0]), rows(i["ctx"][0])
    o["consts"], w_c = pack(shape_constants())
    o["hyc"], w_h = pack(hyena_constants())
    w_in, b_in = i["w_in"][0], i["b_in"][0]
    cols = {
        "c": np.stack([columns(i["c"][0]), columns(i["c_ctx"])], 2).reshape(P, -1),
        "g1n": columns(i["norm1_g"][0]), "g2n": columns(i["norm2_g"][0]),
        "b_ada": columns(i["b_ada"][0]), "b_hy": columns(b_in[: 3 * D_HY]),
        "cw": np.concatenate([columns(i["hy_conv_w"][0][j]) for j in range(3)], 1),
        "cb": columns(i["hy_conv_b"][0]),
        "skip": np.concatenate([columns(i["hy_skip"][0][j]) for j in range(2)], 1),
    }
    small = lambda v: np.pad(v[:, None], ((0, P - v.shape[0]), (0, 0)))
    cols |= {"f1b": small(i["hy_f1_b"][0]), "f2b": small(i["hy_f2_b"][0]), "f3b": small(i["hy_f3_b"][0]),
             "freq": small(i["hy_sin_freq"][0])}
    for l in range(LAYERS):
        cols[f"mixw{l}"] = columns(i["norm_mix_w_2"][l])
        cols[f"ffnw{l}"] = columns(i["norm_ffn_w_2"][l])
        cols[f"scw{l}"] = np.concatenate([columns(i["ssd_conv_w_2"][l][j]) for j in range(4)], 1)
        cols[f"scb{l}"] = columns(i["ssd_conv_b_2"][l])
        cols[f"snw{l}"] = columns(i["ssd_norm_w_2"][l])
        cols[f"fcw{l}"] = np.concatenate([columns(i["ffn_conv_w_2"][l][j]) for j in range(3)], 1)
        cols[f"fcb{l}"] = columns(i["ffn_conv_b_2"][l])
    o["cols"], w_v = pack(cols)
    padk = lambda w: np.pad(w, ((0, P - w.shape[0]), (0, 0)))
    o["hyw"], w_w = pack({"f1": padk(i["hy_f1_w"][0]), "f2": padk(i["hy_f2_w"][0]),
                          "f3": padk(i["hy_f3_w"][0]), "f4": padk(i["hy_f4_w"][0])})
    o["b_ada_row"] = i["b_ada"][0][None]
    o["b_in_row"] = b_in[None]
    o["qk_g"] = np.concatenate([i["q_norm_g"][0], i["k_norm_g"][0]])[None]
    o["dt_bias"] = i["ssd_dt_bias_2"].reshape(1, -1)
    o["a_log"] = i["ssd_a_log_2"].reshape(1, -1)
    o["ssd_d"] = i["ssd_d_2"].reshape(1, -1)
    o["final_w"] = i["norm_final_w_2"][None]
    r, wr = np.arange(SEQ // GRID_W), min(WIN_ROWS, SEQ // GRID_W)
    start = np.clip(r - wr // 2, 0, SEQ // GRID_W - wr)
    assert wr == SEQ // GRID_W and (start == 0).all()
    col = np.arange(GRID_W)
    dr = r[None, :] - r[:, None] + WIN_ROWS - 1
    dc = np.clip(col[None, :] - col[:, None], -(WIN_COLS - 1), WIN_COLS - 1) + WIN_COLS - 1
    bias = i["na_rpb"][0][:, dr[:, None, :, None], dc[None, :, None, :]].reshape(NA_HEADS, TT, P, SEQ)
    o["rpb"] = np.ascontiguousarray(bias.transpose(0, 2, 1, 3)).reshape(NA_HEADS, P, TT * SEQ)
    cs = np.clip(col - WIN_COLS // 2, 0, GRID_W - WIN_COLS)
    ok = (col[None, :] >= cs[:, None]) & (col[None, :] < cs[:, None] + WIN_COLS)
    okf = np.broadcast_to(ok[None, :, None, :], (4, GRID_W, 4, GRID_W)).reshape(TT, P, SEQ)
    o["na_mask"] = np.ascontiguousarray(np.where(okf, 0.0, NEG).astype(np.float32).transpose(1, 0, 2)).reshape(P, -1)
    o["w_ada"] = chunked(i["w_ada"][0], 2, 512)
    o["w_in_hy"] = chunked(w_in[:, :3 * D_HY], 8, P)
    o["w_in"] = chunked(w_in[:, 3 * D_HY:], 2, 512)
    o["w_hy_out"] = chunked(i["w_hy_out"][0], 2, 512)
    o["w_na_out"] = chunked(i["w_na_out"][0], 2, 512)
    o["w_out"] = chunked(i["w_out"][0], 2, 512)
    o["w_pq"] = chunked(i["peer_w_q"][0], 8, P)
    keys = i["peer_keys"][0].reshape(2 * PEER_HEADS, N_KEYS, P)
    o["keysT"] = np.ascontiguousarray(keys.transpose(2, 0, 1)).reshape(P, -1)
    o["peer_u"], o["peer_v"] = i["peer_u"][0], i["peer_v"][0]
    w2 = i["w_in_2"]
    pick = lambda l, *n: np.concatenate([w2[l][:, C2[a]:C2[b]] for a, b in n], 1)
    o["w2_qkv"] = np.stack([chunked(pick(l, ("q", "ki")), 2, 512) for l in range(LAYERS)])
    o["w2_small"] = np.stack([chunked(pick(l, ("ki", "z"), ("dt", "ga")), 8, 104) for l in range(LAYERS)])
    o["w2_z"] = np.stack([chunked(pick(l, ("z", "xbc")), 2, 512) for l in range(LAYERS)])
    o["w2_xbc"] = np.stack([chunked(pick(l, ("xbc", "dt")), 8, P) for l in range(LAYERS)])
    o["w2_g"] = np.stack([chunked(pick(l, ("ga", "end")), 2, 512) for l in range(LAYERS)])
    o["w2_pa"] = np.stack([chunked(i["w_proj_attn_2"][l], 2, 512) for l in range(LAYERS)])
    o["w2_ps"] = np.stack([chunked(i["w_proj_ssd_2"][l], 2, 512) for l in range(LAYERS)])
    o["w2_o"] = np.stack([chunked(i["w_out_2"][l], 2, 512) for l in range(LAYERS)])
    up = i["ffn_w_up_2"].reshape(LAYERS, D, 2, FT // 2, 2 * P).transpose(0, 1, 3, 2, 4).reshape(LAYERS, D, 2 * FFN)
    o["w2_up"] = np.stack([chunked(up[l], 8, P) for l in range(LAYERS)])
    dn = i["ffn_w_down_2"]
    o["w2_dn"] = np.stack([chunked(dn[l], 1, D) for l in range(LAYERS)])
    return {k: np.ascontiguousarray(v) for k, v in o.items()}, {"consts": w_c, "hyc": w_h, "cols": w_v, "hyw": w_w}


def psum_banks(order):
    bank, before, held, r = {}, {}, [0] * BANKS, 0
    for name, i in order:
        if name.endswith(".dn"):
            b = 4 + i
        elif name.endswith(".up"):
            b = i % 4
        else:
            b, r = r, (r + 1) % BANKS
        bank[(name, i)], before[(name, i)] = b, held[b]
        held[b] += 1
    return bank, before


def psum_order():
    g = []
    add = lambda name, n=1: g.extend((name, i) for i in range(n))
    def ada(ch):
        g.append(("ada", ch))
        if ch >= 1 and ch - 1 in ADA_COLS:
            g.append(("adaT", ADA_COLS.index(ch - 1)))

    for i in range(3):
        ada(i), g.append(("mlp", i))
    ada(3), add("filter", 8), ada(4), add("absum", 2), ada(5)
    for o in range(2):
        g.extend([("dftf", 4 * o + i) for i in range(4)] + [("nyq", o)])
        ada(6 + o)
    for ch in range(8, 12):
        ada(ch)
    add("hT0", KD), add("hcT", KD)
    add("zhy", 12), add("zqkv", 2), add("vrow", 2)
    for o in range(2):
        g.extend([("spec", 4 * o + i) for i in range(4)] + [("zqkv", 2 + 4 * o + i) for i in range(4)])
        g.extend([("conv", 4 * o + i) for i in range(4)])
        if o == 0:
            add("yrow", 2)
    add("naT", 8), add("nacT", 4)
    for h in range(NA_HEADS + 1):
        if h < NA_HEADS:
            g.extend([("nas", 2 * h), ("nas", 2 * h + 1)])
        if h >= 1:
            if h % 2 == 0:
                g.extend([("gate", h - 2), ("gate", h - 1)])
            g.extend([("nap", 2 * h - 2), ("nap", 2 * h - 1), ("nao", h - 1)])
    add("mix", 8), add("mT", KD), add("wout", 4)
    add("hfT", KD), add("hfrow", 4), add("pq", 16), add("ps", 8)
    add("acc", 4)
    for l in range(LAYERS):
        L = f"L{l}."
        add(L + "hT", KD), add(L + "qkv", 8), add(L + "small", 2), add(L + "xbc", 24)
        add(L + "qT", 10), add(L + "qiT", 5), add(L + "is", 6)
        g.extend([(L + "z", n) for n in range(4)])
        for t in range(TT):
            banks = range(2 * t, 4 * t + 2)
            g.extend([(L + "s", b) for b in banks] + [(L + "z", 4 + 2 * t), (L + "z", 5 + 2 * t)])
            if t == 0:
                g.append((L + "acs", 0))
            g.extend([(L + "p", b) for b in banks])
            g.extend([(L + "o", 2 * t), (L + "o", 2 * t + 1)])
        add(L + "X", 8), add(L + "Brow", 1), add(L + "cb", 2)
        add(L + "st", 4)
        for i in range(SSD_G * TT):
            g.extend([(L + "seg", 2 * i), (L + "seg", 2 * i + 1)])
            if i >= 1:
                g.extend([(L + "y", i - 1)] + ([(L + "yo", i - 1)] if (i - 1) % TT else []))
            if i % TT:
                g.extend([(L + "gate", i - 1), (L + "gate", i)])
        i = SSD_G * TT
        g.extend([(L + "y", i - 1), (L + "yo", i - 1)])
        add(L + "pa", 4), add(L + "yT", 16), add(L + "ps", 4)
        add(L + "mT", KD), add(L + "wo", 4)
        add(L + "fT", KD), add(L + "up", 2 * FT), add(L + "dn", 4)
    return g


ADA_COLS = [0, 1, 2, 3, 6, 7, 8, 9]


def weight_order(turn):
    w = []

    def rows(name, out, n, groups, k_parts=4, l=None, first=0, split=True, width=CHUNK):
        for j in range(n):
            a, b = groups(j)
            for k in range(k_parts):
                ends = k == k_parts - 1
                w.append((name, l, first + j * k_parts + k, width, turn[(out, b)] + 1 if ends else turn[(out, a)],
                          ends, split))

    def features(name, out, n, l=None):
        w.extend((name, l, j, CHUNK, turn[(out, j)] + 1, True, True) for j in range(n))

    two = lambda j: (2 * j, 2 * j + 1)
    rows("w_ada", "ada", 12, lambda j: (j, j), split=False)
    features("w_in_hy", "zhy", 12)
    rows("w_in", "zqkv", 3, lambda j: ((0, 1), (2, 5), (6, 9))[j])
    for h in range(1, NA_HEADS + 1):
        for k in range(2):
            kp, c = 2 * ((h - 1) % 2) + k, (h - 1) // 2
            done = turn[("nap", 2 * h - 2)] if kp < 2 else turn[("gate", 2 * c)] if kp == 2 else turn[("gate", 2 * c + 1)] + 1
            w.append(("w_in", None, 12 + 4 * c + kp, CHUNK, done, kp == 3, True))
    rows("w_hy_out", "mix", 2, two, 2)
    rows("w_na_out", "mix", 2, lambda j: (4 + 2 * j, 5 + 2 * j), 2)
    rows("w_out", "wout", 2, two)
    features("w_pq", "pq", 16)
    for l in range(LAYERS):
        L = f"L{l}."
        rows("w2_qkv", L + "qkv", 4, two, l=l)
        rows("w2_small", L + "small", 1, two, 1, l=l, width=8 * 104)
        features("w2_xbc", L + "xbc", 24, l)
        rows("w2_z", L + "z", 4, two, l=l)
        rows("w2_g", L + "gate", 4, two, l=l)
        rows("w2_pa", L + "pa", 2, two, l=l)
        rows("w2_ps", L + "ps", 2, two, 8, l=l)
        rows("w2_o", L + "wo", 2, two, l=l)
        for c in range(FT // 2 + 1):
            if c < FT // 2:
                w.extend(("w2_up", l, 4 * c + m, CHUNK, turn[(L + "up", 4 * c + m)] + 1, True, True) for m in range(4))
            for k in range(2 * c - 2, 2 * c):
                if k >= 0:
                    last = k == FT - 1
                    done = ("dn", 3) if last else ("dn", 0) if c == FT // 2 else ("up", 4 * c + 3)
                    w.append(("w2_dn", l, k, CHUNK, turn[(L + done[0], done[1])] + (done != ("dn", 0)), last, True))
    return w


class Progress:

    def __init__(self, eng, steps):
        self.eng, self.steps, self.n, self.last = eng, steps, 0, None

    def done(self, ins):
        self.n += 1
        ins.then_inc(self.steps, 1)
        self.last = (self.steps, self.n)

    def reaches(self, ins, sem, value):
        ins.then_inc(sem, 1)
        self.last = (sem, value)

    def settle(self):
        self.eng.wait_ge(*self.last)


def build(nc, d, where, out):
    ctx = ExitStack()
    sb = lambda n, cols, rows=P, dt=F32: ctx.enter_context(nc.sbuf_tensor(n, [rows, cols], dt))
    order = psum_order()
    turn = {g: n for n, g in enumerate(order)}
    assert len(turn) == len(order)
    bank_of, before_of = psum_banks(order)
    wplan = weight_order(turn)
    split_chunks = [c for c, w in enumerate(wplan) if w[6]]
    split_turn = {c: n for n, c in enumerate(split_chunks)}
    inner_turn = {c: n for n, c in enumerate(c for c, w in enumerate(wplan) if not w[5])}
    SPLIT_OUT = ("nao", "mT") + tuple(f"L{l}.{n}" for l in range(LAYERS) for n in ("hT", "o", "yT", "mT", "fT"))
    hi_turn = {g: n for n, g in enumerate(g for g in order if g[0] in SPLIT_OUT)}

    wring = ctx.enter_context(nc.sbuf_tensor("wring", [P, RING, CHUNK], F32))
    w_hi = ctx.enter_context(nc.sbuf_tensor("w_hi", [P, SPLIT_RING, CHUNK], F32R))
    w_lo = ctx.enter_context(nc.sbuf_tensor("w_lo", [P, SPLIT_RING, CHUNK], F32R))
    x = ctx.enter_context(nc.sbuf_tensor("x_rows", [P, TT, D], F32))
    a_hi = ctx.enter_context(nc.sbuf_tensor("a_hi", [P, 2 * KD, SEQ], F32R))
    a_lo = ctx.enter_context(nc.sbuf_tensor("a_lo", [P, 2 * KD, SEQ], F32R))
    n_c = sum(n for _, n in where["consts"].values())
    n_v = sum(n for _, n in where["cols"].values())
    consts, cols = sb("consts", n_c), sb("cols", n_v)
    dve_junk = sb("dve_junk", D)
    small = sb("small_values", 1024)
    ARENA = 24520
    arena = sb("arena", ARENA)
    psum = ctx.enter_context(nc.psum_tensor("psum", [P, BANKS, 512], F32))

    def K(name):
        a, n = where["consts"][name]
        return consts[:, a:a + n]

    def V(name, j=0, n=1):
        a, _ = where["cols"][name]
        return cols[:, a + j:a + j + n]

    def area(at, *shape):
        n = int(np.prod(shape))
        assert at + n <= ARENA, (at, n)
        ap = arena[:, at:at + n]
        if len(shape) == 2:
            ap = ap.rearrange("p (a b) -> p a b", b=shape[1])
        if len(shape) == 3:
            ap = ap.rearrange("p (a b c) -> p a b c", b=shape[1], c=shape[2])
        return ap

    def sm(at, n):
        return small[:, at:at + n]

    ident, upto, ones, zeros = K("ident"), K("upto"), K("ones"), K("causal")[:, 0:P]

    ss, std, rinv = sm(0, 4), sm(4, 4), sm(8, 4)
    cT = sm(12, 16).rearrange("p (k v) -> p k v", v=2)
    adaT = sm(28, 64).rearrange("p (k v) -> p k v", v=2)
    mod_a = sm(92, 24).rearrange("p (s k) -> p s k", k=8)
    one_row = sm(116, 128)
    nsum, nstd, ninv = sm(244, 48), sm(292, 48), sm(340, 48)
    amax, asum, ainv = sm(388, 16), sm(404, 16), sm(420, 16)
    dt_s = sm(436, 64)
    adt = sm(500, 64)
    acs_s, last_s, nacs_s = sm(564, 64), sm(628, 32), sm(660, 64)
    eacs, dstate = sm(724, 64), sm(788, 32)
    negA = sm(820, 32)
    lnw = sm(852, 4)
    gsum, gstd, ginv = sm(856, 8), sm(864, 8), sm(872, 8)
    wi_s = sm(880, 16)
    best8 = sm(896, 8)
    t64 = sm(904, 64)

    sems = {}

    def S(name):
        if name not in sems:
            sems[name] = ctx.enter_context(nc.semaphore(name))
        return sems[name]

    psum_filled = S("psum_filled")
    bank_read = [S(f"bank_read{b}") for b in range(BANKS)]
    weights_in = [S(f"weights_in{r}") for r in range(RING)]

    second_block = [w[0] for w in wplan].index("w2_qkv")
    weights_used = S("weights_used")
    hi_ready = S("weights_hi_ready")
    lo_ready = S("weights_lo_ready")

    def used(c):
        return (psum_filled, wplan[c][4]) if wplan[c][5] else (weights_used, inner_turn[c] + 1)

    class SplitStream:

        def __init__(self, step):
            self.step, self.n = step, 0

        def before(self, n):
            while self.n < len(split_chunks):
                c = split_chunks[self.n]
                freed = [c - RING]
                if self.n >= SPLIT_RING:
                    freed.append(split_chunks[self.n - SPLIT_RING])
                if max(wplan[f][4] for f in freed) > n or (c >= second_block and n <= turn[("acc", 3)]):
                    break
                self.step(self.n, c)
                self.n += 1

    streams = {}

    def due(eng, name, i):
        if id(eng) in streams:
            streams[id(eng)].before(turn[(name, i)])

    def bank(name, i):
        return psum[:, bank_of[(name, i)], :]

    def wait_filled(eng, name, i):
        due(eng, name, i)
        eng.wait_ge(psum_filled, turn[(name, i)] + 1)

    def read_value(name, i):
        return bank_read[bank_of[(name, i)]], before_of[(name, i)] + 1

    def wait_read(eng, name, i):
        due(eng, name, i)
        eng.wait_ge(*read_value(name, i))

    hyc_n = sum(n for _, n in where["hyc"].values())
    hyw_n = sum(n for _, n in where["hyw"].values())
    A_K = hyc_n
    A_G = A_K + 5120
    A_R = A_G + 2048
    hyc = arena[:, 0:hyc_n]

    def HC(name):
        a, n = where["hyc"][name]
        return hyc[:, a:a + n]

    def HC3(name, n):
        return HC(name).rearrange("p (k n) -> p k n", n=n)

    def HW(name):
        a, n = where["hyw"][name]
        return arena[:, A_R + a:A_R + a + n]

    Kr = area(A_K, 2, 2, 512)
    Ki = area(A_K + 2048, 2, 2, 512)
    Kr0 = area(A_K + 4096, 2, 512)
    G = area(A_G, 2, D)
    A_F = A_R + hyw_n
    filt = area(A_F, 2, 4, 512)
    A_FT = A_F + 4096
    mlp_h = area(A_FT, SEQ)
    mlp_k = area(A_FT + 256, SEQ)
    mlp_u = area(A_FT + 512, SEQ)
    rnorm = area(A_FT + 1024, 2, 512)
    fabs = area(A_FT + 2048, 2, 2, 512)
    xs = area(A_FT + 2048, TT, D)
    A_CTX = A_FT + 4096
    xc = area(A_CTX, TT, D)
    modT = [area(A_F, KD, SEQ), area(A_F + 2048, KD, SEQ), area(6144, KD, SEQ)]
    ada_row = area(A_CTX + 2048, 2, 512)[0:2]
    zcT = area(A_R, 12, SEQ)
    qkv = area(A_R + 3072, TT, 1536)
    kvc = area(A_R + 6144, TT, D)
    bias_qkv = area(A_R + 8192, 1536)
    A_M = A_R + 9728
    zpre = area(A_M, 4, SEQ)
    vrow = area(A_M + 1024, TT, 512)
    prod_r = area(A_M, 2, 512)
    prod_i = area(A_M + 2048, 2, 512)
    tmp_a = dve_junk[:, 0:512]
    y1T = zcT[:, HY_T:2 * HY_T, :]
    HY_AT, NA_AT = KD, KD + HY_T
    naq = area(0, TT, D)
    nat = area(2048, TT, D)
    nakc = area(4096, TT, 512)
    naqT = area(5120, 8, SEQ)
    nakcT = area(7168, 4, SEQ)
    assert 8192 <= A_G
    nabias = area(A_M, 2, TT * SEQ)
    namask = area(A_M + 1024, TT * SEQ)
    nap = [area(A_M + 1536, 2, 512), area(0, 2, 512)]
    napT = area(A_M + 2560, 4, SEQ)
    qk_g = area(A_R + 8192 + 1024, 2 * HD)
    bias_gate = [qkv[:, 1, 0:D], area(A_R + 8192, D)]

    def sig(n):
        return area(A_R + 512 * n, 512) if n < 6 else qkv[:, 0, 512 * (n - 6):512 * (n - 5)]

    merged = area(6144, TT, D)
    assert 6144 + 2048 <= A_G
    keysT = area(0, 16, P)
    pqT = area(2048, 16, SEQ)
    A_S = A_G + 2048
    scr = area(A_S, TT * 16, P)
    scw = area(A_S + 4096, 2, P)
    cand = area(A_S + 4352, 1, 256)
    candw = area(A_S + 4608, 1, 256)
    oh = area(A_S + 4864, 16, 16)
    tops = area(A_S + 5120, 2, 16)
    topi_u = area(A_S + 5152, 32).bitcast(U32).rearrange("p (a b) -> p a b", b=16)
    topi = area(A_S + 5184, 2, 16)
    bests = area(A_S + 5216, 2, 16)
    bpos_u = area(A_S + 5248, 16).bitcast(U32).unsqueeze(1)
    bpos = area(A_S + 5264, 2, 16)
    b_sh = area(A_S + 5296, 32).bitcast(U32).rearrange("p (a b) -> p a b", b=16)
    i_two = area(A_S + 5328, 2, 16)
    pidx = area(A_S + 5360, TT * 128).bitcast(I32).rearrange("p (a b) -> p a b", b=16)
    pexp = area(A_S + 5616, TT * 8, 16)
    psum_e = area(A_S + 5872, TT * 8)
    pinv = area(A_S + 5888, 1)
    pdot = area(A_S + 5904, 16)
    pact = area(A_S + 5920, 16)
    pw = area(A_S + 5936, 16)
    u_rows = area(0, U_RING, D)
    assert U_RING * D <= A_G
    V_ON = RING * CHUNK // D
    v_ring_rows = wring[:].rearrange("p a b -> p (a b)")

    def v_row(j):
        return v_ring_rows[:, j * D:(j + 1) * D] if j < V_ON else area(A_S + 6144 + (j - V_ON) * D, D)

    assert CHUNK == D and V_ON <= V_RING
    assert A_S + 6144 + (V_RING - V_ON) * D <= A_FT + 2048
    diag = area(A_CTX + 16, TOPK, P)

    qkv2 = area(0, TT, 2048)
    small2 = area(4096, TT, 104)
    qkT = area(4352, 10, SEQ)
    qiT = area(6912, 5, SEQ)
    isc, iscw = area(8192, TT, SEQ), area(8704, TT, SEQ)
    kid = area(9216, TT, P)
    madd = area(9216, TT, SEQ)
    rel = area(9728, 8, SEQ)
    pr = area(9728, 8, SEQ)
    prT = area(11776, TT, D)
    AT_AT = KD
    X = area(0, TT, SSD_INNER)
    Xdt = area(4352, TT, SSD_INNER)
    Brow = area(8448, 512)
    Xdec = area(8960, SSD_INNER)
    Lm = area(8960, 2, D)
    cb = area(11008, 8, P)
    st = area(12032, 4, 512)
    zs = area(14080, TT, SSD_INNER)
    xbcT = area(18176, 24, SEQ)
    sig2 = area(18176, TT, 2048)
    merged2 = area(8448, TT, D)
    GLU_AT = KD
    conv_o = area(5632, 8, SEQ)
    final_w = area(12032, D)
    amax2, asum2, ainv2 = sm(12, 8), sm(20, 8), sm(28, 8)
    x64, u64, v64 = sm(40, 64), sm(104, 64), sm(168, 64)
    dtb, alog, dskip = sm(244, 64), sm(308, 64), sm(372, 64)
    SCALE2 = HD2 ** -0.5

    def index_heads(b_):
        if b_ < 2:
            return 0, P, list(range(b_, IDX_HEADS, 2))
        first = 4 * ((b_ - 2) // 2) + b_ % 2
        return 1, SEQ, [first, first + 2]

    MAGIC = 1.5 * 2.0 ** 23
    C1, C2_, C3 = 6.28125, 0.0019350051879882812, 3.0199159819e-07
    BIG = lambda l: f"L{l}."
    U_TURNS, V_TURNS = TOPK // U_RING, TOPK // V_RING

    def row_b(name, a, n):
        return d[name][0:1, a:a + n].to_broadcast([P, n])

    block = ctx.enter_context(nc.Block())

    def finish(sp):
        sp.wait_ge(S("out_ready"), 2)
        sp.dma_start(out, x[:]).then_inc(S("out_stored"), 16)
        sp.wait_ge(S("out_stored"), 16)

    @block.sync
    def _(sp):
        sp.dma_start(consts[:], d["consts"]).then_inc(S("consts_in"), 16)
        sp.dma_start(x[:], d["x"].rearrange("p (a b) -> p a b", b=D)).then_inc(S("x_in"), 16)
        for c, (name, l, i, n, *_) in enumerate(wplan):
            if second_block <= c < second_block + RING:
                sp.wait_ge(S("v_used"), TOPK * (TT * PEER_HEADS - 1) + TOPK - V_RING + c % RING + 1)
            if c >= RING:
                if c - RING in split_turn:
                    sp.wait_ge(lo_ready, split_turn[c - RING] + 1)
                else:
                    sp.wait_ge(*used(c - RING))
            src = d[name][i] if l is None else d[name][l, i]
            sp.dma_start(wring[:, c % RING, 0:n], src).then_inc(weights_in[c % RING], 16)
        finish(sp)

    @block.tensor
    def _(pe):
        state = {"turn": 0, "chunk": 0}

        def open_(name, i, early=False):
            if not early:
                assert turn[(name, i)] == state["turn"], (name, i, order[state["turn"]])
                state["turn"] += 1
            if before_of[(name, i)]:
                pe.wait_ge(bank_read[bank_of[(name, i)]], before_of[(name, i)])
            return bank(name, i)

        def close(ins):
            ins.then_inc(psum_filled, 1)

        def take(name, l=None):
            c = state["chunk"]
            assert wplan[c][:2] == (name, l), (wplan[c], name, l)
            state["chunk"] += 1
            if c not in split_turn:
                pe.wait_ge(weights_in[c % RING], 16 * (c // RING + 1))
                return wring[:, c % RING, :]
            n, width = split_turn[c], wplan[c][3]
            pe.wait_ge(lo_ready, n + 1)
            return w_hi[:, n % SPLIT_RING, 0:width], w_lo[:, n % SPLIT_RING, 0:width]

        def chunk_used(ins):
            assert not wplan[state["chunk"] - 1][5]
            ins.then_inc(weights_used, 1)

        mm = lambda o, a, b, start, stop: nc.tensor.matmul(o, a, b, start=start, stop=stop, skip_group_check=True)

        def product(o, w_part, a_part, k0, nk, lhs_is_a, start, stop):
            for k in range(nk):
                pairs = ((w_hi, a_hi), (w_lo, a_hi), (w_hi, a_lo))
                if not lhs_is_a:
                    pairs = ((w_hi, a_hi), (w_hi, a_lo), (w_lo, a_hi))
                for p_, (wt, at_) in enumerate(pairs):
                    w_, a_ = w_part(wt, k), a_part(at_, k0 + k)
                    m = mm(o, a_ if lhs_is_a else w_, w_ if lhs_is_a else a_, start and k == 0 and p_ == 0,
                           stop and k == nk - 1 and p_ == 2)
            return m

        def rows_mm(o, a0, nk, t, w, n, start=True, stop=True, at=0):
            W = w[0].shape[-1] // nk
            part = lambda wt, k: w[wt is w_lo][:, k * W + at:k * W + at + n]
            return product(o, part, lambda at_, k: at_[:, k, t * P:(t + 1) * P], a0, nk, True, start, stop)

        def columns_of_rows(name, l, outs, srcs, k_parts=4, nk=2, before=None):
            o = [open_(*g) for g in outs]
            for kp in range(k_parts):
                if before and kp == k_parts // 2:
                    before()
                w = take(name, l)
                for n, g in enumerate(outs):
                    m = rows_mm(o[n], srcs[n] + nk * kp, nk, g[1] % 2, w, 512, kp == 0, kp == k_parts - 1)
                    if kp == k_parts - 1:
                        close(m)
                if kp < k_parts - 1:
                    chunk_used(m)

        def feature_mm(name, l, out_, i):
            w = take(name, l)
            o = open_(out_, i)
            part = lambda wt, k: w[wt is w_lo][:, k * P:(k + 1) * P]
            close(product(o[:, 0:SEQ], part, lambda at_, k: at_[:, k, :], 0, KD, False, True, True))

        def transposes(name, i, srcs):
            o = open_(name, i)
            for j, s in enumerate(srcs):
                n = s.shape[0]
                m = nc.tensor.transpose(o[0:s.shape[-1], j * n:(j + 1) * n], s, ident[0:n, 0:n])
            close(m)

        tile = lambda t: slice(t * P, (t + 1) * P)

        def ada_columns(ci):
            wait_read(pe, "ada", ADA_COLS[ci])
            o = open_("adaT", ci)
            for j in range(4):
                m = nc.tensor.transpose(o[:, 2 * j:2 * j + 2], ada_row[0:2, ci % 2, j * P:(j + 1) * P],
                                        ident[0:2, 0:2])
            close(m)

        def ada(ch):
            o = open_("ada", ch)
            for kk in range(KD):
                if kk % 2 == 0:
                    w = take("w_ada")
                wk = w[:, kk % 2 * 512:kk % 2 * 512 + 512]
                if ch in ADA_COLS:
                    m = mm(o[0:2, :], cT[:, kk, :], wk, kk == 0, kk == KD - 1)
                else:
                    m = mm(o, cT[:, kk, 0:1].to_broadcast([P, P]), wk, kk == 0, kk == KD - 1)
                if kk % 2 and kk < KD - 1:
                    chunk_used(m)
            close(m)
            if ch >= 1 and ch - 1 in ADA_COLS:
                ada_columns(ADA_COLS.index(ch - 1))

        pe.wait_ge(S("consts_in"), 16)
        pe.wait_ge(S("c_ready"), 1)
        for i in range(3):
            ada(i)
            if i == 0:
                pe.wait_ge(S("hyc_in"), 16)
                pe.wait_ge(S("hyw_in"), 16)
            o = open_("mlp", i)
            if i:
                pe.wait_ge(S("mlp_h"), i)
            rhs = HC("feats")[0:64, :] if i == 0 else mlp_h[0:64, :]
            close(mm(o[0:64, 0:SEQ], HW(f"f{i + 1}")[0:64, :], rhs, True, True))
        ada(3)
        pe.wait_ge(S("mlp_h"), 3)
        for t in range(TT):
            for j in range(4):
                o = open_("filter", 4 * t + j)
                close(mm(o, mlp_h[0:64, tile(t)], HW("f4")[0:64, j * 512:(j + 1) * 512], True, True))
        ada(4)
        for o_ in range(2):
            o = open_("absum", o_)
            pe.wait_ge(S("fabs_ready"), 2 * o_ + 2)
            for t in range(TT):
                for j in range(2):
                    m = mm(o, ones, fabs[:, t, j, :], t + j == 0, t + j == 2)
            close(m)
        ada(5)
        for o_ in range(2):
            pe.wait_ge(S("filters_ready"), o_ + 1)
            for i in range(4):
                o = open_("dftf", 4 * o_ + i)
                f, kind = i % 2, i // 2
                for t in range(TT):
                    m = mm(o, HC3("dft_s" if kind else "dft_c", SEQ)[:, t, tile(f)],
                           filt[:, t, 2 * o_ + kind, :], t == 0, t == TT - 1)
                close(m)
            o = open_("nyq", o_)
            for t in range(TT):
                m = mm(o[0:1, :], HC("alt")[:, t:t + 1], filt[:, t, 2 * o_, :], t == 0, t == TT - 1)
            close(m)
            ada(6 + o_)
        for ch in range(8, 12):
            ada(ch)

        pe.wait_ge(S("scaled"), 1)
        for k in range(KD):
            transposes("hT0", k, [xs[:, t, tile(k)] for t in range(TT)])
        for k in range(KD):
            transposes("hcT", k, [xc[:, t, tile(k)] for t in range(TT)])
        pe.wait_ge(S("modulated_lo"), KD)
        for m_ in range(12):
            feature_mm("w_in_hy", None, "zhy", m_)
        columns_of_rows("w_in", None, [("zqkv", 0), ("zqkv", 1)], [0, 0])
        pe.wait_ge(S("modulated_lo"), 2 * KD)

        pe.wait_ge(S("conv_done"), 4)
        for t in range(TT):
            transposes("vrow", t, [zcT[:, m_, tile(t)] for m_ in range(HY_T)])
        for o_ in range(2):
            for t in range(TT):
                wait_read(pe, "vrow" if o_ == 0 else "yrow", t)
            for i in range(4):
                f, kind = i // 2, i % 2
                o = open_("spec", 4 * o_ + i)
                for t in range(TT):
                    m = mm(o, HC3("dft_i" if kind else "dft_c", SEQ)[:, t, tile(f)], vrow[:, t, :],
                           t == 0, t == TT - 1)
                close(m)
            columns_of_rows("w_in", None, [("zqkv", 2 + 4 * o_ + n) for n in range(4)], [0, 0, KD, KD])
            pe.wait_ge(S("product_ready"), 2 * o_ + 2)
            for m_ in range(HY_T):
                o = open_("conv", 4 * o_ + m_)
                for f in range(2):
                    mm(o[:, 0:SEQ], prod_r[:, f, tile(m_)], HC3("idft_r", SEQ)[:, f, :], f == 0, False)
                    m = mm(o[:, 0:SEQ], prod_i[:, f, tile(m_)], HC3("idft_i", SEQ)[:, f, :], False, f == 1)
                close(m)
            if o_ == 0:
                pe.wait_ge(S("y1_ready"), HY_T)
                for t in range(TT):
                    transposes("yrow", t, [y1T[:, m_, tile(t)] for m_ in range(HY_T)])

        pe.wait_ge(S("na_rows"), 1)
        for g in range(8):
            transposes("naT", g, [nat[:, t, tile(g)] for t in range(TT)])
        for g in range(4):
            transposes("nacT", g, [nakc[:, t, tile(g)] for t in range(TT)])
        for g in range(8):
            wait_read(pe, "naT", g)
        for g in range(4):
            wait_read(pe, "nacT", g)

        def na_scores(h):
            p_, s_ = h // 2, slice(64 * (h % 2), 64 * (h % 2) + 64)
            pe.wait_ge(S("bias_ready"), h + 1)
            for t in range(TT):
                o = open_("nas", 2 * h + t)
                q = naqT[s_, p_, tile(t)]
                mm(o[:, 0:SEQ], q, naqT[s_, 4 + p_, :], True, False)
                mm(o[:, 0:SEQ], ident, nabias[:, h % 2, t * SEQ:(t + 1) * SEQ], False, False)
                close(mm(o[:, SEQ:2 * SEQ], q, nakcT[s_, p_, :], False, True))

        def na_out(h):
            for t in range(TT):
                pe.wait_ge(S("na_prob"), 2 * h + t + 1)
                transposes("nap", 2 * h + t, [nap[h % 2][:, t, tile(j)] for j in range(4)])
            for t in range(TT):
                wait_read(pe, "nap", 2 * h + t)
            o = open_("nao", h)
            p_ = h // 2
            for j in range(4):
                v = qkv[:, j, D + p_ * P:D + (p_ + 1) * P] if j < 2 else kvc[:, j - 2, 512 + p_ * P:512 + (p_ + 1) * P]
                m = mm(o[:, 0:SEQ], v, napT[:, j, :], j == 0, j == 3)
            close(m)

        gate_banks = []

        def half_gates(h):
            c, part = (h - 1) // 2, (h - 1) % 2
            if part == 0:
                gate_banks[:] = [open_("gate", 2 * c + t, early=True) for t in range(TT)]
            for kp in (2 * part, 2 * part + 1):
                w = take("w_in")
                for t in range(TT):
                    m = rows_mm(gate_banks[t], 2 * kp, 2, t, w, 512, kp == 0, kp == 3)
                    if kp == 3:
                        close(m)
                if kp < 3:
                    chunk_used(m)
            if part:
                state["turn"] += TT

        for h in range(NA_HEADS + 1):
            if h < NA_HEADS:
                na_scores(h)
            if h >= 1:
                half_gates(h)
                na_out(h - 1)

        pe.wait_ge(S("yh_ready"), HY_T)
        wait_read(pe, "nao", NA_HEADS - 1)
        wait_read(pe, "nao", NA_HEADS - 2)
        for n, (name, at_) in enumerate((("w_hy_out", HY_AT), ("w_na_out", NA_AT))):
            for half in range(2):
                g = 4 * n + 2 * half
                columns_of_rows(name, None, [("mix", g), ("mix", g + 1)], [at_, at_], 2)
        pe.wait_ge(S("merged"), 1)
        for k in range(KD):
            transposes("mT", k, [merged[:, t, tile(k)] for t in range(TT)])
        for k in range(KD):
            wait_read(pe, "mT", k)
        for c in range(2):
            columns_of_rows("w_out", None, [("wout", 2 * c), ("wout", 2 * c + 1)], [0, 0])

        pe.wait_ge(S("scaled"), 2)
        for k in range(KD):
            transposes("hfT", k, [xs[:, t, tile(k)] for t in range(TT)])
        for k in range(KD):
            wait_read(pe, "hfT", k)
        for t in range(TT):
            for half in range(2):
                transposes("hfrow", 2 * t + half, [modT[2][:, 4 * half + j, tile(t)] for j in range(4)])
        pe.wait_ge(S("modulated_lo"), 3 * KD)
        for m_ in range(16):
            feature_mm("w_pq", None, "pq", m_)
        pe.wait_ge(S("keys_in"), 16)
        for m_ in range(16):
            wait_read(pe, "pq", m_)
        for t in range(TT):
            for q_ in range(4):
                o = open_("ps", 4 * t + q_)
                for j in range(4):
                    m = mm(o[:, tile(j)], pqT[:, 4 * q_ + j, tile(t)], keysT[:, 4 * q_ + j, :], j == 0, j == 3)
                close(m)

        for t in range(TT):
            acc = [open_("acc", 2 * t + half) for half in range(2)]
            for half in range(2):
                mm(acc[half], zeros, G[:, 1, 0:512], True, False)
            for h in range(PEER_HEADS):
                g = t * PEER_HEADS + h
                pe.wait_ge(S("diag_ready"), g + 1)
                for j in range(TOPK):
                    r = j % V_RING
                    pe.wait_ge(S(f"v_in{r}"), 16 * (V_TURNS * g + j // V_RING + 1))
                    for half in range(2):
                        m = mm(acc[half], diag[:, j, :], v_row(r)[:, half * 512:(half + 1) * 512], False, False)
                    m.then_inc(S("v_used"), 1)
            for half in range(2):
                close(mm(acc[half], zeros, G[:, 1, 0:512], False, True))

        for l in range(LAYERS):
            L = f"L{l}."

            pe.wait_ge(S("scaled"), 3 + 2 * l)
            for k in range(KD):
                transposes(L + "hT", k, [xs[:, t, tile(k)] for t in range(TT)])
            for k in range(KD):
                wait_read(pe, L + "hT", k)
            for c in range(4):
                columns_of_rows("w2_qkv", l, [(L + "qkv", 2 * c), (L + "qkv", 2 * c + 1)], [0, 0])
            w = take("w2_small", l)
            for t in range(TT):
                close(rows_mm(open_(L + "small", t)[:, 0:104], 0, KD, t, w, 104))
            for m_ in range(24):
                feature_mm("w2_xbc", l, L + "xbc", m_)
            pe.wait_ge(S("roped"), l + 1)
            for h in range(10):
                transposes(L + "qT", h, [qkv2[:, t, tile(h)] for t in range(TT)])
            for h in range(5):
                transposes(L + "qiT", h, [kid[:, t, :] if h == 4 else qkv2[:, t, 1536 + h * P:1536 + (h + 1) * P]
                                          for t in range(TT)])
            for h in range(5):
                wait_read(pe, L + "qiT", h)
            for b_ in range(6):
                t, n_keys, heads_b = index_heads(b_)
                per = len(heads_b)
                o = open_(L + "is", b_)
                for j, h in enumerate(heads_b):
                    s_ = slice(64 * (h % 2), 64 * (h % 2) + 64)
                    m = mm(o[:, j * n_keys:(j + 1) * n_keys], qiT[s_, h // 2, tile(t)], qiT[s_, 4, 0:n_keys],
                           j == 0, j == per - 1)
                close(m)
            def z_columns(c):
                columns_of_rows("w2_z", l, [(L + "z", 2 * c), (L + "z", 2 * c + 1)], [0, 0])

            z_columns(0)
            z_columns(1)
            for h in range(10):
                wait_read(pe, L + "qT", h)
            for t in range(TT):
                n_keys, per = (P, 4) if t == 0 else (SEQ, 2)
                for b_ in range(8 // per):
                    o = open_(L + "s", 2 * t + b_)
                    for j in range(per):
                        h = b_ * per + j
                        m = mm(o[:, j * n_keys:(j + 1) * n_keys], qkT[:, h, tile(t)], qkT[:, 8 + h // 4, 0:n_keys],
                               j == 0, j == per - 1)
                    close(m)
                z_columns(2 + t)
                if t == 0:
                    pe.wait_ge(S("adt_ready"), l + 1)
                    o = open_(L + "acs", 0)
                    for c in range(TT):
                            mm(o[:, 32 * c:32 * c + 32], upto, adt[:, 32 * c:32 * c + 32], c == 0, False)
                    close(mm(o[:, 64:96], ones, adt[:, 0:32], False, True))
                pe.wait_ge(S("prob2"), TT * l + t + 1)
                for b_ in range(2 * t + 2):
                    kt, half = b_ // 2, b_ % 2
                    transposes(L + "p", 2 * t + b_, [pr[:, 4 * half + j, tile(kt)] for j in range(4)])
                for b_ in range(2 * t + 2):
                    wait_read(pe, L + "p", 2 * t + b_)
                for c in range(KVH):
                    o = open_(L + "o", 2 * t + c)
                    for kt in range(t + 1):
                        m = mm(o, qkv2[:, kt, 1280 + c * P:1280 + (c + 1) * P], prT[:, kt, 512 * c:512 * c + 512],
                               kt == 0, kt == t)
                    close(m)
            pe.wait_ge(S("xbc_ready"), 24 * l + 24)
            for t in range(TT):
                for q_ in range(4):
                    transposes(L + "X", 4 * t + q_, [xbcT[:, 4 * q_ + j, tile(t)] for j in range(4)])
            transposes(L + "Brow", 0, [xbcT[:, 16 + g, tile(0)] for g in range(4)])
            for c in range(TT):
                o = open_(L + "cb", c)
                for g in range(4):
                    m = mm(o[:, tile(g)], xbcT[:, 16 + g, tile(c)], xbcT[:, 20 + g, tile(c)], g == 0, g == 3)
                close(m)
            wait_read(pe, L + "Brow", 0)
            pe.wait_ge(S("xdec_ready"), l + 1)
            for g in range(4):
                close(mm(open_(L + "st", g), Brow[:, tile(g)], Xdec[:, 512 * g:512 * g + 512], True, True))

            def ssd_out(i):
                g, c = i // TT, i % TT
                pe.wait_ge(S("decay_ready"), 8 * l + i + 1)
                o = open_(L + "y", i)
                for h in range(HPG):
                    m = mm(o[:, SSD_P * h:SSD_P * (h + 1)], Lm[:, i % 2, tile(h)],
                           Xdt[:, c, 512 * g + SSD_P * h:512 * g + SSD_P * (h + 1)], h == 0, h == HPG - 1)
                close(m)
                if c:
                    wait_read(pe, L + "st", g)
                    close(mm(open_(L + "yo", i), xbcT[:, 20 + g, tile(c)], st[:, g, :], True, True))

            for i in range(SSD_G * TT):
                g, c = i // TT, i % TT
                for half in range(2):
                    o = open_(L + "seg", 2 * i + half)
                    mm(o.rearrange("p (a b) -> p a b", b=P), ident, K("after").unsqueeze(1).to_broadcast([P, 4, P]),
                       True, False)
                    for j in range(4):
                        h = g * HPG + 4 * half + j
                        m = mm(o[:, tile(j)], adt[:, 32 * c + h:32 * c + h + 1].to_broadcast([P, P]), upto,
                               False, j == 3)
                    close(m)
                if i:
                    ssd_out(i - 1)
                if c:
                    columns_of_rows("w2_g", l, [(L + "gate", i - 1), (L + "gate", i)], [0, 0])
            ssd_out(SSD_G * TT - 1)
            for t in range(TT * KVH):
                wait_read(pe, L + "o", t)
            for c in range(2):
                columns_of_rows("w2_pa", l, [(L + "pa", 2 * c), (L + "pa", 2 * c + 1)], [AT_AT] * 2)
            pe.wait_ge(S("y_ready"), l + 1)
            for m_ in range(16):
                transposes(L + "yT", m_, [X[:, t, tile(m_)] for t in range(TT)])
            for m_ in range(8):
                wait_read(pe, L + "yT", m_)

            def latter_yT():
                for m_ in range(8, 16):
                    wait_read(pe, L + "yT", m_)

            for c in range(2):
                columns_of_rows("w2_ps", l, [(L + "ps", 2 * c), (L + "ps", 2 * c + 1)], [0, 0], 8, before=latter_yT)
            pe.wait_ge(S("merged"), 2 + l)
            for k in range(KD):
                transposes(L + "mT", k, [merged2[:, t, tile(k)] for t in range(TT)])
            for k in range(KD):
                wait_read(pe, L + "mT", k)
            for c in range(2):
                columns_of_rows("w2_o", l, [(L + "wo", 2 * c), (L + "wo", 2 * c + 1)], [0, 0])
            pe.wait_ge(S("scaled"), 4 + 2 * l)
            for k in range(KD):
                transposes(L + "fT", k, [xs[:, t, tile(k)] for t in range(TT)])
            for k in range(KD):
                wait_read(pe, L + "fT", k)
            down = [open_(L + "dn", n, early=True) for n in range(4)]
            for c in range(FT // 2 + 1):
                if c < FT // 2:
                    for m_ in range(4):
                        feature_mm("w2_up", l, L + "up", 4 * c + m_)
                for k in range(2 * c - 2, 2 * c) if c else ():
                    w = take("w2_dn", l)
                    pe.wait_ge(S("glu_ready"), FT * l + k + 1)
                    for n in range(4):
                        m = rows_mm(down[n], GLU_AT + k % GLU_RING, 1, n % 2, w, 512, k == 0, k == FT - 1,
                                    at=512 * (n // 2))
                        if k == FT - 1:
                            close(m)
                    if k < FT - 1:
                        chunk_used(m)
            state["turn"] += 4

    @block.scalar
    def _(act):
        a = Progress(act, S("scalar_steps"))
        A = nc.scalar.activation
        act.dma_start(cols[:], d["cols"]).then_inc(S("cols_in"), 16)
        act.dma_start(arena[:, A_R:A_R + hyw_n], d["hyw"]).then_inc(S("hyw_in"), 16)
        act.dma_start(hyc, d["hyc"]).then_inc(S("hyc_in"), 16)

        def weights_high(n, c):
            act.wait_ge(weights_in[c % RING], 16 * (c // RING + 1))
            if n >= SPLIT_RING:
                act.wait_ge(*used(split_chunks[n - SPLIT_RING]))
            width = wplan[c][3]
            a.reaches(A(w_hi[:, n % SPLIT_RING, 0:width], wring[:, c % RING, 0:width], ACT.Copy), hi_ready, n + 1)

        streams[id(act)] = SplitStream(weights_high)

        def read_high(name, i, out_, in_, **kw):
            wait_filled(act, name, i)
            a.reaches(A(out_, in_, ACT.Copy, **kw), S("read_high"), hi_turn[(name, i)] + 1)

        def read_out(name, i, out_, in_, func=ACT.Copy, **kw):
            wait_filled(act, name, i)
            a.reaches(A(out_, in_, func, **kw), *read_value(name, i))

        def norm_std(n, srcs):
            for s_, v in enumerate(srcs):
                a.done(A(xs[:, s_ % TT, :], v, ACT.Square, accum_out=ss[:, s_:s_ + 1]))
                a.settle()
            a.reaches(A(std[:, 0:len(srcs)], ss[:, 0:len(srcs)], ACT.Sqrt, scale=1.0 / D, bias=K("epscol")),
                     S("std_ready"), n + 1)

        def modulated_high(n):
            for k in range(KD):
                wait_read(act, ("hT0", "hcT", "hfT")[n], k)
                at_ = KD * (n % 2) + k
                a.reaches(A(a_hi[:, at_, :], modT[n][:, k, :], ACT.Copy), S("modulated_hi"), KD * n + k + 1)

        act.wait_ge(S("cols_in"), 16)
        a.reaches(A(cT, V("c", 0, 16).rearrange("p (k v) -> p k v", v=2), ACT.Silu), S("c_ready"), 1)

        def ada_row_out(ch):
            if ch in ADA_COLS:
                ci = ADA_COLS.index(ch)
                if ci >= 2:
                    wait_filled(act, "adaT", ci - 2)
                read_out("ada", ch, ada_row[0:2, ci % 2, :], bank("ada", ch)[0:2, :])

        for i in range(3):
            ada_row_out(i)
            act.wait_ge(S("mlp_arg"), i + 1)
            a.reaches(A(mlp_h[0:64, :], mlp_u[0:64, :], ACT.Sin), S("mlp_h"), i + 1)
        ada_row_out(3)
        for t in range(TT):
            for j in range(4):
                wait_read(act, "filter", 4 * t + j)
        for o_ in range(2):
            if o_:
                wait_filled(act, "absum", 0)
            for t in range(TT):
                a.reaches(A(fabs[:, t, :, :], filt[:, t, 2 * o_:2 * o_ + 2, :], ACT.Abs), S("fabs_ready"),
                         2 * o_ + t + 1)
        for o_ in range(2):
            for i in range(4):
                f, kind = i % 2, i // 2
                wait_filled(act, "dftf", 4 * o_ + i)
                b_ = bank("dftf", 4 * o_ + i)
                if kind == 0 and f == 0:
                    a.done(A(Kr0[:, o_, :], b_, ACT.Copy))
                    a.settle()
                read_out("dftf", 4 * o_ + i, (Ki if kind else Kr)[:, o_, f, :], b_)
            read_out("nyq", o_, Kr0[0:1, o_, :], bank("nyq", o_)[0:1, :])
            ada_row_out(6 + o_)
        act.wait_ge(S("x_in"), 16)
        act.wait_ge(S("ctx_in"), 16)
        norm_std(0, [x[:, 0, :], x[:, 1, :], xc[:, 0, :], xc[:, 1, :]])
        ada_row_out(8)
        ada_row_out(9)
        modulated_high(0)
        modulated_high(1)
        for m_ in range(12):
            if m_ >= 4:
                act.wait_ge(S("conv_done"), m_ - 3)
            read_out("zhy", m_, zpre[:, m_ % 4, :], bank("zhy", m_)[:, 0:SEQ], ACT.Identity, bias=V("b_hy", m_))
        for t in range(TT):
            read_out("vrow", t, vrow[:, t, :], bank("vrow", t))
        for t in range(TT):
            read_out("yrow", t, vrow[:, t, :], bank("yrow", t))
        due(act, "conv", 7)
        act.wait_ge(S("na_sumsq"), 1)
        a.reaches(A(nstd, nsum, ACT.Sqrt, scale=1.0 / HD, bias=K("epscol")), S("na_std"), 1)
        for g in range(8):
            read_out("naT", g, naqT[:, g, :], bank("naT", g)[:, 0:SEQ])
        for g in range(4):
            read_out("nacT", g, nakcT[:, g, :], bank("nacT", g)[:, 0:SEQ])

        def na_turned(h):
            if h >= 1:
                wait_filled(act, "nao", h - 1)
            for t in range(TT):
                read_out("nap", 2 * h + t, napT[:, :, t * P:(t + 1) * P],
                         bank("nap", 2 * h + t).rearrange("p (a b) -> p a b", b=P))
            s_ = slice(64 * (h % 2), 64 * (h % 2) + 64)
            read_high("nao", h, a_hi[s_, NA_AT + h // 2, :], bank("nao", h)[s_, 0:SEQ])

        for h in range(NA_HEADS + 1):
            if h < NA_HEADS:
                for t in range(TT):
                    due(act, "nas", 2 * h + t)
                    act.wait_ge(S("na_max"), 2 * h + t + 1)
                    if h >= 2:
                        wait_filled(act, "nap", 2 * h - 4 + t)
                    read_out("nas", 2 * h + t, nap[h % 2][:, t, :], bank("nas", 2 * h + t), ACT.Exp,
                             bias=amax[:, 2 * h + t:2 * h + t + 1],
                             accum_out=asum[:, 2 * h + t:2 * h + t + 1])
            if h >= 1:
                na_turned(h - 1)
        for n in range(8):
            wait_read(act, "gate", n)
            a.reaches(A(sig(n), sig(n), ACT.Sigmoid), S("sig_ready"), n + 1)
        for k in range(KD):
            read_high("mT", k, a_hi[:, k, :], bank("mT", k)[:, 0:SEQ])
        due(act, "wout", 3)
        act.wait_ge(S("x_updated"), 1)
        norm_std(1, [x[:, 0, :], x[:, 1, :]])
        modulated_high(2)
        for n in range(1, 4, 2):
            read_out("hfrow", n, xs[:, n // 2, 512 * (n % 2):512 * (n % 2) + 512], bank("hfrow", n))
        for m_ in range(1, 16, 2):
            read_out("pq", m_, pqT[:, m_, :], bank("pq", m_)[:, 0:SEQ])
        for t in range(TT):
            for q_ in range(4):
                n = 16 * t + 4 * q_
                read_out("ps", 4 * t + q_, scr[:, n:n + 4, :],
                         bank("ps", 4 * t + q_).rearrange("p (a b) -> p a b", b=P))

        def pick_exp(g):
            act.wait_ge(S("peer_shifted"), g + 1)
            a.reaches(A(pexp[:, g, :], bests[:, g % 2, :], ACT.Exp, accum_out=psum_e[:, g:g + 1]), S("peer_exp"), g + 1)

        pick_exp(0)
        pick_exp(1)
        for g in range(TT * PEER_HEADS):
            act.wait_ge(S("dots_ready"), g + 1)
            a.reaches(A(pact, pdot, ACT.Gelu), S("gelu_ready"), g + 1)
            if g + 2 < TT * PEER_HEADS:
                pick_exp(g + 2)

        def scaled_high(name, n, wcol):
            for k in range(n):
                read_high(name, k, a_hi[:, k, :], bank(name, k)[:, 0:SEQ], scale=V(wcol, k))

        for l in range(LAYERS):
            L = f"L{l}."
            due(act, L + "hT", 0)
            act.wait_ge(S("x_updated"), 2 + 2 * l)
            norm_std(2 + 2 * l, [x[:, 0, :], x[:, 1, :]])
            scaled_high(L + "hT", KD, f"mixw{l}")
            for n in range(8):
                read_out(L + "qkv", n, qkv2[:, n % 2, 512 * (n // 2):512 * (n // 2) + 512], bank(L + "qkv", n))
            for t in range(TT):
                read_out(L + "small", t, small2[:, t, :], bank(L + "small", t)[:, 0:104])
            act.wait_ge(S("rows_in"), 48)
            for m_ in range(24):
                due(act, L + "xbc", m_)
                act.wait_ge(S("xconv"), 24 * l + m_ + 1)
                a.reaches(A(xbcT[:, m_, :], xbcT[:, m_, :], ACT.Silu), S("xbc_ready"), 24 * l + m_ + 1)
            for h in range(10):
                read_out(L + "qT", h, qkT[:, h, :], bank(L + "qT", h)[:, 0:SEQ])
            for h in range(5):
                read_out(L + "qiT", h, qiT[:, h, :], bank(L + "qiT", h)[:, 0:SEQ])
            for b_ in range(6):
                _, n_keys, heads_b = index_heads(b_)
                if b_ == 2:
                    act.wait_ge(S("rel_used"), TT * l + 1)
                read_out(L + "is", b_, rel[:, heads_b[0]:heads_b[-1] + 1:2, 0:n_keys],
                         bank(L + "is", b_).rearrange("p (h k) -> p h k", k=n_keys), ACT.Relu)
            act.wait_ge(S("dt_abs"), l + 1)
            a.done(A(u64, u64, ACT.Exp, scale=-1.0))
            a.reaches(A(negA, alog[:, 32 * l:32 * l + 32], ACT.Exp), S("dt_exp"), l + 1)

            def z_out(n):
                read_out(L + "z", n, zs[:, n % 2, 512 * (n // 2):512 * (n // 2) + 512], bank(L + "z", n), ACT.Silu)

            for n in range(4):
                z_out(n)
            for t in range(TT):
                n_keys = P * (t + 1)
                act.wait_ge(S("max2"), TT * l + t + 1)
                for h in range(H2):
                    a.done(A(pr[:, h, 0:n_keys], pr[:, h, 0:n_keys], ACT.Exp, bias=amax2[:, h:h + 1],
                             accum_out=asum2[:, h:h + 1]))
                a.settle()
                act.sem_inc(S("exp2"), 1)
                z_out(4 + 2 * t)
                z_out(5 + 2 * t)
                if t == 0:
                    act.wait_ge(S("acs_ready"), l + 1)
                    a.done(A(eacs, acs_s, ACT.Exp))
                    a.reaches(A(dstate, last_s, ACT.Exp), S("acs_exp"), l + 1)
                if t:
                    for c in range(KVH):
                        wait_filled(act, L + "o", c)
                for b_ in range(2 * t + 2):
                    kt, half = b_ // 2, b_ % 2
                    read_out(L + "p", 2 * t + b_, prT[:, kt, 512 * half:512 * half + 512], bank(L + "p", 2 * t + b_))
                for c in range(KVH):
                    read_high(L + "o", 2 * t + c, a_hi[:, AT_AT + 4 * c:AT_AT + 4 * c + 4, t * P:(t + 1) * P],
                              bank(L + "o", 2 * t + c).rearrange("p (h q) -> p h q", q=P))
            for t in range(TT):
                for q_ in range(4):
                    read_out(L + "X", 4 * t + q_, X[:, t, 512 * q_:512 * q_ + 512], bank(L + "X", 4 * t + q_))
            read_out(L + "Brow", 0, Brow, bank(L + "Brow", 0))
            for c in range(TT):
                read_out(L + "cb", c, cb[:, 4 * c:4 * c + 4, :],
                         bank(L + "cb", c).rearrange("p (g q) -> p g q", q=P))
            for g in range(4):
                read_out(L + "st", g, st[:, g, :], bank(L + "st", g))
            for i in range(SSD_G * TT):
                g, c = i // TT, i % TT
                if i >= 2:
                    wait_filled(act, L + "y", i - 2)
                for half in range(2):
                    wait_filled(act, L + "seg", 2 * i + half)
                    for j in range(4):
                        h = g * HPG + 4 * half + j
                        o = Lm[:, i % 2, (4 * half + j) * P:(4 * half + j + 1) * P]
                        src, bias = bank(L + "seg", 2 * i + half)[:, j * P:(j + 1) * P], nacs_s[:, 32 * c + h:32 * c + h + 1]
                        if j < 3:
                            a.done(A(o, src, ACT.Exp, bias=bias))
                        else:
                            a.reaches(A(o, src, ACT.Exp, bias=bias), *read_value(L + "seg", 2 * i + half))
                for n in (i - 1, i) if c else ():
                    read_out(L + "gate", n, sig2[:, n % 2, 512 * (n // 2):512 * (n // 2) + 512], bank(L + "gate", n),
                             ACT.Sigmoid)
            due(act, L + "pa", 0)
            act.wait_ge(S("yz_ready"), l + 1)
            for t in range(TT):
                for g in range(SSD_G):
                    a.done(A(Lm[:, g // 2, g % 2 * 512:g % 2 * 512 + 512], X[:, t, 512 * g:512 * g + 512], ACT.Square,
                             accum_out=gsum[:, 4 * t + g:4 * t + g + 1]))
                a.settle()
            a.reaches(A(gstd, gsum, ACT.Sqrt, scale=1.0 / 512, bias=K("epscol")), S("gstd_ready"), l + 1)
            scaled_high(L + "yT", 16, f"snw{l}")
            for k in range(KD):
                read_high(L + "mT", k, a_hi[:, k, :], bank(L + "mT", k)[:, 0:SEQ])
            due(act, L + "wo", 3)
            act.wait_ge(S("x_updated"), 3 + 2 * l)
            norm_std(3 + 2 * l, [x[:, 0, :], x[:, 1, :]])
            scaled_high(L + "fT", KD, f"ffnw{l}")
            for i in range(FT):
                due(act, L + "up", 4 * (i // 2) + i % 2)
                act.wait_ge(S("gate_conv"), FT * l + i + 1)
                o = conv_o[:, (i // 2) % 2 * 4 + i % 2, :]
                a.reaches(A(o, o, ACT.Silu), S("gate_silu"), FT * l + i + 1)
        due(act, BIG(LAYERS - 1) + "dn", 3)
        act.wait_ge(S("x_updated"), 6)
        norm_std(6, [x[:, 0, :], x[:, 1, :]])

    @block.vector
    def _(dve):
        v = Progress(dve, S("vector_steps"))
        T = nc.vector

        def readv(name, i, ins):
            v.reaches(ins, *read_value(name, i))

        def norm_scale(n, srcs, dsts):
            dve.wait_ge(S("std_ready"), n + 1)
            m = len(srcs)
            v.done(T.reciprocal(rinv[:, 0:m], std[:, 0:m]))
            v.settle()
            for i, (s_, o) in enumerate(zip(srcs, dsts)):
                ins = T.tensor_scalar(o, s_, rinv[:, i:i + 1], None, ALU.mult)
                if i < m - 1:
                    v.done(ins)
            v.reaches(ins, S("scaled"), n + 1)

        def modulated(n, name, s_, shift, c):
            for k in range(KD):
                wait_filled(dve, name, k)
                readv(name, k, T.tensor_scalar(modT[n][:, k, :], bank(name, k)[:, 0:SEQ], mod_a[:, s_, k:k + 1],
                                               adaT[:, shift + k, c:c + 1], ALU.mult, ALU.add))
            for k in range(KD):
                dve.wait_ge(S("modulated_hi"), KD * n + k + 1)
                at_ = KD * (n % 2) + k
                v.reaches(T.tensor_tensor(a_lo[:, at_, :], modT[n][:, k, :], a_hi[:, at_, :].bitcast(F32),
                                          ALU.subtract), S("modulated_lo"), KD * n + k + 1)

        def read_low(name, i, hi, lo, in_, scale=None):
            wait_filled(dve, name, i)
            dve.wait_ge(S("read_high"), hi_turn[(name, i)] + 1)
            if scale is None:
                ins = T.tensor_tensor(lo, in_, hi.bitcast(F32), ALU.subtract)
            else:
                ins = T.scalar_tensor_tensor(out=lo, in0=in_, scalar=scale, in1=hi.bitcast(F32), op0=ALU.mult,
                                             op1=ALU.subtract)
            readv(name, i, ins)

        def tt(o, a_, b_, op):
            v.done(T.tensor_tensor(o, a_, b_, op))

        def ts(o, a_, s1, s2, op0, op1=None):
            v.done(T.tensor_scalar(o, a_, s1, s2, op0, op1) if op1 is not None else
                   T.tensor_scalar(o, a_, s1, None, op0))

        def stt(o, a_, s_, b_, op0, op1):
            v.done(T.scalar_tensor_tensor(out=o, in0=a_, scalar=s_, in1=b_, op0=op0, op1=op1))

        dve.wait_ge(S("cols_in"), 16)
        u, kk = mlp_u[0:64, :], mlp_k[0:64, :]

        def ada_out(ch):
            if ch - 1 in ADA_COLS:
                ci = ADA_COLS.index(ch - 1)
                wait_filled(dve, "adaT", ci)
                readv("adaT", ci, T.tensor_tensor(
                    adaT[:, 4 * ci:4 * ci + 4, :], bank("adaT", ci)[:, 0:8].rearrange("p (j v) -> p j v", v=2),
                    V("b_ada", 4 * (ch - 1), 4).unsqueeze(2).to_broadcast([P, 4, 2]), ALU.add))
            if ch not in ADA_COLS:
                wait_filled(dve, "ada", ch)
                dve.wait_ge(S("bias_g_in"), 32)
                g_, half = ch // 10, ch % 2
                gs = G[:, g_, 512 * half:512 * half + 512]
                readv("ada", ch, T.tensor_tensor(gs, bank("ada", ch), gs, ALU.add))

        for i in range(3):
            ada_out(i)
            wait_filled(dve, "mlp", i)
            readv("mlp", i, T.tensor_scalar(u, bank("mlp", i)[0:64, 0:SEQ], V(f"f{i + 1}b")[0:64, :],
                                            V("freq")[0:64, :], ALU.add, ALU.mult))
            v.settle()
            ts(kk, u, 1.0 / (2 * math.pi), MAGIC, ALU.mult, ALU.add)
            v.settle()
            ts(kk, kk, -MAGIC, None, ALU.add)
            for cc in (C1, C2_, C3):
                v.settle()
                stt(u, kk, -cc, u, ALU.mult, ALU.add)
            v.settle()
            v.reaches(T.tensor_scalar(u, u, 3.1415925, -3.1415925, ALU.min, ALU.max), S("mlp_arg"), i + 1)
        ada_out(3)
        dve.wait_ge(S("hyc_in"), 16)
        for t in range(TT):
            for j in range(4):
                wait_filled(dve, "filter", 4 * t + j)
                readv("filter", 4 * t + j, T.tensor_tensor(filt[:, t, j, :], bank("filter", 4 * t + j),
                                                           HC3("decay", 512)[:, t, :], ALU.mult))
        ada_out(4)
        for o_ in range(2):
            wait_filled(dve, "absum", o_)
            readv("absum", o_, T.reciprocal(rnorm[:, o_, :], bank("absum", o_)))
            for t in range(TT):
                fw, bw, tmp = filt[:, t, 2 * o_, :], filt[:, t, 2 * o_ + 1, :], dve_junk[:, t * 512:(t + 1) * 512]
                v.settle()
                if t == 0:
                    stt(tmp, bw, HC("not_first"), fw, ALU.mult, ALU.add)
                else:
                    tt(tmp, bw, fw, ALU.add)
                v.settle()
                tt(bw, bw, fw, ALU.subtract)
                v.settle()
                tt(fw, tmp, rnorm[:, o_, :], ALU.mult)
                ins = T.tensor_tensor(bw, bw, rnorm[:, o_, :], ALU.mult)
                if t == TT - 1:
                    v.reaches(ins, S("filters_ready"), o_ + 1)
                else:
                    v.done(ins)
        for ch in range(5, 8):
            ada_out(ch)
        norm_scale(0, [x[:, 0, :], x[:, 1, :], xc[:, 0, :], xc[:, 1, :]],
                   [xs[:, 0, :], xs[:, 1, :], xc[:, 0, :], xc[:, 1, :]])
        for ch in range(8, 12):
            ada_out(ch)
        v.settle()
        for s_, (sc, c, g_) in enumerate(((8, 0, "g1n"), (8, 1, "g1n"), (24, 0, "g2n"))):
            ins = T.scalar_tensor_tensor(out=mod_a[:, s_, :], in0=adaT[:, sc:sc + 8, c], scalar=1.0,
                                         in1=V(g_, 0, 8), op0=ALU.add, op1=ALU.mult)
            v.done(ins)
        v.settle()
        modulated(0, "hT0", 0, 0, 0)
        modulated(1, "hcT", 1, 0, 1)
        for m_ in range(12):
            wait_read(dve, "zhy", m_)
            z, o = zpre[:, m_ % 4, :], zcT[:, m_, :]
            ts(o, z, V("cw", 12 + m_), V("cb", m_), ALU.mult, ALU.add)
            v.settle()
            stt(o[:, 1:SEQ], z[:, 0:SEQ - 1], V("cw", m_), o[:, 1:SEQ], ALU.mult, ALU.add)
            v.settle()
            v.reaches(T.scalar_tensor_tensor(out=o[:, 0:SEQ - 1], in0=z[:, 1:SEQ], scalar=V("cw", 24 + m_),
                                            in1=o[:, 0:SEQ - 1], op0=ALU.mult, op1=ALU.add),
                     S("conv_done"), m_ + 1)
        dve.wait_ge(S("bias_qkv_in"), 16)

        def projected(n):
            j, src, t = (0, 0, n) if n < 2 else ((n - 2) // 4 + 1, (n - 2) // 2 % 2, n % 2)
            wait_filled(dve, "zqkv", n)
            o = qkv[:, t, j * 512:(j + 1) * 512] if src == 0 else kvc[:, t, (j - 1) * 512:j * 512]
            readv("zqkv", n, T.tensor_tensor(o, bank("zqkv", n), bias_qkv[:, j * 512:(j + 1) * 512], ALU.add))

        for n in range(2):
            projected(n)

        def gated_parts(at_, value, gate, sem, n):
            v.done(T.tensor_tensor(a_hi[:, at_, :], value, gate, ALU.mult))
            v.done(T.tensor_tensor(value, value, gate, ALU.mult))
            v.settle()
            v.reaches(T.tensor_tensor(a_lo[:, at_, :], value, a_hi[:, at_, :].bitcast(F32), ALU.subtract), sem, n)

        for o_ in range(2):
            for f in range(2):
                yr, yi = bank("spec", 4 * o_ + 2 * f), bank("spec", 4 * o_ + 2 * f + 1)
                kr, ki = Kr[:, o_, f, :], Ki[:, o_, f, :]
                k2 = Kr0[:, o_, :] if f == 0 else kr
                wait_filled(dve, "spec", 4 * o_ + 2 * f + 1)
                v.settle()
                tt(prod_r[:, f, :], yr, kr, ALU.mult)
                tt(tmp_a, yi, ki, ALU.mult)
                readv("spec", 4 * o_ + 2 * f, T.tensor_tensor(prod_i[:, f, :], yr, ki, ALU.mult))
                v.settle()
                tt(prod_r[:, f, :], prod_r[:, f, :], tmp_a, ALU.subtract)
                v.settle()
                readv("spec", 4 * o_ + 2 * f + 1, T.tensor_tensor(tmp_a, yi, k2, ALU.mult))
                v.settle()
                v.reaches(T.tensor_tensor(prod_i[:, f, :], prod_i[:, f, :], tmp_a, ALU.add),
                         S("product_ready"), 2 * o_ + f + 1)
            for n in range(2 + 4 * o_, 6 + 4 * o_):
                projected(n)
            src, tmp_y = (zcT, y1T)[o_], dve_junk[:, 512:512 + SEQ]
            for m_ in range(HY_T):
                gate = zcT[:, HY_T * (o_ + 1) + m_, :]
                wait_filled(dve, "conv", 4 * o_ + m_)
                readv("conv", 4 * o_ + m_, T.scalar_tensor_tensor(
                    out=tmp_y, in0=src[:, m_, :], scalar=V("skip", 4 * o_ + m_),
                    in1=bank("conv", 4 * o_ + m_)[:, 0:SEQ], op0=ALU.mult, op1=ALU.add))
                v.settle()
                if o_ == 0:
                    v.reaches(T.tensor_tensor(y1T[:, m_, :], tmp_y, gate, ALU.mult), S("y1_ready"), m_ + 1)
                    v.settle()
                else:
                    gated_parts(HY_AT + m_, tmp_y, gate, S("yh_ready"), m_ + 1)
                    v.settle()
        wait_filled(dve, "conv", 7)
        heads = lambda ap: ap.rearrange("p (h e) -> p h e", e=HD)
        for t in range(TT):
            tt(nat[:, t, :], qkv[:, t, 0:D], qkv[:, t, 0:D], ALU.mult)
            tt(nakc[:, t, :], kvc[:, t, 0:512], kvc[:, t, 0:512], ALU.mult)
        v.settle()
        for t in range(TT):
            v.done(T.tensor_reduce(nsum[:, 16 * t:16 * t + 16], heads(nat[:, t, :]), AX, ALU.add))
            ins = T.tensor_reduce(nsum[:, 32 + 8 * t:40 + 8 * t], heads(nakc[:, t, :]), AX, ALU.add)
            if t == 0:
                v.done(ins)
            else:
                v.reaches(ins, S("na_sumsq"), 1)
        dve.wait_ge(S("na_std"), 1)
        v.done(T.reciprocal(ninv, nstd))
        v.settle()
        for t in range(TT):
            ts(ninv[:, 16 * t:16 * t + 8], ninv[:, 16 * t:16 * t + 8], HD ** -0.5, None, ALU.mult)
        v.settle()
        dve.wait_ge(S("qk_g_in"), 16)
        for t in range(TT):
            inv = ninv[:, 16 * t:16 * t + 16].unsqueeze(2).to_broadcast([P, 16, HD])
            tt(heads(naq[:, t, :]), heads(qkv[:, t, 0:D]), inv, ALU.mult)
            inv = ninv[:, 32 + 8 * t:40 + 8 * t].unsqueeze(2).to_broadcast([P, 8, HD])
            tt(heads(nakc[:, t, :]), heads(kvc[:, t, 0:512]), inv, ALU.mult)
        v.settle()
        for t in range(TT):
            for s_ in range(2):
                g_ = qk_g[:, HD * s_:HD * (s_ + 1)].unsqueeze(1).to_broadcast([P, 8, HD])
                hs = heads(naq[:, t, 512 * s_:512 * s_ + 512])
                tt(hs, hs, g_, ALU.mult)
            tt(heads(nakc[:, t, :]), heads(nakc[:, t, :]), g_, ALU.mult)
        v.settle()
        for t in range(TT):
            c64 = K("rope_c")[:, HD * t:HD * t + HD].unsqueeze(1).to_broadcast([P, 16, HD])
            tt(heads(nat[:, t, :]), heads(naq[:, t, :]), c64, ALU.mult)
            for ab in range(2):
                pick = lambda ap: ap.rearrange("p (h f b e) -> p h f b e", f=2, b=2, e=16)
                for f in range(2):
                    s64 = K("rope_s")[:, HD * t + 32 * f + 16 * ab:HD * t + 32 * f + 16 * ab + 16]
                    tt(pick(dve_junk[:])[:, :, f, ab, :], pick(naq[:, t, :])[:, :, f, 1 - ab, :],
                       s64.unsqueeze(1).to_broadcast([P, 16, 16]), ALU.mult)
            v.settle()
            ins = T.tensor_tensor(nat[:, t, :], nat[:, t, :], dve_junk[:], ALU.add)
            if t == 0:
                v.done(ins)
                v.settle()
            else:
                v.reaches(ins, S("na_rows"), 1)
        dve.wait_ge(S("na_mask_in"), 16)

        def masked_bias(h):
            dve.wait_ge(S(f"rpb_in{h % 2}"), 16 * (h // 2 + 1))
            v.reaches(T.tensor_tensor(nabias[:, h % 2, :], nabias[:, h % 2, :], namask, ALU.add),
                     S("bias_ready"), h + 1)

        def na_low(h):
            s_, at_ = slice(64 * (h % 2), 64 * (h % 2) + 64), NA_AT + h // 2
            read_low("nao", h, a_hi[s_, at_, :], a_lo[s_, at_, :], bank("nao", h)[s_, 0:SEQ])

        def gate_bias(c):
            dve.wait_ge(S("bias_gate_in"), 32)
            for n in (2 * c, 2 * c + 1):
                wait_filled(dve, "gate", n)
                readv("gate", n, T.tensor_tensor(sig(n), bank("gate", n), bias_gate[c // 2][:, c % 2 * 512:c % 2 * 512 + 512],
                                                 ALU.add))

        masked_bias(0)
        for h in range(NA_HEADS):
            if h + 1 < NA_HEADS:
                masked_bias(h + 1)
            for t in range(TT):
                i = 2 * h + t
                wait_filled(dve, "nas", i)
                v.reaches(T.tensor_reduce(amax[:, i:i + 1], bank("nas", i), AX, ALU.max, negate=True),
                         S("na_max"), i + 1)
            for t in range(TT):
                i = 2 * h + t
                wait_read(dve, "nas", i)
                v.done(T.reciprocal(ainv[:, i:i + 1], asum[:, i:i + 1]))
                v.settle()
                v.reaches(T.tensor_scalar(nap[h % 2][:, t, :], nap[h % 2][:, t, :], ainv[:, i:i + 1], None, ALU.mult),
                         S("na_prob"), i + 1)
            if h:
                if h % 2 == 0:
                    gate_bias(h // 2 - 1)
                na_low(h - 1)
        gate_bias(NA_HEADS // 2 - 1)
        na_low(NA_HEADS - 1)
        dve.wait_ge(S("sig_ready"), 8)
        for n in range(8):
            src, half, t = n // 4, n // 2 % 2, n % 2
            sg = sig(2 * (2 * src + half) + t)
            mg = merged[:, t, 512 * half:512 * half + 512]
            wait_filled(dve, "mix", n)
            if src == 0:
                readv("mix", n, T.tensor_tensor(mg, bank("mix", n), sg, ALU.mult))
            else:
                readv("mix", n, T.tensor_tensor(sg, bank("mix", n), sg, ALU.mult))
                v.settle()
                ins = T.tensor_tensor(mg, mg, sg, ALU.add)
                if n == 7:
                    v.reaches(ins, S("merged"), 1)
                else:
                    v.done(ins)
        for k in range(KD):
            read_low("mT", k, a_hi[:, k, :], a_lo[:, k, :], bank("mT", k)[:, 0:SEQ])
        for n in range(4):
            c, t = n // 2, n % 2
            wait_filled(dve, "wout", n)
            tmp = dve_junk[:, 512 * (n % 2):512 * (n % 2) + 512]
            readv("wout", n, T.tensor_tensor(tmp, bank("wout", n), G[:, 0, 512 * c:512 * c + 512], ALU.mult))
            v.settle()
            xv = x[:, t, 512 * c:512 * c + 512]
            ins = T.tensor_tensor(xv, xv, tmp, ALU.add)
            if n == 3:
                v.reaches(ins, S("x_updated"), 1)
            else:
                v.done(ins)
        norm_scale(1, [x[:, 0, :], x[:, 1, :]], [xs[:, 0, :], xs[:, 1, :]])
        modulated(2, "hfT", 2, 16, 0)
        for n in range(0, 4, 2):
            wait_filled(dve, "hfrow", n)
            readv("hfrow", n, T.tensor_copy(xs[:, n // 2, 512 * (n % 2):512 * (n % 2) + 512], bank("hfrow", n)))
        for m_ in range(0, 16, 2):
            wait_filled(dve, "pq", m_)
            readv("pq", m_, T.tensor_copy(pqT[:, m_, :], bank("pq", m_)[:, 0:SEQ]))

        def best_sixteen(n, vals, work, top, pos):
            for i in range(n):
                v.done(T.max(top[:, i, 0:8], vals[:, i, :]))
            v.settle()
            for i in range(n):
                v.done(T.max_index(pos[:, i, 0:8], top[:, i, 0:8], vals[:, i, :]))
            for i in range(n):
                v.done(T.match_replace(work[:, i, :], top[:, i, 0:8], vals[:, i, :], TAKEN))
            v.settle()
            for i in range(n):
                v.done(T.max(top[:, i, 8:16], work[:, i, :]))
            v.settle()
            for i in range(n):
                v.done(T.max_index(pos[:, i, 8:16], top[:, i, 8:16], work[:, i, :]))
            v.settle()

        bc = lambda ap, ax, shape: ap.unsqueeze(ax).to_broadcast(shape)
        heads_n = TT * PEER_HEADS

        def pick(g):
            if g % PEER_HEADS == 0:
                for q_ in range(4):
                    wait_read(dve, "ps", 4 * (g // PEER_HEADS) + q_)
            best_sixteen(2, scr[:, 2 * g:2 * g + 2, :], scw, tops, topi_u)
            v.done(T.tensor_copy(topi, topi_u))
            tt(cand[:, 0, :].rearrange("p (a b) -> p a b", b=16), bc(tops[:, 0, :], 2, [P, 16, 16]),
               bc(tops[:, 1, :], 1, [P, 16, 16]), ALU.add)
            v.settle()
            if g >= 2:
                dve.wait_ge(S("peer_exp"), g - 1)
            best = bests[:, g % 2:g % 2 + 1, :]
            best_sixteen(1, cand, candw, best, bpos_u)
            ts(b_sh[:, 0, :], bpos_u[:, 0, :], 4, None, ALU.logical_shift_right)
            ts(b_sh[:, 1, :], bpos_u[:, 0, :], 15, None, ALU.bitwise_and)
            v.done(T.tensor_copy(pinv, best[:, 0, 0:1]))
            v.settle()
            v.done(T.tensor_copy(bpos, b_sh))
            v.reaches(T.tensor_scalar(best, best, pinv, None, ALU.subtract), S("peer_shifted"), g + 1)
            v.settle()
            for s_ in range(2):
                tt(oh, bc(bpos[:, s_, :], 2, [P, 16, 16]), bc(K("count16"), 1, [P, 16, 16]), ALU.is_equal)
                v.settle()
                tt(oh, oh, bc(topi[:, s_, :], 1, [P, 16, 16]), ALU.mult)
                v.settle()
                v.done(T.tensor_reduce(i_two[:, s_, :], oh, AX, ALU.add))
                v.settle()
            v.reaches(T.scalar_tensor_tensor(out=pidx[:, g, :], in0=i_two[:, 0, :], scalar=float(N_KEYS),
                                             in1=i_two[:, 1, :], op0=ALU.mult, op1=ALU.add), S("picks_ready"), g + 1)

        for n in range(8):
            wait_filled(dve, "ps", n)
        pick(0)
        pick(1)
        for g in range(heads_n):
            t = g // PEER_HEADS
            for j in range(TOPK):
                s_ = j % U_RING
                dve.wait_ge(S(f"u_in{s_}"), 16 * (U_TURNS * g + j // U_RING + 1))
                v.settle()
                v.reaches(T.tensor_tensor_reduce(out=dve_junk[:], in0=u_rows[:, s_, :], in1=xs[:, t, :], scale=1.0,
                                                scalar=0.0, op0=ALU.mult, op1=ALU.add,
                                                accum_out=pdot[:, j:j + 1]), S("u_used"), TOPK * g + j + 1)
            v.settle()
            dve.sem_inc(S("dots_ready"), 1)
            dve.wait_ge(S("peer_exp"), g + 1)
            v.done(T.reciprocal(pinv, psum_e[:, g:g + 1]))
            dve.wait_ge(S("gelu_ready"), g + 1)
            v.settle()
            stt(pw, pact, pinv, pexp[:, g, :], ALU.mult, ALU.mult)
            v.settle()
            if g:
                dve.wait_ge(S("v_used"), TOPK * g)
            v.reaches(T.tensor_tensor(diag, bc(ident, 1, [P, TOPK, P]), bc(pw, 2, [P, TOPK, P]), ALU.mult),
                     S("diag_ready"), g + 1)
            if g + 2 < heads_n:
                pick(g + 2)
            if g % PEER_HEADS == PEER_HEADS - 1:
                for half in range(2):
                    wait_filled(dve, "acc", 2 * t + half)
                    hs = slice(512 * half, 512 * half + 512)
                    readv("acc", 2 * t + half, T.tensor_tensor(dve_junk[:, hs], bank("acc", 2 * t + half),
                                                               G[:, 1, hs], ALU.mult))
                    v.settle()
                    ins = T.tensor_tensor(x[:, t, hs], x[:, t, hs], dve_junk[:, hs], ALU.add)
                    if g == heads_n - 1 and half:
                        v.reaches(ins, S("x_updated"), 2)
                    else:
                        v.done(ins)
                        v.settle()

        def scaled_low(name, ks, wcol):
            for k in ks:
                read_low(name, k, a_hi[:, k, :], a_lo[:, k, :], bank(name, k)[:, 0:SEQ], V(wcol, k))

        def rope2(view, heads_, r, c_, s_):
            xr = view[:, :, 0:2 * r]
            t1 = dve_junk[:, 0:heads_ * 2 * r].rearrange("p (h e) -> p h e", e=2 * r)
            t2 = dve_junk[:, 512:512 + heads_ * 2 * r].rearrange("p (h e) -> p h e", e=2 * r)
            tt(t1, xr, bc(c_, 1, [P, heads_, 2 * r]), ALU.mult)
            for ab in range(2):
                tt(t2[:, :, ab * r:(ab + 1) * r], xr[:, :, (1 - ab) * r:(2 - ab) * r],
                   bc(s_[:, ab * r:(ab + 1) * r], 1, [P, heads_, r]), ALU.mult)
            v.settle()
            tt(xr, t1, t2, ALU.add)
            v.settle()

        def conv_in(name, i, o, wcol, bcol, taps, stride, col):
            wait_filled(dve, name, i)
            ps = bank(name, i)[:, 0:SEQ]
            ts(o, ps, V(wcol, stride * (taps - 1) + col), V(bcol, col), ALU.mult, ALU.add)
            for j in range(1, taps):
                v.settle()
                ins = T.scalar_tensor_tensor(out=o[:, j:SEQ], in0=ps[:, 0:SEQ - j],
                                             scalar=V(wcol, stride * (taps - 1 - j) + col), in1=o[:, j:SEQ],
                                             op0=ALU.mult, op1=ALU.add)
                if j < taps - 1:
                    v.done(ins)
            readv(name, i, ins)
            v.settle()

        for l in range(LAYERS):
            L = f"L{l}."
            norm_scale(2 + 2 * l, [x[:, 0, :], x[:, 1, :]], [xs[:, 0, :], xs[:, 1, :]])
            scaled_low(L + "hT", range(KD), f"mixw{l}")
            for n in range(8):
                wait_read(dve, L + "qkv", n)
            for t in range(TT):
                wait_read(dve, L + "small", t)
                rope2(qkv2[:, t, 0:1280].rearrange("p (h e) -> p h e", e=HD2), 10, 16,
                      K("rope2_ca")[:, 32 * t:32 * t + 32], K("rope2_sa")[:, 32 * t:32 * t + 32])
                rope2(qkv2[:, t, 1536:2048].rearrange("p (h e) -> p h e", e=IDX_DIM), 8, 8,
                      K("rope2_ci")[:, 16 * t:16 * t + 16], K("rope2_si")[:, 16 * t:16 * t + 16])
                rope2(small2[:, t, 0:64].unsqueeze(1), 1, 8,
                      K("rope2_ci")[:, 16 * t:16 * t + 16], K("rope2_si")[:, 16 * t:16 * t + 16])
                v.done(T.tensor_copy(kid[:, t, 0:64], small2[:, t, 0:64]))
                v.done(T.tensor_copy(kid[:, t, 64:128], small2[:, t, 0:64]))
            v.settle()
            dve.sem_inc(S("roped"), 1)
            for m_ in range(24):
                conv_in(L + "xbc", m_, xbcT[:, m_, :], f"scw{l}", f"scb{l}", 4, 24, m_)
                dve.sem_inc(S("xconv"), 1)
            dve.wait_ge(S("rows_in"), 48)
            h64 = lambda ap: ap.rearrange("p (t h) -> p t h", h=32)
            tt(h64(x64), small2[:, :, 72:104], bc(dtb[:, 32 * l:32 * l + 32], 1, [P, TT, 32]), ALU.add)
            v.settle()
            ts(v64, x64, -1.0, None, ALU.mult)
            v.settle()
            v.reaches(T.tensor_tensor(u64, x64, v64, ALU.max), S("dt_abs"), l + 1)
            for t in range(TT):
                n_keys = P * (t + 1)
                for b_ in range(2) if t == 0 else range(2, 6):
                    wait_read(dve, L + "is", b_)
                sc, sw = isc[:, t, 0:n_keys], iscw[:, t, 0:n_keys]
                ca = K("causal")[:, SEQ - n_keys:SEQ]
                wi = small2[:, t, 64:72]
                ts(sc, rel[:, 0, 0:n_keys], wi[:, 0:1], None, ALU.mult)
                for h in range(1, IDX_HEADS):
                    v.settle()
                    ins = T.scalar_tensor_tensor(out=sc, in0=rel[:, h, 0:n_keys], scalar=wi[:, h:h + 1], in1=sc,
                                                 op0=ALU.mult, op1=ALU.add)
                    if h < IDX_HEADS - 1:
                        v.done(ins)
                v.reaches(ins, S("rel_used"), TT * l + t + 1)
                v.settle()
                tt(sc, sc, ca, ALU.add)
                for r in range(SEL // 8):
                    a_, b_ = (sc, sw) if r % 2 == 0 else (sw, sc)
                    v.settle()
                    v.done(T.max(best8, a_))
                    v.settle()
                    v.done(T.match_replace(b_, best8, a_, TAKEN))
                v.settle()
                ts(sw, sc, TAKEN, -NEG, ALU.is_equal, ALU.mult)
                v.settle()
                stt(madd[:, t, 0:n_keys], sw, NEG, ca, ALU.add, ALU.add)
            v.settle()
            dve.wait_ge(S("dt_exp"), l + 1)
            t2_, p_ = dve_junk[:, 0:64], dve_junk[:, 64:128]
            ts(v64, u64, 2.0, None, ALU.add)
            v.settle()
            v.done(T.reciprocal(v64, v64))
            v.settle()
            tt(v64, u64, v64, ALU.mult)
            v.settle()
            tt(t2_, v64, v64, ALU.mult)
            v.settle()
            ts(p_, t2_, 1.0 / 15, None, ALU.mult)
            for n in (13, 11, 9, 7, 5, 3):
                v.settle()
                stt(p_, p_, 1.0 / n, t2_, ALU.add, ALU.mult)
            v.settle()
            stt(p_, p_, 1.0, v64, ALU.add, ALU.mult)
            v.settle()
            ts(p_, p_, 2.0, None, ALU.mult)
            v.settle()
            stt(dt_s, x64, 0.0, p_, ALU.max, ALU.add)
            v.settle()
            v.reaches(T.scalar_tensor_tensor(out=h64(adt), in0=h64(dt_s), scalar=-1.0,
                                            in1=bc(negA, 1, [P, TT, 32]), op0=ALU.mult, op1=ALU.mult),
                     S("adt_ready"), l + 1)
            def attended_low(t):
                for c in range(KVH):
                    at_ = slice(AT_AT + 4 * c, AT_AT + 4 * c + 4)
                    tok = slice(t * P, (t + 1) * P)
                    read_low(L + "o", 2 * t + c, a_hi[:, at_, tok], a_lo[:, at_, tok],
                             bank(L + "o", 2 * t + c).rearrange("p (h q) -> p h q", q=P))

            for t in range(TT):
                n_keys, per = (P, 4) if t == 0 else (SEQ, 2)
                if t:
                    wait_filled(dve, L + "p", 1)
                for b_ in range(8 // per):
                    wait_filled(dve, L + "s", 2 * t + b_)
                    readv(L + "s", 2 * t + b_, T.scalar_tensor_tensor(
                        out=pr[:, b_ * per:(b_ + 1) * per, 0:n_keys],
                        in0=bank(L + "s", 2 * t + b_).rearrange("p (h k) -> p h k", k=n_keys), scalar=SCALE2,
                        in1=bc(madd[:, t, 0:n_keys], 1, [P, per, n_keys]), op0=ALU.mult, op1=ALU.add))
                v.settle()
                v.reaches(T.tensor_reduce(amax2, pr[:, :, 0:n_keys], AX, ALU.max, negate=True), S("max2"),
                         TT * l + t + 1)
                if t:
                    attended_low(0)
                dve.wait_ge(S("exp2"), TT * l + t + 1)
                v.done(T.reciprocal(ainv2, asum2))
                v.settle()
                v.reaches(T.tensor_tensor(pr[:, :, 0:n_keys], pr[:, :, 0:n_keys], bc(ainv2, 2, [P, 8, n_keys]),
                                         ALU.mult), S("prob2"), TT * l + t + 1)
                if t == 0:
                    wait_filled(dve, L + "acs", 0)
                    v.done(T.tensor_copy(acs_s, bank(L + "acs", 0)[:, 0:64]))
                    v.settle()
                    ts(nacs_s, acs_s, -1.0, None, ALU.mult)
                    readv(L + "acs", 0, T.tensor_tensor(last_s, bank(L + "acs", 0)[:, 64:96], acs_s[:, 0:32], ALU.subtract))
                    v.settle()
                    dve.sem_inc(S("acs_ready"), 1)
            attended_low(1)
            h32 = lambda ap: ap.rearrange("p (h e) -> p h e", e=SSD_P)
            for t in range(TT):
                for q_ in range(4):
                    wait_read(dve, L + "X", 4 * t + q_)
                if t == 0:
                    wait_filled(dve, L + "o", 3)
                tt(h32(Xdt[:, t, :]), h32(X[:, t, :]), bc(dt_s[:, 32 * t:32 * t + 32], 2, [P, 32, SSD_P]), ALU.mult)
                v.settle()
                if t == 0:
                    dve.wait_ge(S("acs_exp"), l + 1)
                    v.reaches(T.tensor_tensor(h32(Xdec), h32(Xdt[:, 0, :]), bc(dstate, 2, [P, 32, SSD_P]), ALU.mult),
                             S("xdec_ready"), l + 1)
            def ssd_y(i):
                g, c = i // TT, i % TT
                xv = X[:, c, 512 * g:512 * g + 512]
                wait_filled(dve, L + "y", i)
                readv(L + "y", i, T.tensor_tensor(xv, xv, bank(L + "y", i), ALU.add))
                if c:
                    wait_filled(dve, L + "yo", i)
                    tmp = dve_junk[:, 0:512]
                    readv(L + "yo", i, T.tensor_tensor(
                        h32(tmp), h32(bank(L + "yo", i)),
                        bc(eacs[:, 32 * c + 8 * g:32 * c + 8 * g + 8], 2, [P, 8, SSD_P]), ALU.mult))
                    v.settle()
                    tt(xv, xv, tmp, ALU.add)
                v.settle()

            for i in range(SSD_G * TT):
                g, c = i // TT, i % TT
                for half in range(2):
                    wait_read(dve, L + "seg", 2 * i + half)
                if i == 0:
                    wait_read(dve, L + "cb", 0)
                    wait_read(dve, L + "cb", 1)
                lm = Lm[:, i % 2, :].rearrange("p (h q) -> p h q", q=P)
                v.reaches(T.tensor_tensor(lm, lm, bc(cb[:, 4 * c + g, :], 1, [P, HPG, P]), ALU.mult),
                         S("decay_ready"), 8 * l + i + 1)
                if i == 0:
                    for t in range(TT):
                        tt(h32(X[:, t, :]), h32(X[:, t, :]), bc(dskip[:, 32 * l:32 * l + 32], 2, [P, 32, SSD_P]), ALU.mult)
                    v.settle()
                if i:
                    ssd_y(i - 1)
            ssd_y(SSD_G * TT - 1)
            for n in range(8):
                wait_read(dve, L + "z", n)
            for t in range(TT):
                ins = T.tensor_tensor(X[:, t, :], X[:, t, :], zs[:, t, :], ALU.mult)
                if t == 0:
                    v.done(ins)
                else:
                    v.reaches(ins, S("yz_ready"), l + 1)
            dve.wait_ge(S("gstd_ready"), l + 1)
            v.done(T.reciprocal(ginv, gstd))
            v.settle()
            for t in range(TT):
                xg = X[:, t, :].rearrange("p (g e) -> p g e", e=512)
                ins = T.tensor_tensor(xg, xg, bc(ginv[:, 4 * t:4 * t + 4], 2, [P, 4, 512]), ALU.mult)
                if t == 0:
                    v.done(ins)
                else:
                    v.reaches(ins, S("y_ready"), l + 1)
            for n in range(8):
                wait_read(dve, L + "gate", n)
            for n in range(8):
                name, src, m_ = ("pa", 0, n) if n < 4 else ("ps", 1, n - 4)
                c, t = m_ // 2, m_ % 2
                if n == 4:
                    scaled_low(L + "yT", range(16), f"snw{l}")
                sg = sig2[:, t, D * src + 512 * c:D * src + 512 * c + 512]
                mg = merged2[:, t, 512 * c:512 * c + 512]
                wait_filled(dve, L + name, m_)
                if src == 0:
                    readv(L + name, m_, T.tensor_tensor(mg, bank(L + name, m_), sg, ALU.mult))
                else:
                    readv(L + name, m_, T.tensor_tensor(sg, bank(L + name, m_), sg, ALU.mult))
                    v.settle()
                    ins = T.tensor_tensor(mg, mg, sg, ALU.add)
                    if n == 7:
                        v.reaches(ins, S("merged"), 2 + l)
                    else:
                        v.done(ins)
            for k in range(KD):
                read_low(L + "mT", k, a_hi[:, k, :], a_lo[:, k, :], bank(L + "mT", k)[:, 0:SEQ])

            def residual(name, value):
                for i in range(4):
                    c, t = i // 2, i % 2
                    wait_filled(dve, name, i)
                    xv = x[:, t, 512 * c:512 * c + 512]
                    readv(name, i, T.tensor_tensor(xv, xv, bank(name, i), ALU.add))
                v.settle()
                dve.sem_inc(S("x_updated"), 1)

            residual(L + "wo", 3 + 2 * l)
            norm_scale(3 + 2 * l, [x[:, 0, :], x[:, 1, :]], [xs[:, 0, :], xs[:, 1, :]])
            scaled_low(L + "fT", range(KD), f"ffnw{l}")
            for c in range(FT // 2):
                for m_ in range(4):
                    col = 2 * c + m_ if m_ < 2 else FT + 2 * c + m_ - 2
                    o = conv_o[:, c % 2 * 4 + m_, :]
                    conv_in(L + "up", 4 * c + m_, o, f"fcw{l}", f"fcb{l}", 3, 2 * FT, col)
                    if m_ < 2:
                        dve.sem_inc(S("gate_conv"), 1)
                for m_ in range(2):
                    i = 2 * c + m_
                    dve.wait_ge(S("gate_silu"), FT * l + i + 1)
                    gated_parts(GLU_AT + i % GLU_RING, conv_o[:, c % 2 * 4 + m_, :],
                                conv_o[:, c % 2 * 4 + 2 + m_, :], S("glu_ready"), FT * l + i + 1)
            residual(L + "dn", 4 + 2 * l)
        dve.wait_ge(S("std_ready"), 7)
        v.done(T.reciprocal(rinv[:, 0:2], std[:, 0:2]))
        dve.wait_ge(S("final_w_in"), 16)
        v.settle()
        for t in range(TT):
            v.reaches(T.scalar_tensor_tensor(out=x[:, t, :], in0=x[:, t, :], scalar=rinv[:, t:t + 1], in1=final_w,
                                            op0=ALU.mult, op1=ALU.mult), S("out_ready"), t + 1)

    @block.gpsimd
    def _(pool):
        pool.dma_start(xc, d["ctx"].rearrange("p (a b) -> p a b", b=D)).then_inc(S("ctx_in"), 16)
        for g_, at in enumerate((2 * D, 5 * D)):
            pool.dma_start(G[:, g_, :], row_b("b_ada_row", at, D)).then_inc(S("bias_g_in"), 16)
        def weights_low(n, c):
            pool.wait_ge(hi_ready, n + 1)
            width, r = wplan[c][3], n % SPLIT_RING
            nc.gpsimd.tensor_tensor(w_lo[:, r, 0:width], wring[:, c % RING, 0:width],
                                    w_hi[:, r, 0:width].bitcast(F32), ALU.subtract).then_inc(lo_ready, 1)

        streams[id(pool)] = SplitStream(weights_low)
        wait_filled(pool, "hcT", KD - 1)
        pool.dma_start(bias_qkv, row_b("b_in_row", 3 * D_HY, 1536)).then_inc(S("bias_qkv_in"), 16)
        wait_filled(pool, "conv", 7)
        pool.wait_ge(S("yh_ready"), HY_T)
        pool.dma_start(qk_g, row_b("qk_g", 0, 2 * HD)).then_inc(S("qk_g_in"), 16)
        pool.dma_start(namask, d["na_mask"]).then_inc(S("na_mask_in"), 16)
        for h in range(NA_HEADS):
            if h >= 2:
                wait_filled(pool, "nas", 2 * (h - 2) + 1)
            pool.dma_start(nabias[:, h % 2, :], d["rpb"][h]).then_inc(S(f"rpb_in{h % 2}"), 16)
            if h == 1:
                pool.wait_ge(S("na_rows"), 1)
                for part in range(2):
                    pool.dma_start(bias_gate[part], row_b("b_in_row", 3 * D_HY + 1536 + part * D, D)
                                   ).then_inc(S("bias_gate_in"), 16)
        wait_filled(pool, "mT", KD - 1)
        pool.wait_ge(S("merged"), 1)
        wait_filled(pool, "gate", 7)
        pool.dma_start(keysT, d["keysT"].rearrange("p (a b) -> p a b", b=P)).then_inc(S("keys_in"), 16)

        def gather(dst, table, g, j, sem):
            pool.indirect_dma_start(out=dst, out_offset=None, in_=d[table],
                                    in_offset=bass.IndirectOffsetOnAxis(
                                        ap=pidx[:, g, j:j + 1], axis=0)
                                    ).then_inc(S(sem), 16)

        wait_filled(pool, "pq", 15)
        last = [c for c, w in enumerate(wplan) if w[0] == "w_pq"][-1]
        pool.wait_ge(lo_ready, split_turn[last] + 1)
        for g in range(TT * PEER_HEADS):
            pool.wait_ge(S("picks_ready"), g + 1)
            for j in range(TOPK):
                n = TOPK * g + j
                if n >= U_RING:
                    pool.wait_ge(S("u_used"), n - U_RING + 1)
                gather(u_rows[:, j % U_RING, :], "peer_u", g, j, f"u_in{j % U_RING}")
            for j in range(TOPK):
                n = TOPK * g + j
                if n >= V_RING:
                    pool.wait_ge(S("v_used"), n - V_RING + 1)
                gather(v_row(j % V_RING), "peer_v", g, j, f"v_in{j % V_RING}")

        wait_filled(pool, "acc", 3)
        due(pool, "L0.hT", 0)
        pool.wait_ge(S("x_updated"), 2)
        for name, dst in (("dt_bias", dtb), ("a_log", alog), ("ssd_d", dskip)):
            pool.dma_start(dst, row_b(name, 0, 64)).then_inc(S("rows_in"), 16)
        wait_filled(pool, f"L{LAYERS - 1}.mT", KD - 1)
        pool.dma_start(final_w, row_b("final_w", 0, D)).then_inc(S("final_w_in"), 16)
        due(pool, f"L{LAYERS - 1}.dn", 3)
    ctx.close()


def kernel(**inputs):
    import concourse.bacc as bacc
    from concourse.bass_utils import run_bass_kernel_spmd

    arrays, where = lay_out(inputs)
    nc = bacc.Bacc("TRN2", target_bir_lowering=False, num_devices=1)
    d = {n: nc.dram_tensor(f"in_{n}", a.shape, mybir.dt.from_np(a.dtype), kind="ExternalInput").ap()
         for n, a in arrays.items()}
    out = nc.dram_tensor("out_rows", (P, TT, D), F32, kind="ExternalOutput").ap()
    build(nc, d, where, out)
    r = run_bass_kernel_spmd(nc, [{f"in_{n}": a for n, a in arrays.items()}], core_ids=[0])
    return r.results[0]["out_rows"].transpose(1, 0, 2).reshape(1, SEQ, D)
```
